# Optimizing a Trainium2 kernel written in Bass

```python
import math
import jax, jax.numpy as jnp
from jax import lax
import numpy as np

D_MODEL = 2048
BATCH = 1
SEQ = 256
DEPTH = 1

HEAD_DIM = 128
N_MIX_HEADS = D_MODEL // HEAD_DIM
A_HEADS = N_MIX_HEADS // 4
B_HEADS = (N_MIX_HEADS - A_HEADS) // 2
C_HEADS = N_MIX_HEADS - A_HEADS - B_HEADS
A_DK = HEAD_DIM
A_DV = HEAD_DIM
A_W = A_HEADS * A_DK
B_W = B_HEADS * HEAD_DIM
C_W = C_HEADS * HEAD_DIM
MIX_W = A_W + B_W + C_W
IN_SPLITS = [A_W, A_W, A_W, A_W, B_W, B_W, B_W, B_HEADS, C_W, C_W, C_W]
IN_COLS = sum(IN_SPLITS)
A_CHUNK = 64
B_Q_BLOCK = 128
C_BLOCK = 256
C_TOPK = 3
C_Q_BLOCK = 64
D_FF = 5632
CONV_W = 3
PLE_DIM = 256
EPS = 1e-6
TINY = 1e-30
NEG = -1e30


def rmsnorm(x, g):
    xf = x.astype(jnp.float32)
    y = xf * lax.rsqrt(jnp.mean(xf * xf, axis=-1, keepdims=True) + EPS)
    return (y * g.astype(jnp.float32)).astype(x.dtype)

def heads(t, n):
    b, s, _ = t.shape
    return t.reshape(b, s, n, -1).transpose(0, 2, 1, 3)

def merge_blocks(o):
    nqb, b, h, q, d = o.shape
    return o.transpose(1, 0, 3, 2, 4).reshape(b, nqb * q, h * d)

def alibi_slopes(n):
    return jnp.exp2(-8.0 * jnp.arange(1, n + 1, dtype=jnp.float32) / n)

def hgrn2_lower_bounds(lb_logits):
    sm = jax.nn.softmax(lb_logits.astype(jnp.float32), axis=0)
    return jnp.cumsum(sm, axis=0) - sm[0:1]

def hgrn2_mixer(q, f_logit, i, g, lb, o_norm_g):
    bsz, s, _ = q.shape
    dt = q.dtype
    z = f_logit.astype(jnp.float32)
    lbf = lb.astype(jnp.float32)
    f = lbf + (1.0 - lbf) * jax.nn.sigmoid(z)
    log_f = jnp.log(jnp.maximum(f, TINY))
    k = (1.0 - lbf) * jax.nn.sigmoid(-z)
    qh = heads(jax.nn.silu(q.astype(jnp.float32)), A_HEADS)
    kh = heads(k, A_HEADS)
    gh = heads(log_f, A_HEADS)
    vh = heads(i.astype(jnp.float32), A_HEADS)
    nc = s // A_CHUNK

    def chunks(t):
        return t.reshape(bsz, A_HEADS, nc, A_CHUNK, t.shape[-1]).transpose(2, 0, 1, 3, 4)

    causal = jnp.tril(jnp.ones((A_CHUNK, A_CHUNK), dtype=bool))[:, :, None]

    def step(state, xs):
        qc, kc, gc, vc = xs
        b = jnp.cumsum(gc, axis=2)
        o_inter = jnp.einsum('bhtd,bhde->bhte', qc * jnp.exp(b), state)
        diff = b[:, :, :, None, :] - b[:, :, None, :, :]
        decay = jnp.where(causal, jnp.exp(jnp.where(causal, diff, 0.0)), 0.0)
        attn = jnp.einsum('bhtd,bhsd,bhtsd->bhts', qc, kc, decay)
        o = o_inter + jnp.einsum('bhts,bhse->bhte', attn, vc)
        b_last = b[:, :, -1:, :]
        k_dec = kc * jnp.exp(b_last - b)
        state = jnp.exp(b_last[:, :, 0, :])[..., None] * state + jnp.einsum('bhsd,bhse->bhde', k_dec, vc)
        return state, o

    s0 = jnp.zeros((bsz, A_HEADS, A_DK, A_DV), jnp.float32)
    _, o = lax.scan(step, s0, (chunks(qh), chunks(kh), chunks(gh), chunks(vh)))
    o = o.transpose(1, 2, 0, 3, 4).reshape(bsz, A_HEADS, s, A_DV)
    o = rmsnorm(o, o_norm_g) * jax.nn.silu(heads(g.astype(jnp.float32), A_HEADS))
    return o.transpose(0, 2, 1, 3).reshape(bsz, s, A_W).astype(dt)

def fox_mixer(q, k, v, f_logit, b_f, qn_g, kn_g):
    bsz, s, _ = q.shape
    dt = q.dtype
    qh = rmsnorm(heads(q, B_HEADS), qn_g)
    kh = rmsnorm(heads(k, B_HEADS), kn_g)
    vh = heads(v, B_HEADS)
    log_f = jax.nn.log_sigmoid(f_logit.astype(jnp.float32) + b_f.astype(jnp.float32))
    fcum = jnp.cumsum(log_f, axis=1).transpose(0, 2, 1)
    nqb = s // B_Q_BLOCK
    qb = qh.reshape(bsz, B_HEADS, nqb, B_Q_BLOCK, HEAD_DIM).transpose(2, 0, 1, 3, 4)
    fq = fcum.reshape(bsz, B_HEADS, nqb, B_Q_BLOCK).transpose(2, 0, 1, 3)
    kpos = jnp.arange(s)
    scale = HEAD_DIM ** -0.5

    def block(xs):
        qi, fi, bi = xs
        qpos = bi * B_Q_BLOCK + jnp.arange(B_Q_BLOCK)
        logits = (jnp.einsum('bhqd,bhkd->bhqk', qi, kh).astype(jnp.float32) * scale
                  + fi[..., None] - fcum[:, :, None, :])
        logits = jnp.where(kpos[None, :] <= qpos[:, None], logits, NEG)
        w = jax.nn.softmax(logits, axis=-1).astype(dt)
        return jnp.einsum('bhqk,bhkd->bhqd', w, vh)

    o = lax.map(block, (qb, fq, jnp.arange(nqb)))
    return merge_blocks(o)

def moba_mixer(q, k, v, qn_g, kn_g, slopes):
    bsz, s, _ = q.shape
    dt = q.dtype
    h = C_HEADS
    qh = rmsnorm(heads(q, h), qn_g)
    kh = rmsnorm(heads(k, h), kn_g)
    vh = heads(v, h)
    nb = -(-s // C_BLOCK)
    s_pad = nb * C_BLOCK
    pad = ((0, 0), (0, 0), (0, s_pad - s), (0, 0))
    kp = jnp.pad(kh, pad)
    vp = jnp.pad(vh, pad)
    kblk = kp.reshape(bsz, h, nb, C_BLOCK, HEAD_DIM)
    vblk = vp.reshape(bsz, h, nb, C_BLOCK, HEAD_DIM)
    pos = jnp.arange(s)
    own = pos // C_BLOCK
    topk = min(C_TOPK, nb - 1)
    scale = HEAD_DIM ** -0.5
    kflat = kblk.reshape(bsz * h * nb, C_BLOCK, HEAD_DIM)
    vflat = vblk.reshape(bsz * h * nb, C_BLOCK, HEAD_DIM)
    bh_off = (jnp.arange(bsz * h, dtype=jnp.int32) * nb).reshape(bsz, h, 1, 1)
    blk_off = jnp.arange(C_BLOCK)
    sl = slopes[None, :, None, None]
    nqb = s // C_Q_BLOCK

    def to_blocks(t):
        t = t.reshape((bsz, h, nqb, C_Q_BLOCK) + t.shape[3:])
        return jnp.moveaxis(t, 2, 0)

    if topk > 0:
        kbar = jnp.mean(kblk.astype(jnp.float32), axis=3)
        gate = jnp.einsum('bhsd,bhnd->bhsn', qh.astype(jnp.float32), kbar)
        past = jnp.arange(nb)[None, :] < own[:, None]
        gate = jnp.where(past, gate, NEG)
        gval, gidx = lax.top_k(gate, topk)
        gvalid = gval > NEG / 2
        xs = (to_blocks(qh), jnp.arange(nqb), to_blocks(gidx), to_blocks(gvalid))
    else:
        xs = (to_blocks(qh), jnp.arange(nqb))

    def block(xs):
        qi, bi = xs[0], xs[1]
        qpos = bi * C_Q_BLOCK + jnp.arange(C_Q_BLOCK)
        start = (bi * C_Q_BLOCK // C_BLOCK) * C_BLOCK
        k_own = lax.dynamic_slice_in_dim(kp, start, C_BLOCK, axis=2)
        v_own = lax.dynamic_slice_in_dim(vp, start, C_BLOCK, axis=2)
        dist = (qpos[:, None] - (start + blk_off)[None, :]).astype(jnp.float32)
        s_own = jnp.einsum('bhqd,bhkd->bhqk', qi, k_own).astype(jnp.float32) * scale - sl * dist
        scores = [jnp.where(dist >= 0, s_own, NEG)]
        flats = []
        if topk > 0:
            idx, valid = xs[2], xs[3]
            flat = bh_off + idx
            for j in range(topk):
                fj = flat[..., j]
                flats.append(fj)
                kg = kflat[fj]
                kpos_g = idx[..., j][..., None] * C_BLOCK + blk_off
                dist_g = (qpos[None, None, :, None] - kpos_g).astype(jnp.float32)
                sj = jnp.einsum('bhqd,bhqkd->bhqk', qi, kg).astype(jnp.float32) * scale - sl * dist_g
                scores.append(jnp.where(valid[..., j][..., None], sj, NEG))
        w = jax.nn.softmax(jnp.concatenate(scores, axis=-1), axis=-1).astype(dt)
        out = jnp.einsum('bhqk,bhkd->bhqd', w[..., :C_BLOCK], v_own)
        for j, fj in enumerate(flats):
            vg = vflat[fj]
            wj = w[..., (j + 1) * C_BLOCK:(j + 2) * C_BLOCK]
            out = out + jnp.einsum('bhqk,bhqkd->bhqd', wj, vg)
        return out

    o = lax.map(block, xs)
    return merge_blocks(o)

def conv_ffn(x, w_gate, w_up, conv_w, conv_b, w_down):
    hg = x @ w_gate
    hg = lax.conv_general_dilated(hg, conv_w[:, None, :], window_strides=(1,),
                                  padding=[(CONV_W - 1, 0)],
                                  dimension_numbers=('NWC', 'WIO', 'NWC'),
                                  feature_group_count=hg.shape[-1]) + conv_b
    return (jax.nn.gelu(hg, approximate=True) * (x @ w_up)) @ w_down

def first_inputs(seed: int = 0) -> dict:
    key = jax.random.key(seed)
    ks = jax.random.split(key, 21)
    f32 = jnp.float32

    def nrm(k, shape, scale):
        return jax.random.normal(k, shape, f32) * scale

    return {
        "x": nrm(ks[0], (BATCH, SEQ, D_MODEL), 1.0),
        "p": nrm(ks[1], (DEPTH, BATCH, SEQ, PLE_DIM), 1.0),
        "attn_norm": 1.0 + nrm(ks[2], (DEPTH, D_MODEL), 0.02),
        "w_in": nrm(ks[3], (DEPTH, D_MODEL, IN_COLS), D_MODEL ** -0.5),
        "fox_bf": nrm(ks[4], (DEPTH, B_HEADS), 0.1),
        "lb_logits": nrm(ks[5], (DEPTH, A_W), 0.1),
        "hgrn_onorm": 1.0 + nrm(ks[6], (DEPTH, A_DV), 0.02),
        "fox_qnorm": 1.0 + nrm(ks[7], (DEPTH, HEAD_DIM), 0.02),
        "fox_knorm": 1.0 + nrm(ks[8], (DEPTH, HEAD_DIM), 0.02),
        "moba_qnorm": 1.0 + nrm(ks[9], (DEPTH, HEAD_DIM), 0.02),
        "moba_knorm": 1.0 + nrm(ks[10], (DEPTH, HEAD_DIM), 0.02),
        "w_out": nrm(ks[11], (DEPTH, MIX_W, D_MODEL), MIX_W ** -0.5),
        "ffn_norm": 1.0 + nrm(ks[12], (DEPTH, D_MODEL), 0.02),
        "w_gate": nrm(ks[13], (DEPTH, D_MODEL, D_FF), D_MODEL ** -0.5),
        "w_up": nrm(ks[14], (DEPTH, D_MODEL, D_FF), D_MODEL ** -0.5),
        "conv_w": nrm(ks[15], (DEPTH, CONV_W, D_FF), CONV_W ** -0.5),
        "conv_b": nrm(ks[16], (DEPTH, D_FF), 0.01),
        "w_down": nrm(ks[17], (DEPTH, D_FF, D_MODEL), D_FF ** -0.5),
        "ple_norm": 1.0 + nrm(ks[18], (DEPTH, D_MODEL), 0.02),
        "w_ple_gate": nrm(ks[19], (DEPTH, D_MODEL, D_MODEL), D_MODEL ** -0.5),
        "w_ple_proj": nrm(ks[20], (DEPTH, PLE_DIM, D_MODEL), PLE_DIM ** -0.5),
    }

def first_block(x, p, attn_norm, w_in, fox_bf, lb_logits, hgrn_onorm, fox_qnorm, fox_knorm,
              moba_qnorm, moba_knorm, w_out, ffn_norm, w_gate, w_up, conv_w, conv_b, w_down,
              ple_norm, w_ple_gate, w_ple_proj):
    lbs = hgrn2_lower_bounds(lb_logits)
    slopes = alibi_slopes(C_HEADS)
    split_idx = []
    acc = 0
    for n in IN_SPLITS[:-1]:
        acc += n
        split_idx.append(acc)
    h = x
    for i in range(DEPTH):
        a = rmsnorm(h, attn_norm[i])
        proj = a @ w_in[i]
        aq, af, ai, ag, bq, bk, bv, bf, cq, ck, cv = jnp.split(proj, split_idx, axis=-1)
        oa = hgrn2_mixer(aq, af, ai, ag, lbs[i], hgrn_onorm[i])
        ob = fox_mixer(bq, bk, bv, bf, fox_bf[i], fox_qnorm[i], fox_knorm[i])
        oc = moba_mixer(cq, ck, cv, moba_qnorm[i], moba_knorm[i], slopes)
        h = h + jnp.concatenate([oa, ob, oc], axis=-1) @ w_out[i]
        c = rmsnorm(h, ffn_norm[i])
        h = h + conv_ffn(c, w_gate[i], w_up[i], conv_w[i], conv_b[i], w_down[i])
        e = rmsnorm(h, ple_norm[i])
        h = h + jax.nn.sigmoid(e @ w_ple_gate[i]) * (p[i] @ w_ple_proj[i])
    return h


MIX_WIDTH = D_MODEL
SB_HEADS = 8
SB_HEAD_DIM = 128
SB_WIDTH = SB_HEADS * SB_HEAD_DIM
SB_BLOCK = 128
SSD_HEADS = 16
SSD_HEAD_DIM = 64
SSD_WIDTH = SSD_HEADS * SSD_HEAD_DIM
SSD_GROUPS = 2
SSD_STATE = 128
SSD_CONV = 4
SSD_CHUNK = 128
SSD_CONV_DIM = SSD_WIDTH + 2 * SSD_GROUPS * SSD_STATE
IN_PROJ_DIM = 3 * SB_WIDTH + SSD_WIDTH + SSD_CONV_DIM + SSD_HEADS
PEER_HEADS = 8
PEER_N_KEYS = 128
PEER_N_EXPERTS = PEER_N_KEYS * PEER_N_KEYS
PEER_KEY_DIM = 256
PEER_HALF = PEER_KEY_DIM // 2
PEER_TOPK = 16
PEER_TOKEN_BLOCK = 128
RMS_EPS = 1e-6


def rms_norm(x, gain):
    xf = x.astype(jnp.float32)
    inv = lax.rsqrt(jnp.mean(xf * xf, axis=-1, keepdims=True) + RMS_EPS)
    return (xf * inv).astype(x.dtype) * gain

def stick_breaking_attention(q, k, v):
    b, s, h, dh = q.shape
    nb = s // SB_BLOCK
    scale = dh ** -0.5
    kf = k.astype(jnp.float32)
    vf = v.astype(jnp.float32)
    key_pos = jnp.arange(s)
    q_blocks = q.reshape(b, nb, SB_BLOCK, h, dh).transpose(1, 0, 2, 3, 4)

    def block(args):
        qb, bi = args
        q_pos = bi * SB_BLOCK + jnp.arange(SB_BLOCK)
        logits = jnp.einsum('bqhd,bkhd->bhqk', qb.astype(jnp.float32), kf) * scale
        causal = key_pos[None, :] < q_pos[:, None]
        log_beta = jax.nn.log_sigmoid(logits)
        log_keep = jnp.where(causal, jax.nn.log_sigmoid(-logits), 0.0)
        later = lax.cumsum(log_keep, axis=3, reverse=True) - log_keep
        weights = jnp.where(causal, jnp.exp(jnp.where(causal, log_beta + later, 0.0)), 0.0)
        return jnp.einsum('bhqk,bkhd->bqhd', weights, vf)

    out = lax.map(block, (q_blocks, jnp.arange(nb)))
    return out.transpose(1, 0, 2, 3, 4).reshape(b, s, h, dh).astype(q.dtype)

def ssd_scan(x, dt, a, bmat, cmat):
    f32 = jnp.float32
    b, s, h, p = x.shape
    g, n = bmat.shape[-2], bmat.shape[-1]
    hg = h // g
    nc, l = s // SSD_CHUNK, SSD_CHUNK
    xf = (x.astype(f32) * dt[..., None]).reshape(b, nc, l, g, hg, p)
    a_dt = (dt * a).reshape(b, nc, l, g, hg).transpose(0, 3, 4, 1, 2)
    bf = bmat.astype(f32).reshape(b, nc, l, g, n)
    cf = cmat.astype(f32).reshape(b, nc, l, g, n)
    a_cs = jnp.cumsum(a_dt, axis=-1)
    seg = a_cs[..., :, None] - a_cs[..., None, :]
    tri = jnp.tril(jnp.ones((l, l), dtype=bool))
    decay = jnp.where(tri, jnp.exp(jnp.where(tri, seg, 0.0)), 0.0).transpose(0, 3, 1, 2, 4, 5)
    cb = jnp.einsum('bclgn,bcsgn->bcgls', cf, bf)
    scores = cb[:, :, :, None] * decay
    y_diag = jnp.einsum('bcghls,bcsghp->bclghp', scores, xf)
    decay_states = jnp.exp(a_cs[..., -1:] - a_cs).transpose(0, 3, 4, 1, 2)
    states = jnp.einsum('bclgn,bclghp->bcghpn', bf, xf * decay_states[..., None])
    chunk_decay = jnp.exp(a_cs[..., -1]).transpose(3, 0, 1, 2)

    def step(carry, inp):
        st, dec = inp
        return carry * dec[..., None, None] + st, carry

    init = jnp.zeros((b, g, hg, p, n), f32)
    _, prev = lax.scan(step, init, (states.transpose(1, 0, 2, 3, 4, 5), chunk_decay))
    prev = prev.transpose(1, 0, 2, 3, 4, 5)
    state_decay_out = jnp.exp(a_cs).transpose(0, 3, 4, 1, 2)
    y_off = jnp.einsum('bclgn,bcghpn->bclghp', cf, prev) * state_decay_out[..., None]
    return (y_diag + y_off).reshape(b, s, h, p)

def hybrid_mixer(xn, w_in, sb_q_norm, sb_k_norm, conv_w, conv_b, dt_bias, a_log, d_skip,
                 sb_out_norm, ssd_out_norm, w_out):
    b, s, _ = xn.shape
    proj = xn @ w_in
    o1 = SB_WIDTH
    o2 = 2 * SB_WIDTH
    o3 = 3 * SB_WIDTH
    o4 = o3 + SSD_WIDTH
    o5 = o4 + SSD_CONV_DIM
    q, k, v, z, xbc, dt_raw = jnp.split(proj, [o1, o2, o3, o4, o5], axis=-1)
    q = rms_norm(q.reshape(b, s, SB_HEADS, SB_HEAD_DIM), sb_q_norm)
    k = rms_norm(k.reshape(b, s, SB_HEADS, SB_HEAD_DIM), sb_k_norm)
    v = v.reshape(b, s, SB_HEADS, SB_HEAD_DIM)
    attn = stick_breaking_attention(q, k, v).reshape(b, s, SB_WIDTH)
    attn = rms_norm(attn, sb_out_norm)
    xbc = lax.conv_general_dilated(xbc, conv_w, window_strides=(1,), padding=[(SSD_CONV - 1, 0)],
                                   dimension_numbers=('NWC', 'WIO', 'NWC'),
                                   feature_group_count=SSD_CONV_DIM) + conv_b
    xbc = jax.nn.silu(xbc)
    xs, bm, cm = jnp.split(xbc, [SSD_WIDTH, SSD_WIDTH + SSD_GROUPS * SSD_STATE], axis=-1)
    xs = xs.reshape(b, s, SSD_HEADS, SSD_HEAD_DIM)
    bm = bm.reshape(b, s, SSD_GROUPS, SSD_STATE)
    cm = cm.reshape(b, s, SSD_GROUPS, SSD_STATE)
    dt = jax.nn.softplus(dt_raw.astype(jnp.float32) + dt_bias.astype(jnp.float32))
    a = -jnp.exp(a_log.astype(jnp.float32))
    y = ssd_scan(xs, dt, a, bm, cm) + d_skip[:, None] * xs
    y = y.reshape(b, s, SSD_WIDTH).astype(xn.dtype) * jax.nn.silu(z)
    y = rms_norm(y.reshape(b, s, SSD_GROUPS, SSD_WIDTH // SSD_GROUPS),
                 ssd_out_norm.reshape(SSD_GROUPS, SSD_WIDTH // SSD_GROUPS)).reshape(b, s, SSD_WIDTH)
    return jnp.concatenate([attn, y], axis=-1) @ w_out

def peer_ffn(hn, w_query, sub_keys, expert_down, expert_up):
    b, s, d = hn.shape
    t = b * s
    xt = hn.reshape(t, d)
    q = (xt @ w_query).reshape(t, PEER_HEADS, 2, PEER_HALF)
    scores = jnp.einsum('thcd,hckd->thck', q.astype(jnp.float32), sub_keys.astype(jnp.float32))
    top_s, top_i = lax.top_k(scores, PEER_TOPK)
    cand_s = (top_s[:, :, 0, :, None] + top_s[:, :, 1, None, :]).reshape(t, PEER_HEADS, PEER_TOPK * PEER_TOPK)
    cand_i = (top_i[:, :, 0, :, None] * PEER_N_KEYS + top_i[:, :, 1, None, :]).reshape(t, PEER_HEADS, PEER_TOPK * PEER_TOPK)
    best_s, best_pos = lax.top_k(cand_s, PEER_TOPK)
    expert_idx = jnp.take_along_axis(cand_i, best_pos, axis=-1)
    gates = jax.nn.softmax(best_s, axis=-1)
    nblk = t // PEER_TOKEN_BLOCK

    def block(args):
        xb, idx, gb = args
        u = expert_down[idx]
        act = jax.nn.gelu(jnp.einsum('thkd,td->thk', u, xb), approximate=False)
        vv = expert_up[idx]
        return jnp.einsum('thk,thkd->td', (gb * act).astype(vv.dtype), vv)

    out = lax.map(block, (xt.reshape(nblk, PEER_TOKEN_BLOCK, d),
                          expert_idx.reshape(nblk, PEER_TOKEN_BLOCK, PEER_HEADS, PEER_TOPK),
                          gates.reshape(nblk, PEER_TOKEN_BLOCK, PEER_HEADS, PEER_TOPK)))
    return out.reshape(b, s, d).astype(hn.dtype)

def second_inputs(seed: int = 0) -> dict:
    key = jax.random.key(seed)
    ks = jax.random.split(key, 20)
    f32 = jnp.float32
    nrm = lambda k, shape, sc: jax.random.normal(k, shape, f32) * sc
    gain = lambda k, shape: 1.0 + 0.02 * jax.random.normal(k, shape, f32)
    dt0 = jnp.exp(jax.random.uniform(ks[8], (DEPTH, SSD_HEADS), f32, float(np.log(1e-3)), float(np.log(1e-1))))
    return {
        "x": jax.random.normal(ks[0], (BATCH, SEQ, D_MODEL), f32),
        "attn_norm": gain(ks[1], (DEPTH, D_MODEL)),
        "w_in": nrm(ks[2], (DEPTH, D_MODEL, IN_PROJ_DIM), D_MODEL ** -0.5),
        "sb_q_norm": gain(ks[3], (DEPTH, SB_HEAD_DIM)),
        "sb_k_norm": gain(ks[4], (DEPTH, SB_HEAD_DIM)),
        "conv_w": nrm(ks[5], (DEPTH, SSD_CONV, 1, SSD_CONV_DIM), SSD_CONV ** -0.5),
        "conv_b": nrm(ks[6], (DEPTH, SSD_CONV_DIM), 0.02),
        "dt_bias": jnp.log(jnp.expm1(dt0)),
        "a_log": jnp.log(jax.random.uniform(ks[9], (DEPTH, SSD_HEADS), f32, 1.0, 16.0)),
        "d_skip": gain(ks[10], (DEPTH, SSD_HEADS)),
        "sb_out_norm": gain(ks[11], (DEPTH, SB_WIDTH)),
        "ssd_out_norm": gain(ks[12], (DEPTH, SSD_WIDTH)),
        "w_out": nrm(ks[13], (DEPTH, MIX_WIDTH, D_MODEL), MIX_WIDTH ** -0.5),
        "ffn_norm": gain(ks[14], (DEPTH, D_MODEL)),
        "peer_query": nrm(ks[15], (DEPTH, D_MODEL, PEER_HEADS * PEER_KEY_DIM), D_MODEL ** -0.5),
        "peer_sub_keys": nrm(ks[16], (DEPTH, PEER_HEADS, 2, PEER_N_KEYS, PEER_HALF), PEER_HALF ** -0.5),
        "peer_down": nrm(ks[17], (DEPTH, PEER_N_EXPERTS, D_MODEL), D_MODEL ** -0.5),
        "peer_up": nrm(ks[18], (DEPTH, PEER_N_EXPERTS, D_MODEL), (PEER_HEADS * PEER_TOPK) ** -0.5),
    }

def second_block(x, attn_norm, w_in, sb_q_norm, sb_k_norm, conv_w, conv_b, dt_bias, a_log, d_skip,
              sb_out_norm, ssd_out_norm, w_out, ffn_norm, peer_query, peer_sub_keys, peer_down, peer_up):
    h = x
    for layer in range(DEPTH):
        xn = rms_norm(h, attn_norm[layer])
        h = h + hybrid_mixer(xn, w_in[layer], sb_q_norm[layer], sb_k_norm[layer], conv_w[layer],
                             conv_b[layer], dt_bias[layer], a_log[layer], d_skip[layer],
                             sb_out_norm[layer], ssd_out_norm[layer], w_out[layer])
        hn = rms_norm(h, ffn_norm[layer])
        h = h + peer_ffn(hn, peer_query[layer], peer_sub_keys[layer], peer_down[layer], peer_up[layer])
    return h


def setup_inputs(seed=0):
    out = dict(first_inputs(seed))
    for name, value in second_inputs(seed + 1).items():
        if name != "x":
            out[name + "_2"] = value
    return out


def reference(
    x, p, attn_norm, w_in, fox_bf, lb_logits, hgrn_onorm, fox_qnorm, fox_knorm, moba_qnorm,
    moba_knorm, w_out, ffn_norm, w_gate, w_up, conv_w, conv_b, w_down, ple_norm, w_ple_gate,
    w_ple_proj, attn_norm_2, w_in_2, sb_q_norm_2, sb_k_norm_2, conv_w_2, conv_b_2, dt_bias_2,
    a_log_2, d_skip_2, sb_out_norm_2, ssd_out_norm_2, w_out_2, ffn_norm_2, peer_query_2,
    peer_sub_keys_2, peer_down_2, peer_up_2,
):
    x = first_block(
        x, p, attn_norm, w_in, fox_bf, lb_logits, hgrn_onorm, fox_qnorm, fox_knorm, moba_qnorm,
        moba_knorm, w_out, ffn_norm, w_gate, w_up, conv_w, conv_b, w_down, ple_norm, w_ple_gate,
        w_ple_proj,
    )
    return second_block(
        x, attn_norm_2, w_in_2, sb_q_norm_2, sb_k_norm_2, conv_w_2, conv_b_2, dt_bias_2,
        a_log_2, d_skip_2, sb_out_norm_2, ssd_out_norm_2, w_out_2, ffn_norm_2, peer_query_2,
        peer_sub_keys_2, peer_down_2, peer_up_2,
    )


_drawn_inputs = setup_inputs


def setup_inputs(seed=0):
    import zlib

    import numpy as np

    out = dict(_drawn_inputs(seed))
    spreads = {}
    factors = {'attn_norm': 3.446,
     'fox_bf': 3.882,
     'hgrn_onorm': 7.961,
     'fox_qnorm': 8.0,
     'fox_knorm': 8.0,
     'moba_qnorm': 8.0,
     'moba_knorm': 8.0,
     'ffn_norm': 3.72,
     'conv_b': 8.0,
     'ple_norm': 64.0,
     'attn_norm_2': 3.591,
     'sb_q_norm_2': 24.406,
     'sb_k_norm_2': 21.863,
     'conv_b_2': 27.152,
     'd_skip_2': 64.0,
     'sb_out_norm_2': 50.224,
     'ssd_out_norm_2': 54.624,
     'ffn_norm_2': 64.0}
    for name, (base, spread) in spreads.items():
        noise = np.random.default_rng([zlib.crc32(name.encode()), seed]).standard_normal(out[name].shape)
        drawn = base * np.exp(spread * noise) if base else spread * noise
        out[name] = __import__('jax').numpy.asarray(drawn.astype(out[name].dtype))
    for name, factor in factors.items():
        out[name] = (out[name] * factor).astype(out[name].dtype)
    return out
```

```python
import numpy as np
import concourse.bass as bass
from concourse import mybir
from contextlib import ExitStack

F32 = mybir.dt.float32
U32 = mybir.dt.uint32
I32 = mybir.dt.int32
ALU = mybir.AluOpType
ACT = mybir.ActivationFunctionType
AX = mybir.AxisListType

EPS = 1e-6
SCALE = 128.0 ** -0.5
NEG = -1e30
SLOPES = [float(np.float32(2.0) ** np.float32(-8.0 * (i + 1) / 6.0)) for i in range(6)]

COLS = [("attn_norm", 16), ("ffn_norm", 16), ("ple_norm", 16), ("attn_norm_2", 16), ("ffn_norm_2", 16),
        ("lb", 4), ("hgrn", 1), ("foxq", 1), ("foxk", 1), ("mobq", 1), ("mobk", 1),
        ("cw0", 44), ("cw1", 44), ("cw2", 44), ("cb", 44), ("sbq", 1), ("sbk", 1),
        ("c20", 12), ("c21", 12), ("c22", 12), ("c23", 12), ("cb2", 12),
        ("sbo", 8), ("sso", 8), ("dsk", 8), ("bf", 1), ("dtb", 1), ("alog", 1)]
COFF = {}
_n = 0
for _k, _w in COLS:
    COFF[_k] = _n
    _n += _w
NCOL = _n


class Eng:

    def __init__(self, sem, chain):
        self.sem, self.n, self.q, self.chain = sem, 0, [], chain

    def op(self, fn, *after, inc=True, chain=None):
        waits = []
        stack = list(after)
        while stack:
            a = stack.pop(0)
            if isinstance(a, list):
                stack = a + stack
            elif a is not None:
                waits.append(a)
        if (self.chain if chain is None else chain) and self.n:
            waits.append((self.sem, self.n))
        if inc:
            self.n += 1
        self.q.append((waits, fn, (self.sem, 1) if inc else None))
        return (self.sem, self.n)

    def dma(self, out, in_, sem, count, *after):
        waits = []
        for a in after:
            waits += a if isinstance(a, list) else [a] if a is not None else []
        self.q.append((waits, lambda e: e.dma_start(out, in_), (sem, 16)))
        return (sem, 16 * count)

    def emit(self, eng):
        seen = {}
        for waits, fn, inc in self.q:
            for sem, v in waits:
                if seen.get(sem.name, 0) < v:
                    eng.wait_ge(sem, v)
                    seen[sem.name] = v
            ins = fn(eng)
            if inc is not None:
                ins.then_inc(*inc)


class Slot:
    def __init__(self, ap, sem=None):
        self.ap, self.sem, self.free, self.n = ap, sem, None, 0


def build(nc, x, pT, colsd, w1fm, w1v, w1f, wo1, wgu, wdn, plg, plp, w2fm, w2v, w2d, wo2, wq, sk, dn, up, out):
    ctx = ExitStack()
    with ctx:
        def sb(name, n, dt=F32, p=128):
            return ctx.enter_context(nc.sbuf_tensor(name, [p, n], dt))

        sems = {}

        def sem(name):
            sems[name] = ctx.enter_context(nc.semaphore(name))
            return sems[name]

        V = Eng(sem("s_v"), True)
        A = Eng(sem("s_a"), True)
        P = Eng(sem("s_p"), True)
        T = Eng(sem("s_t"), False)
        S = Eng(sem("s_s"), False)

        NR = 4
        ring = sb("ring", NR * 2048)
        slots = [Slot(ring[:, i * 2048:(i + 1) * 2048], sem(f"s_w{i}")) for i in range(NR)]
        arena = sb("arena", 32768)
        hsb = sb("hsb", 4096)
        h = hsb[:, :].rearrange("p (t d) -> p t d", t=2)
        act = sb("act", 4096)
        actT = act[:, :].rearrange("p (k t) -> p k t", k=16)
        cols = sb("cols", NCOL)
        ident = sb("ident", 128)
        ones = sb("ones", 256)
        tri = sb("tri", 128)
        small = sb("small", 144)
        oh = sb("oh", 2048)
        picks = sb("picks", 768)
        iot = sb("iot", 128)
        banks = [Slot(ctx.enter_context(nc.psum_tensor(f"b{i}", [128, 512], F32))[:, :]) for i in range(8)]

        def col(name, i=0, p=128):
            return cols[0:p, COFF[name] + i:COFF[name] + i + 1]

        at = [0]

        def carve(n, where=None):
            if where is not None:
                at[0] = where
            a = arena[:, at[0]:at[0] + n]
            at[0] += n
            assert at[0] <= 32768, at[0]
            return a

        loads = [0]

        def load(src):
            s = slots[loads[0] % NR]
            loads[0] += 1
            s.n += 1
            tok = S.dma(s.ap, src, s.sem, s.n, s.free)
            return s, tok

        nb = [0]

        def bank():
            b = banks[nb[0] % 8]
            nb[0] += 1
            return b

        def mm(o, l, r, start, stop, *after, inc=False):
            return T.op(lambda e: e.matmul(o, l, r, start=start, stop=stop), *after, inc=inc)

        def tr(o, i, *after, inc=False):
            return T.op(lambda e: e.transpose(o, i, ident[:, :]), *after, inc=inc)

        def act_(o, i, f, *after, bias=0.0, scale=1.0, acc=None):
            if acc is None:
                return A.op(lambda e: e.activation(o, i, f, bias=bias, scale=scale), *after)
            return A.op(lambda e: e.activation(o, i, f, bias=bias, scale=scale, accum_out=acc), *after)

        def cp(o, i, *after):
            return A.op(lambda e: e.activation(o, i, ACT.Copy), *after)

        def tt(o, a, b, op, *after, E=None):
            return (E or V).op(lambda e: e.tensor_tensor(o, a, b, op), *after)

        def ts(o, a, s1, s2, op0, op1, *after, E=None):
            if op1 is None:
                return (E or V).op(lambda e: e.tensor_scalar(o, a, s1, None, op0), *after)
            return (E or V).op(lambda e: e.tensor_scalar(o, a, s1, s2, op0, op1), *after)

        def stt(o, a, s, b, op0, op1, *after):
            return V.op(lambda e: e.scalar_tensor_tensor(out=o, in0=a, scalar=s, in1=b, op0=op0, op1=op1), *after)

        def recip(o, i, *after):
            return V.op(lambda e: e.reciprocal(o, i), *after)

        def memset(E, o, v, *after):
            return E.op(lambda e: e.memset(o, v), *after)

        def asel(o, i, pattern, op, fill, base, cm, *after):
            return P.op(lambda e: e.affine_select(out=o, in_=i, pattern=pattern, compare_op=op, fill=fill,
                                                  base=base, channel_multiplier=cm), *after)

        def bc(ap, n):
            return ap.unsqueeze(2).to_broadcast([ap.shape[0], ap.shape[1], n])

        def bm(ap, n):
            return ap.unsqueeze(1).to_broadcast([ap.shape[0], n, ap.shape[1]])

        s_c = sem("s_c")
        t_cols = A.dma(cols[:, :], colsd, s_c, 1)
        s_x = sem("s_x")
        t_x = A.dma(h[:, :, :], x.rearrange("(t p) d -> p t d", p=128), s_x, 1)
        memset(P, ident[:, :], 0.0)
        t_id = asel(ident[:, :], ident[:, :], [[-1, 128]], ALU.not_equal, 1.0, 0, 1)
        memset(P, ones[:, :], 1.0)
        memset(P, tri[:, :], 1.0)
        asel(tri[:, :], tri[:, :], [[-1, 128]], ALU.is_ge, 0.0, 0, 1)
        t_const = P.op(lambda e: e.iota(iot[:, :], pattern=[[1, 128]], base=0, channel_multiplier=0,
                                        allow_small_or_imprecise_dtypes=True))

        def norm_T(gain, tmp, t_in, t_free):
            xn = tmp.rearrange("p (t d) -> p t d", t=2)
            for t in range(2):
                act_(xn[:, t, :], h[:, t, :], ACT.Square, t_in, t_free, acc=small[:, t:t + 1])
            ta = (A.sem, A.n)
            tv = ts(small[:, 2:4], small[:, 0:2], 1.0 / 2048, EPS, ALU.mult, ALU.add, ta)
            ta = act_(small[:, 4:6], small[:, 2:4], ACT.Sqrt, tv)
            recip(small[:, 6:8], small[:, 4:6], ta)
            for t in range(2):
                tv = ts(xn[:, t, :], h[:, t, :], small[:, 6 + t:7 + t], None, ALU.mult, None)
            done = []
            for g in range(8):
                b = bank()
                for k in (2 * g, 2 * g + 1):
                    for t in range(2):
                        o = (k % 2) * 256 + t * 128
                        tp = tr(b.ap[:, o:o + 128], xn[:, t, k * 128:(k + 1) * 128], tv, b.free, t_id,
                                inc=(k % 2 == 1 and t == 1))
                if g % 2 == 0:
                    b.free = tt(actT[:, 2 * g:2 * g + 2, :], b.ap.rearrange("p (k t) -> p k t", k=2),
                                bc(cols[:, COFF[gain] + 2 * g:COFF[gain] + 2 * g + 2], 256), ALU.mult, tp, t_cols)
                    done = [b.free] + done[1:]
                else:
                    for k in (2 * g, 2 * g + 1):
                        b.free = act_(actT[:, k, :], b.ap[:, (k % 2) * 256:(k % 2) * 256 + 256], ACT.Identity,
                                      tp, t_cols, scale=col(gain, k))
                    done = done[:1] + [b.free]
            return done

        def fm_tiles(src, i0, n, t_act, sink):
            for i in range(i0, i0 + n, 2):
                b = bank()
                m = min(2, i0 + n - i)
                for j in range(m):
                    s, tl = load(src[i + j, :, :])
                    for k in range(16):
                        tp = mm(b.ap[:, j * 256:j * 256 + 256], s.ap[:, k * 128:(k + 1) * 128], actT[:, k, :],
                                k == 0, k == 15, t_act, tl, b.free, inc=(k == 15))
                    s.free = tp
                b.free = sink(i - i0, m, b, tp)

        def rows8(src, nk, lhs, t_l):
            for k in range(nk):
                s, tl = load(src[k, :, :])
                for t in range(2):
                    for c in range(4):
                        b = banks[t * 4 + c]
                        last = k == nk - 1
                        tp = mm(b.ap, lhs(k, t), s.ap[:, c * 512:(c + 1) * 512], k == 0, last,
                                tl, t_l(k) if callable(t_l) else t_l, b.free if k == 0 else None,
                                inc=last or (t == 1 and c == 3))
                s.free = tp
            return tp

        def add_h(tp):
            for t in range(2):
                for c in range(4):
                    b = banks[t * 4 + c]
                    b.free = tt(h[:, t, c * 512:(c + 1) * 512], h[:, t, c * 512:(c + 1) * 512], b.ap, ALU.add, tp)
            return b.free

        def rs_bcast(o, src_aps, n, tp, t_free, sq):
            w = o.shape[1]
            b = bank()
            ta = tp
            for i, a in enumerate(src_aps):
                ta = act_(sq[i], a, ACT.Square, tp, t_free)
            for i in range(len(src_aps)):
                tq = mm(b.ap[:, 0:w], ones[:, 0:128], sq[i], i == 0, i == len(src_aps) - 1, ta, b.free, t_const,
                        inc=(i == len(src_aps) - 1))
            tv = ts(o, b.ap[:, 0:w], 1.0 / n, EPS, ALU.mult, ALU.add, tq)
            b.free = tv
            ta = act_(o, o, ACT.Sqrt, tv)
            return recip(o, o, ta)

        def av_T(o, v0, v1, w, *after):
            mm(o[:, 0:256], v0, w[:, 0:256], True, False, *after)
            return mm(o[:, 128:256], v1, w[:, 256:384], False, True, inc=True)

        t_h = t_x
        tA = norm_T("attn_norm", carve(4096, 24576), t_h, None)

        V1 = carve(4096, 0).rearrange("p (t c) -> p t c", t=2)
        Qa = carve(1024)
        Ka = carve(1024)
        Ga = carve(1024)
        Gs = carve(1024)
        QK = carve(6144).rearrange("p (i t) -> p i t", t=256)
        MIX = carve(4096).rearrange("p (k t) -> p k t", t=256)
        base1 = at[0]
        X = [carve(1024), carve(1024)]
        EX = carve(1024)
        AT = carve(1536)
        DL = carve(512)
        M = carve(128 * 8)
        DIST = carve(384)
        CM = carve(384)
        SQ = carve(1024)
        RS = carve(1024)
        base2 = at[0]

        tp = rows8(w1v, 16, lambda k, t: actT[:, k, t * 128:(t + 1) * 128], tA)
        for t in range(2):
            for c in range(4):
                b = banks[t * 4 + c]
                b.free = t_v1 = cp(V1[:, t, c * 512:(c + 1) * 512], b.ap, tp)

        t_m = memset(P, M, 0.0, tA)
        for li in range(7):
            L = 1 << li
            m = M[:, li * 128:(li + 1) * 128].rearrange("p (b u l) -> p b u l", u=2, l=L)[:, :, 1, :]
            n = 64 // L
            memset(P, m, 1.0)
            asel(m, m, [[-2 * L, n], [0, L]], ALU.is_ge, 0.0, 0, 1)
            asel(m, m, [[2 * L, n], [0, L]], ALU.is_ge, 0.0, L - 1, -1)
        cp_m = P.op(lambda e: e.tensor_copy(M[:, 896:1024], ident[:, :]))
        memset(P, CM, 0.0)
        for o in (0, 256):
            asel(CM[:, o:o + 128], CM[:, o:o + 128], [[-1, 128]], ALU.is_ge, NEG, 0, 1)
        for o, base in ((0, 0), (128, -128), (256, 0)):
            P.op(lambda e, o=o, base=base: e.iota(DIST[:, o:o + 128], pattern=[[1, 128]], base=base,
                                                  channel_multiplier=-1, allow_small_or_imprecise_dtypes=True))
        for o in (0, 256):
            t_masks = asel(DIST[:, o:o + 128], DIST[:, o:o + 128], [[-1, 128]], ALU.is_ge, -1e33, 0, 1)

        lbv = small[:, 16:20]
        lb1 = small[:, 20:24]
        tv = tt(lbv, cols[:, COFF["lb"]:COFF["lb"] + 4], cols[:, COFF["lb"]:COFF["lb"] + 4], ALU.subtract, t_cols)
        ta = act_(lbv, lbv, ACT.Exp, tv)
        recip(lb1, lbv, ta)
        tt(lb1, lbv, lb1, ALU.mult)
        tt(lbv, lb1, lb1, ALU.subtract)
        t_lb = ts(lb1, lbv, -1.0, 1.0, ALU.mult, ALU.add)

        def sink_hg(i, m, b, tp):
            if i < 4:
                return act_(Qa[:, i * 256:i * 256 + 512], b.ap, ACT.Silu, tp)
            if i < 8:
                j = (i - 4) * 256
                act_(Ga[:, j:j + 512], b.ap, ACT.Sigmoid, tp)
                return act_(Ka[:, j:j + 512], b.ap, ACT.Sigmoid, tp, scale=-1.0)
            j = (i - 8) * 256
            return act_(Gs[:, j:j + 512], b.ap, ACT.Silu, tp)

        fm_tiles(w1fm, 0, 12, tA, sink_hg)
        t_hg = (A.sem, A.n)
        for i in range(4):
            r = slice(i * 256, i * 256 + 256)
            ts(Ga[:, r], Ga[:, r], lb1[:, i:i + 1], lbv[:, i:i + 1], ALU.mult, ALU.add, t_hg)
            ts(Ka[:, r], Ka[:, r], lb1[:, i:i + 1], None, ALU.mult, None)
        ts(EX, Ga, 1e-30, 1e18, ALU.max, ALU.mult)
        ts(EX, EX, 1.0, None, ALU.min, None)
        tv = ts(Ga, Ga, 1e-18, None, ALU.max, None)
        act_(EX, EX, ACT.Ln, tv)
        ta = act_(Ga, Ga, ACT.Ln)
        memset(V, AT, 0.0)
        t_g = tt(Ga, Ga, EX, ALU.add, ta)

        fsb = carve(96 + 768, base2)
        wf = fsb[:, 0:96]
        s_f = sem("s_f")
        t_wf = S.dma(wf, w1f, s_f, 1, tA)

        def sink_qk(off):
            def sink(i, m, b, tp):
                return cp(QK[:, off + i:off + i + 2, :], b.ap.rearrange("p (a t) -> p a t", a=2), tp)
            return sink

        def qk_norm(i, gain, extra, t_in):
            src = arena[:, 8192 + i * 256:8192 + i * 256 + 512]
            t = rs_bcast(RS[:, 0:512], [src], 128, t_in, (V.sem, V.n), [SQ[:, 0:512]])
            return stt(src, src, small[:, gain:gain + 1], RS[:, 0:512], ALU.mult, ALU.mult, t)

        for i, (n, s) in enumerate((("foxq", SCALE), ("foxk", 1.0), ("mobq", SCALE), ("mobk", 1.0))):
            ts(small[:, 24 + i:25 + i], col(n), s, None, ALU.mult, None, t_cols)

        def hgrn_level(li):
            L = 1 << li
            x_ = X[li % 2]
            pv = Ga.rearrange("p (b u l) -> p b u l", u=2, l=L)
            ev = EX.rearrange("p (b u l) -> p b u l", u=2, l=L)
            xv = x_.rearrange("p (b u l) -> p b u l", u=2, l=L)
            qv = Qa.rearrange("p (b u l) -> p b u l", u=2, l=L)
            kv = Ka.rearrange("p (b u l) -> p b u l", u=2, l=L)
            tot = pv[:, :, 0, L - 1:L].to_broadcast([128, 512 // L, L])
            dl = DL.rearrange("p (b l) -> p b l", l=L)
            tv = tt(dl, tot, pv[:, :, 0, :], ALU.subtract)
            act_(ev[:, :, 1, :], pv[:, :, 1, :], ACT.Exp, t_g, tv)
            ta = act_(ev[:, :, 0, :], dl, ACT.Exp, tv)
            tt(xv[:, :, 1, :], qv[:, :, 1, :], ev[:, :, 1, :], ALU.mult, ta, xfree[li % 2])
            tv = tt(xv[:, :, 0, :], kv[:, :, 0, :], ev[:, :, 0, :], ALU.mult)
            if L < 128:
                tt(pv[:, :, 1, :], pv[:, :, 1, :], tot, ALU.add)
            return tv

        at4 = AT.rearrange("p (h w) -> p h w", h=4)
        xfree = [None, None]

        def hgrn_mm(lhs, rhs, li, tv):
            for t in range(2):
                b = bank()
                for hh in range(4):
                    tp = mm(b.ap[:, hh * 128:(hh + 1) * 128], lhs[:, hh * 256 + t * 128:hh * 256 + t * 128 + 128],
                            rhs[:, hh * 256 + t * 128:hh * 256 + t * 128 + 128], True, True, tv, b.free,
                            inc=(hh == 3))
                mk = M[:, li * 128:(li + 1) * 128].bitcast(I32)
                b.free = V.op(lambda e, t=t, b=b, mk=mk: e.copy_predicated(
                    at4[:, :, t * 256:t * 256 + 128], bm(mk, 4), b.ap.rearrange("p (h w) -> p h w", h=4)), tp, t_masks)
            return tp

        fm_tiles(w1fm, 12, 12, tA, sink_qk(0))
        t_qk1 = (A.sem, A.n)
        hgrn_mm(Ka, Qa, 7, t_g)
        for li in range(7):
            tv = hgrn_level(li)
            xfree[li % 2] = hgrn_mm(X[li % 2], X[li % 2], li, tv)
        tv = hgrn_level(7)
        b = bank()
        for hh in range(4):
            tp = mm(b.ap[:, hh * 128:(hh + 1) * 128], X[1][:, hh * 256:hh * 256 + 128],
                    X[1][:, hh * 256 + 128:hh * 256 + 256], True, True, tv, b.free, inc=(hh == 3))
        b.free = t_at = cp(at4[:, :, 128:256], b.ap.rearrange("p (h w) -> p h w", h=4), tp, (V.sem, V.n))

        fm_tiles(w1fm, 24, 12, tA, sink_qk(12))
        t_qk2 = (A.sem, A.n)
        b = bank()
        for k in range(16):
            tp = mm(b.ap[0:6, 0:256], wf[:, k * 6:k * 6 + 6], actT[:, k, :], k == 0, k == 15, tA, t_wf, b.free,
                    inc=(k == 15))
        FX = fsb[0:6, 96:352]
        FL = fsb[0:6, 352:608]
        FN = fsb[0:6, 608:864]
        ts(FX, b.ap[0:6, 0:256], col("bf", 0, 6), None, ALU.add, None, tp)
        b.free = (V.sem, V.n)
        act_(FL, FX, ACT.Abs, (V.sem, V.n))
        act_(FL, FL, ACT.Exp, scale=-1.0)
        ta = act_(FL, FL, ACT.Ln, bias=1.0)
        stt(FX, FX, 0.0, FL, ALU.min, ALU.subtract, ta)
        V.op(lambda e: e.tensor_tensor_scan(FL, ones[0:6, 0:256], FX, 0.0, ALU.mult, ALU.add), t_const)
        ts(FN, FL, -1.0, None, ALU.mult, None)
        FMK = carve(1536)
        SEL = carve(768)
        fmk = FMK[0:6, :].rearrange("p (h t) -> p h t", h=6)
        sel = SEL[0:6, :].rearrange("p (h t) -> p h t", h=6)
        tt(fmk, bm(FL, 6), bc(ident[0:6, 0:6], 256), ALU.mult, t_id)
        t_fm = V.op(lambda e: e.tensor_copy(sel, bc(ident[0:6, 0:6], 128)))

        for hp in range(2):
            b = bank()
            for j in range(2):
                hh = 2 * hp + j
                tp = av_T(b.ap[:, j * 256:j * 256 + 256], V1[:, 0, hh * 128:(hh + 1) * 128],
                          V1[:, 1, hh * 128:(hh + 1) * 128], at4[:, hh, :], t_at, t_v1, (V.sem, V.n), b.free)
            t = rs_bcast(RS[:, 0:512], [b.ap], 128, tp, (V.sem, V.n), [SQ[:, 0:512]])
            stt(RS[:, 0:512], b.ap, col("hgrn"), RS[:, 0:512], ALU.mult, ALU.mult, t)
            b.free = (V.sem, V.n)
            t_mix = tt(arena[:, 14336 + hp * 512:14336 + hp * 512 + 512], RS[:, 0:512], Gs[:, hp * 512:hp * 512 + 512],
                       ALU.mult)
        for i in range(0, 24, 2):
            t_n = qk_norm(i, 24 + i // 6, None, t_qk1 if i < 12 else t_qk2)

        LG = carve(1536, base1)
        WT = carve(1536)
        lg = LG.rearrange("p (h w) -> p h w", h=4)
        wt_free = None
        for g in range(3):
            bs = []
            for j in range(4):
                hd = g * 4 + j
                fox = hd < 6
                qi, ki = (hd, 6 + hd) if fox else (6 + hd, 12 + hd)
                b = bank()
                bs.append(b)
                for qt, o, kl in ((0, 0, 128), (1, 128, 256)):
                    q = QK[:, qi, qt * 128:(qt + 1) * 128]
                    tp = mm(b.ap[:, o:o + kl], q, QK[:, ki, 0:kl], True, not fox, t_n, t_fm, b.free, inc=not fox)
                    if fox:
                        mm(b.ap[:, o:o + kl], fmk[:, hd, qt * 128:(qt + 1) * 128], ones[0:6, 0:kl], False, False)
                        tp = mm(b.ap[:, o:o + kl], sel[:, hd, :], FN[:, 0:kl], False, True, inc=True)
                if fox:
                    b.free = tt(lg[:, j, :], b.ap[:, 0:384], CM, ALU.add, tp, t_masks)
                else:
                    b.free = stt(lg[:, j, :], DIST, SLOPES[hd - 6], b.ap[:, 0:384], ALU.mult, ALU.add, tp, t_masks)
            mx = small[:, 32:36]
            mx1 = small[:, 36:40]
            V.op(lambda e: e.tensor_reduce(small[:, 32:36], lg[:, :, 0:128], AX.X, ALU.max, negate=True))
            tv = V.op(lambda e: e.tensor_reduce(small[:, 36:40], lg[:, :, 128:384], AX.X, ALU.max, negate=True))
            for j in range(4):
                act_(lg[:, j, 0:128], lg[:, j, 0:128], ACT.Exp, tv, bias=mx[:, j:j + 1], acc=small[:, 40 + j:41 + j])
                ta = act_(lg[:, j, 128:384], lg[:, j, 128:384], ACT.Exp, bias=mx1[:, j:j + 1],
                          acc=small[:, 44 + j:45 + j])
            recip(small[:, 48:56], small[:, 40:48], ta)
            tt(lg[:, :, 0:128], lg[:, :, 0:128], bc(small[:, 48:52], 128), ALU.mult)
            tv = tt(lg[:, :, 128:384], lg[:, :, 128:384], bc(small[:, 52:56], 256), ALU.mult)
            for j in range(4):
                hd = g * 4 + j
                b = bank()
                for i in range(3):
                    tp = tr(b.ap[:, i * 128:(i + 1) * 128], lg[:, j, i * 128:(i + 1) * 128], tv, b.free, inc=(i == 2))
                w = WT[:, j * 384:(j + 1) * 384]
                ta = b.free = cp(w, b.ap[:, 0:384], tp, wt_free)
                b2 = bank()
                vo = 512 + hd * 128
                tp = av_T(b2.ap, V1[:, 0, vo:vo + 128], V1[:, 1, vo:vo + 128], w, ta, t_v1, b2.free)
                b2.free = ta = cp(MIX[:, 4 + hd, :], b2.ap[:, 0:256], tp)
            wt_free = tp
        tp = rows8(wo1, 16, lambda k, t: MIX[:, k, t * 128:(t + 1) * 128], [t_mix, ta])
        t_h = add_h(tp)

        HT = carve(11264, 0).rearrange("p (k t) -> p k t", t=256)
        PAD = carve(2 * 258)
        CV = carve(2 * 256)
        tA = norm_T("ffn_norm", carve(4096, 24576), t_h, None)
        memset(V, PAD, 0.0)
        for i in range(44):
            b = bank()
            for j in range(2):
                s, tl = load(wgu[2 * i + j, :, :])
                for k in range(16):
                    tp = mm(b.ap[:, j * 256:j * 256 + 256], s.ap[:, k * 128:(k + 1) * 128], actT[:, k, :],
                            k == 0, k == 15, tA, tl, b.free, inc=(k == 15))
                s.free = tp
            pd = PAD[:, (i % 2) * 258:(i % 2) * 258 + 258]
            cv = CV[:, (i % 2) * 256:(i % 2) * 256 + 256]
            ta = cp(pd[:, 2:258], b.ap[:, 0:256], tp, (V.sem, V.n))
            ts(cv, pd[:, 0:256], col("cw0", i), col("cb", i), ALU.mult, ALU.add, ta)
            stt(cv, pd[:, 1:257], col("cw1", i), cv, ALU.mult, ALU.add)
            tv = stt(cv, pd[:, 2:258], col("cw2", i), cv, ALU.mult, ALU.add)
            ta = act_(cv, cv, ACT.Gelu_apprx_tanh, tv)
            b.free = t_ht = tt(HT[:, i, :], cv, b.ap[:, 256:512], ALU.mult, ta)
        tp = rows8(wdn, 44, lambda k, t: HT[:, k, t * 128:(t + 1) * 128], t_ht)
        t_h = add_h(tp)

        tA = norm_T("ple_norm", carve(4096, 24576), t_h, None)
        SG = carve(4096, 0).rearrange("p (t d) -> p t d", t=2)
        PT = carve(512)
        s_pt = sem("s_pt")
        t_pt = S.dma(PT, pT, s_pt, 1, tp)
        tp = rows8(plg, 16, lambda k, t: actT[:, k, t * 128:(t + 1) * 128], tA)
        for t in range(2):
            for c in range(4):
                b = banks[t * 4 + c]
                b.free = t_sg = act_(SG[:, t, c * 512:(c + 1) * 512], b.ap, ACT.Sigmoid, tp)
        tp = rows8(plp, 2, lambda k, t: PT[:, k * 256 + t * 128:k * 256 + (t + 1) * 128], t_pt)
        for t in range(2):
            for c in range(4):
                b = banks[t * 4 + c]
                g = SG[:, t, c * 512:(c + 1) * 512]
                b.free = tt(g, g, b.ap, ALU.mult, tp, t_sg)
        t_h = tt(hsb[:, :], hsb[:, :], arena[:, 0:4096], ALU.add)

        tA = norm_T("attn_norm_2", carve(4096, 24576), t_h, None)
        V2 = carve(2048, 0).rearrange("p (t c) -> p t c", t=2)
        QK = carve(4096).rearrange("p (i t) -> p i t", t=256)
        Z = carve(2048)
        XB = carve(3072).rearrange("p (i t) -> p i t", t=256)
        MIX = carve(4096).rearrange("p (k t) -> p k t", t=256)
        XF = carve(2048).rearrange("p (t c) -> p t c", t=2)
        SQ = carve(2048)
        RS = carve(512)
        PAD = carve(2 * 2 * 259)
        SM = carve(384)
        NM = carve(384)
        SI = carve(384)
        SP = carve(3072).rearrange("p (h w) -> p h w", h=8)
        LM = carve(3072).rearrange("p (h w) -> p h w", h=8)
        LT = carve(384)
        W2D = carve(256)

        t_z = memset(P, SM, 1.0, t_h)
        memset(P, SI, 1.0)
        memset(P, NM, 0.0)
        for o in (0, 256):
            asel(SM[:, o:o + 128], SM[:, o:o + 128], [[1, 128]], ALU.is_gt, 0.0, 0, -1)
            asel(SI[:, o:o + 128], SI[:, o:o + 128], [[1, 128]], ALU.is_ge, 0.0, 0, -1)
            t_masks = asel(NM[:, o:o + 128], NM[:, o:o + 128], [[1, 128]], ALU.is_gt, NEG, 0, -1)
        s_d = sem("s_d")
        t_wd = S.dma(W2D, w2d, s_d, 1, tp, t_h)

        for k2 in range(8):
            s, tl = load(w2v[k2, :, :])
            for kk in range(2):
                k = 2 * k2 + kk
                for t in range(2):
                    for c in range(2):
                        b = banks[t * 2 + c]
                        tp = mm(b.ap, actT[:, k, t * 128:(t + 1) * 128],
                                s.ap[:, kk * 1024 + c * 512:kk * 1024 + (c + 1) * 512], k == 0, k == 15,
                                tA, tl, b.free if k == 0 else None, inc=(kk == 1 and t == 1 and c == 1))
            s.free = tp
        for t in range(2):
            for c in range(2):
                b = banks[t * 2 + c]
                b.free = t_v2 = cp(V2[:, t, c * 512:(c + 1) * 512], b.ap, tp)
        nb[0] = 4

        memset(V, PAD, 0.0)
        ncv = [0]

        def sink_xbc(i, m, b, tp):
            for j in range(2):
                c = i + j
                w = (ncv[0] % 4) * 259
                ncv[0] += 1
                pd = PAD[:, w:w + 259]
                ta = cp(pd[:, 3:259], b.ap[:, j * 256:j * 256 + 256], tp, (V.sem, V.n))
                xo = XB[:, c, :]
                ts(xo, pd[:, 0:256], col("c20", c), col("cb2", c), ALU.mult, ALU.add, ta)
                stt(xo, pd[:, 1:257], col("c21", c), xo, ALU.mult, ALU.add)
                stt(xo, pd[:, 2:258], col("c22", c), xo, ALU.mult, ALU.add)
                tv = stt(xo, pd[:, 3:259], col("c23", c), xo, ALU.mult, ALU.add)
                act_(xo, xo, ACT.Silu, tv)
            return ta

        fm_tiles(w2fm, 24, 12, tA, sink_xbc)
        t_xb = (A.sem, A.n)
        fm_tiles(w2fm, 16, 8, tA, lambda i, m, b, tp: act_(Z[:, i * 256:i * 256 + 512], b.ap, ACT.Silu, tp))
        t_z = (A.sem, A.n)
        b = bank()
        for k in range(16):
            tp = mm(b.ap[0:16, 0:256], W2D[:, k * 16:k * 16 + 16], actT[:, k, :], k == 0, k == 15, tA, t_wd, b.free,
                    inc=(k == 15))
        DT = oh[0:16, 0:256]
        DA = oh[0:16, 256:512]
        CS = oh[0:16, 512:768]
        R = oh[0:16, 768:1152]
        AC = small[0:16, 60:61]
        ts(DT, b.ap[0:16, 0:256], col("dtb", 0, 16), None, ALU.add, None, tp)
        tv = b.free = (V.sem, V.n)
        act_(DA, DT, ACT.Abs, tv)
        act_(DA, DA, ACT.Exp, scale=-1.0)
        act_(DA, DA, ACT.Ln, bias=1.0)
        ta = act_(AC, col("alog", 0, 16), ACT.Exp)
        stt(DT, DT, 0.0, DA, ALU.max, ALU.add, ta)
        ts(AC, AC, -1.0, None, ALU.mult, None)
        ts(DA, DT, AC, None, ALU.mult, None)
        for t in range(2):
            r = slice(t * 128, t * 128 + 128)
            V.op(lambda e, r=r: e.tensor_tensor_scan(CS[:, r], ones[0:16, 0:128], DA[:, r], 0.0, ALU.mult, ALU.add),
                 t_const)
        V.op(lambda e: e.tensor_copy(R[:, 0:128], CS[:, 0:128]))
        V.op(lambda e: e.tensor_copy(R[:, 256:384], CS[:, 128:256]))
        t_R = ts(R[:, 128:256], CS[:, 128:256], CS[:, 127:128], None, ALU.add, None)
        SEL = carve(2048)
        selh = SEL[0:16, :].rearrange("p (h t) -> p h t", h=16)
        t_sel = V.op(lambda e: e.tensor_copy(selh, bc(ident[0:16, 0:16], 128)), t_id)
        b = bank()
        for a, src in enumerate((DT, CS)):
            for t in range(2):
                tp = T.op(lambda e, a=a, t=t, src=src, b=b: e.transpose(
                    b.ap[:, a * 32 + t * 16:a * 32 + t * 16 + 16], src[:, t * 128:(t + 1) * 128], ident[0:16, 0:16]),
                    t_R, b.free, inc=(a == 1 and t == 1))
        TK = small[:, 64:128]
        b.free = t_tk = V.op(lambda e, b=b: e.tensor_copy(TK, b.ap[:, 0:64]), tp)
        for t in range(2):
            for c2 in range(2):
                b = bank()
                for i in range(4):
                    tp = tr(b.ap[:, i * 128:(i + 1) * 128], XB[:, c2 * 4 + i, t * 128:(t + 1) * 128], t_xb, b.free,
                            inc=(i == 3))
                b.free = t_xf = tt(XF[:, t, c2 * 512:(c2 + 1) * 512].rearrange("p (h c) -> p h c", c=64),
                                   b.ap.rearrange("p (h c) -> p h c", c=64),
                                   bc(TK[:, t * 16 + c2 * 8:t * 16 + c2 * 8 + 8], 64), ALU.mult, tp)
        fm_tiles(w2fm, 0, 16, tA, lambda i, m, b, tp: cp(QK[:, i:i + 2, :], b.ap.rearrange("p (a t) -> p a t", a=2), tp))
        t_qk = (A.sem, A.n)

        CB = LM
        for g in range(2):
            b = bank()
            bmT = XB[:, 8 + g, :]
            cmT = XB[:, 10 + g, :]
            mm(b.ap[:, 0:256], bmT[:, 0:128], cmT[:, 0:256], True, True, t_xb, b.free)
            tp = mm(b.ap[:, 256:384], bmT[:, 128:256], cmT[:, 128:256], True, True, inc=True)
            b.free = tt(CB[:, g, :], b.ap[:, 0:384], SI, ALU.mult, tp, t_masks)
        sc_free = [None, None]
        t_y = None
        for pr in range(8):
            by = bank()
            for j in range(2):
                hd = 2 * pr + j
                b = bank()
                sc = SP[:, hd % 2, :]
                tp = mm(b.ap[:, 0:384], selh[:, hd, :], R, True, True, t_sel, t_R, b.free, inc=True)
                ts(sc[:, 0:256], b.ap[:, 0:256], TK[:, 32 + hd:33 + hd], 0.0, ALU.subtract, ALU.min, tp, sc_free[hd % 2])
                tv = ts(sc[:, 256:384], b.ap[:, 256:384], TK[:, 48 + hd:49 + hd], 0.0, ALU.subtract, ALU.min)
                b.free = tv
                ta = act_(sc, sc, ACT.Exp, tv)
                tv = tt(sc, sc, CB[:, hd // 8, :], ALU.mult, ta)
                yo = by.ap[j * 64:j * 64 + 64, :]
                mm(yo[:, 0:256], XF[:, 0, hd * 64:hd * 64 + 64], sc[:, 0:256], True, False, tv, t_xf, by.free)
                tp = mm(yo[:, 128:256], XF[:, 1, hd * 64:hd * 64 + 64], sc[:, 256:384], False, True, inc=True)
                sc_free[hd % 2] = tp
            y = MIX[:, 8 + pr, :]
            by.free = stt(y, XB[:, pr, :], col("dsk", pr), by.ap[:, 0:256], ALU.mult, ALU.add, tp)
            t_y = tt(y, y, Z[:, pr * 256:pr * 256 + 256], ALU.mult, t_z)
        sq8 = [SQ[:, i * 256:(i + 1) * 256] for i in range(8)]
        for g in range(2):
            t = rs_bcast(RS[:, 0:256], [MIX[:, 8 + g * 4 + i, :] for i in range(4)], 512, t_y, (T.sem, T.n), sq8[4 * g:4 * g + 4])
            for i in range(4):
                y = MIX[:, 8 + g * 4 + i, :]
                t_mix = stt(y, y, col("sso", g * 4 + i), RS[:, 0:256], ALU.mult, ALU.mult)

        ts(small[:, 28:29], col("sbq"), SCALE, None, ALU.mult, None)
        ts(small[:, 29:30], col("sbk"), 1.0, None, ALU.mult, None)
        for i in range(0, 16, 2):
            src = arena[:, 2048 + i * 256:2048 + i * 256 + 512]
            t = rs_bcast(RS[:, 0:512], [src], 128, t_qk, (V.sem, V.n), [SQ[:, 0:512]])
            g = 28 + i // 8
            t_n = stt(src, src, small[:, g:g + 1], RS[:, 0:512], ALU.mult, ALU.mult, t)
        for hd in range(8):
            b = bank()
            q, k = QK[:, hd, :], QK[:, 8 + hd, :]
            mm(b.ap[:, 0:256], k[:, 0:128], q[:, 0:256], True, True, t_n, b.free)
            tp = mm(b.ap[:, 256:384], k[:, 128:256], q[:, 128:256], True, True, inc=True)
            l = b.ap[:, 0:384]
            tt(LM[:, hd, :], l, NM, ALU.add, tp, t_masks)
            act_(LT, l, ACT.Abs, tp, (V.sem, V.n))
            act_(LT, LT, ACT.Exp, scale=-1.0)
            ta = act_(LT, LT, ACT.Ln, bias=1.0)
            stt(SP[:, hd, :], l, 0.0, LT, ALU.max, ALU.add, ta)
            b.free = [(V.sem, V.n), ta]
            tv = tt(SP[:, hd, :], SP[:, hd, :], SM, ALU.mult)
            b = bank()
            mm(b.ap[:, 0:256], tri[:, :], SP[:, hd, 0:256], True, False, tv, b.free)
            mm(b.ap[:, 128:256], ones[:, 0:128], SP[:, hd, 256:384], False, True)
            tp = mm(b.ap[:, 256:384], tri[:, :], SP[:, hd, 256:384], True, True, inc=True)
            b.free = tv = tt(LM[:, hd, :], LM[:, hd, :], b.ap[:, 0:384], ALU.subtract, tp)
            ta = act_(LM[:, hd, :], LM[:, hd, :], ACT.Exp, tv)
            b = bank()
            tp = av_T(b.ap, V2[:, 0, hd * 128:(hd + 1) * 128], V2[:, 1, hd * 128:(hd + 1) * 128], LM[:, hd, :],
                      ta, t_v2, b.free)
            b.free = ta = cp(MIX[:, hd, :], b.ap[:, 0:256], tp)
        t = rs_bcast(RS[:, 0:256], [MIX[:, i, :] for i in range(8)], 1024, ta, (V.sem, V.n), sq8)
        for i in range(8):
            t_mix = stt(MIX[:, i, :], MIX[:, i, :], col("sbo", i), RS[:, 0:256], ALU.mult, ALU.mult)
        tp = rows8(wo2, 16, lambda k, t: MIX[:, k, t * 128:(t + 1) * 128], t_mix)
        t_h = add_h(tp)

        tA = norm_T("ffn_norm_2", carve(4096, 28672), t_h, None)
        AG = arena[:, :].rearrange("p (i t) -> p i t", t=256)
        QT = carve(4096, 24576).rearrange("p (i t) -> p i t", t=256)
        SC = carve(2048, 8192)
        WK = carve(2048)
        CA = carve(2048)
        CW = carve(2048)
        TMP = carve(2048)
        TS_ = carve(256)
        TI = carve(256)
        BS = carve(128)
        BP = carve(128).bitcast(U32)
        BA = carve(128)
        BB = carve(128)
        TIU = carve(256).bitcast(U32)
        PK = carve(384)
        SK = carve(2048)
        I0 = 128
        s_sk = sem("s_sk")
        t_sk = S.dma(SK, sk, s_sk, 1, tp, t_h)
        fm_tiles(wq, 0, 16, tA, lambda i, m, b, tp: cp(QT[:, i:i + 2, :], b.ap.rearrange("p (a t) -> p a t", a=2), tp))
        t_q = (A.sem, A.n)
        nb[0] = 0
        tps = []
        for t in range(2):
            for i in range(16):
                b = banks[t * 4 + i // 4]
                tp = mm(b.ap[:, (i % 4) * 128:(i % 4) * 128 + 128], QT[:, i, t * 128:(t + 1) * 128],
                        SK[:, i * 128:(i + 1) * 128], True, True, t_q, t_sk, b.free, inc=(i == 15))
            tps.append(tp)
        sc3 = SC.rearrange("p (i k) -> p i k", k=128)
        wk3 = WK.rearrange("p (i k) -> p i k", k=128)
        ts3 = TS_.rearrange("p (i k) -> p i k", k=16)
        tu3 = TIU.rearrange("p (i k) -> p i k", k=16)
        pkd = None
        for t in range(2):
            for c in range(4):
                b = banks[t * 4 + c]
                b.free = cp(SC[:, c * 512:(c + 1) * 512], b.ap, tps[t], (V.sem, V.n))
            ta = b.free

            def top16(vals, work, best, pos, *after):
                V.op(lambda e: e.max(best[:, 0:8], vals), *after)
                V.op(lambda e: e.max_index(pos[:, 0:8], best[:, 0:8], vals))
                V.op(lambda e: e.match_replace(work, best[:, 0:8], vals, -3.0e38))
                V.op(lambda e: e.max(best[:, 8:16], work))
                V.op(lambda e: e.max_index(pos[:, 8:16], best[:, 8:16], work))

            for i in range(16):
                top16(sc3[:, i, :], wk3[:, i, :], ts3[:, i, :], tu3[:, i, :], ta)
            V.op(lambda e: e.tensor_copy(TI, TIU))
            for hd in range(8):
                ca = CA[:, hd * 256:(hd + 1) * 256].rearrange("p (a b) -> p a b", b=16)
                tt(ca, bc(ts3[:, 2 * hd, :], 16), bm(ts3[:, 2 * hd + 1, :], 16), ALU.add)
            for hd in range(8):
                r = slice(hd * 256, hd * 256 + 256)
                k = slice(hd * 16, hd * 16 + 16)
                top16(CA[:, r], CW[:, r], BS[:, k], BP[:, k])
            bs3 = BS.rearrange("p (h k) -> p h k", k=16)
            gg = PK[:, 256:384]
            g3 = gg.rearrange("p (h k) -> p h k", k=16)
            tv = tt(g3, bs3, bs3[:, :, 0:1].to_broadcast([128, 8, 16]), ALU.subtract, pkd)
            ta = act_(gg, gg, ACT.Exp, tv)
            V.op(lambda e: e.tensor_reduce(small[:, 128:136], g3, AX.X, ALU.add), ta)
            recip(small[:, 136:144], small[:, 128:136])
            tt(g3, g3, bc(small[:, 136:144], 16), ALU.mult)
            bau, bbu = BA.bitcast(U32), BB.bitcast(U32)
            V.op(lambda e: e.tensor_scalar(bau, BP, 4, None, ALU.logical_shift_right))
            V.op(lambda e: e.tensor_scalar(bbu, BP, 15, None, ALU.bitwise_and))
            V.op(lambda e: e.tensor_copy(BA, bau))
            V.op(lambda e: e.tensor_copy(BB, bbu))
            ti3 = TI.rearrange("p (h c k) -> p h c k", c=2, k=16)
            for c, pos in ((0, BA), (1, BB)):
                o3 = TMP.rearrange("p (n a) -> p n a", a=16)
                tt(o3, bc(pos, 16), bm(iot[:, 0:16], 128), ALU.is_equal)
                for hd in range(8):
                    o = TMP[:, hd * 256:(hd + 1) * 256].rearrange("p (k a) -> p k a", a=16)
                    tt(o, o, bm(ti3[:, hd, c, :], 16), ALU.mult)
                V.op(lambda e, c=c, o3=o3: e.tensor_reduce(PK[:, c * 128:(c + 1) * 128], o3, AX.X, ALU.add))
            b = banks[t]
            for c in range(3):
                tp = tr(b.ap[:, c * 128:(c + 1) * 128], PK[:, c * 128:(c + 1) * 128], (V.sem, V.n), b.free, inc=(c == 2))
            pkd = tp
            pk3 = picks[:, :].rearrange("p (c t) -> p c t", c=3)
            b.free = t_pk = V.op(lambda e, b=b, t=t: e.tensor_copy(
                pk3[:, :, t * 128:(t + 1) * 128], b.ap[:, 0:384].rearrange("p (c t) -> p c t", c=3)), tp)

        oh_free = [None, None]
        t_ag = None
        for q in range(64):
            b = bank()
            o = oh[:, (q % 2) * 1024:(q % 2) * 1024 + 1024]
            for j in range(4):
                t = 4 * q + j
                ts(o[:, j * 256:j * 256 + 128], iot[:, :], picks[:, t:t + 1], picks[:, 512 + t:513 + t],
                   ALU.is_equal, ALU.mult, t_pk, oh_free[q % 2])
                tv = ts(o[:, j * 256 + 128:j * 256 + 256], iot[:, :], picks[:, 256 + t:257 + t], None,
                        ALU.is_equal, None)
            for j in range(4):
                tp = mm(b.ap[:, j * 128:(j + 1) * 128], o[:, j * 256 + 128:j * 256 + 256], o[:, j * 256:j * 256 + 128],
                        True, True, tv, b.free, inc=(j == 3))
            oh_free[q % 2] = tp
            b.free = t_ag = cp(AG[:, :, 4 * q:4 * q + 4], b.ap.rearrange("p (t i) -> p i t", t=4), tp, t_pk)
        GE = [picks[:, 0:256], picks[:, 256:512]]
        for i in range(0, 128, 2):
            b = bank()
            for j in range(2):
                s, tl = load(dn[i + j, :, :])
                for k in range(16):
                    tp = mm(b.ap[:, j * 256:j * 256 + 256], s.ap[:, k * 128:(k + 1) * 128], actT[:, k, :],
                            k == 0, k == 15, tl, b.free, inc=(k == 15))
                s.free = tp
            ge = oh[:, (i // 2 % 2) * 512:(i // 2 % 2) * 512 + 512]
            b.free = ta = act_(ge, b.ap, ACT.Gelu, tp, (V.sem, V.n), oh_free)
            a2 = arena[:, i * 256:i * 256 + 512]
            t_act = tt(a2, a2, ge, ALU.mult, ta, t_ag)
        tp = rows8(up, 128, lambda k, t: AG[:, k, t * 128:(t + 1) * 128], t_act)
        t_h = add_h(tp)
        s_out = sem("s_out")
        t_o = S.dma(out.rearrange("(t p) d -> p t d", p=128), h[:, :, :], s_out, 1, t_h)
        S.q.append(([t_o], None, None))

        block = ctx.enter_context(nc.Block())

        @block.sync
        def _(e):
            last = S.q.pop()
            S.emit(e)
            for sm, v in last[0]:
                e.wait_ge(sm, v)

        @block.gpsimd
        def _(e):
            P.emit(e)

        @block.scalar
        def _(e):
            A.emit(e)

        @block.vector
        def _(e):
            V.emit(e)

        @block.tensor
        def _(e):
            T.emit(e)


def lay_out(d):
    g = {k: np.asarray(v) for k, v in d.items()}

    def c(a):
        return np.ascontiguousarray(a)

    def colz(v):
        v = v.reshape(-1)
        if v.size < 128:
            v = np.concatenate([v, np.zeros(128 - v.size, v.dtype)])
        return v.reshape(-1, 128).T

    def fm(w):
        k, n = w.shape
        return w.reshape(k // 128, 128, n // 128, 128).transpose(2, 1, 0, 3).reshape(n // 128, 128, k)

    wi = g["w_in"][0]
    s = [0, 512, 1024, 1536, 2048, 2816, 3584, 4352, 4358, 5126, 5894, 6662]
    aq, af, ai, ag, bq, bk, bv, bf, cq, ck, cv = [wi[:, s[i]:s[i + 1]] for i in range(11)]
    w2 = g["w_in_2"][0]
    q2, k2, v2, z2, x2, d2 = [w2[:, a:b] for a, b in ((0, 1024), (1024, 2048), (2048, 3072), (3072, 4096),
                                                      (4096, 5632), (5632, 5648))]
    par = {"attn_norm": g["attn_norm"], "ffn_norm": g["ffn_norm"], "ple_norm": g["ple_norm"],
           "attn_norm_2": g["attn_norm_2"], "ffn_norm_2": g["ffn_norm_2"], "lb": g["lb_logits"],
           "hgrn": g["hgrn_onorm"], "foxq": g["fox_qnorm"], "foxk": g["fox_knorm"], "mobq": g["moba_qnorm"],
           "mobk": g["moba_knorm"], "cw0": g["conv_w"][0, 0], "cw1": g["conv_w"][0, 1], "cw2": g["conv_w"][0, 2],
           "cb": g["conv_b"], "sbq": g["sb_q_norm_2"], "sbk": g["sb_k_norm_2"],
           "c20": g["conv_w_2"][0, 0], "c21": g["conv_w_2"][0, 1], "c22": g["conv_w_2"][0, 2],
           "c23": g["conv_w_2"][0, 3], "cb2": g["conv_b_2"], "sbo": g["sb_out_norm_2"], "sso": g["ssd_out_norm_2"],
           "dsk": np.repeat(g["d_skip_2"].reshape(-1), 64), "bf": g["fox_bf"], "dtb": g["dt_bias_2"],
           "alog": g["a_log_2"]}
    gu = np.stack([fm(g["w_gate"][0]), fm(g["w_up"][0])], 1).reshape(88, 128, 2048)
    return {
        "x": c(g["x"][0]),
        "pT": c(g["p"][0, 0].reshape(256, 2, 128).transpose(2, 1, 0).reshape(128, 512)),
        "cols": c(np.concatenate([colz(par[k]) for k, _ in COLS], 1)),
        "w1fm": c(fm(np.concatenate([aq, af, ag, bq, bk, cq, ck], 1))),
        "w1v": c(np.concatenate([ai, bv, cv], 1).reshape(16, 128, 2048)),
        "w1f": c(bf.reshape(16, 128, 6).transpose(1, 0, 2).reshape(128, 96)),
        "wo1": c(g["w_out"][0].reshape(16, 128, 2048)),
        "wgu": c(gu),
        "wdn": c(g["w_down"][0].reshape(44, 128, 2048)),
        "plg": c(g["w_ple_gate"][0].reshape(16, 128, 2048)),
        "plp": c(g["w_ple_proj"][0].reshape(2, 128, 2048)),
        "w2fm": c(fm(np.concatenate([q2, k2, z2, x2], 1))),
        "w2v": c(v2.reshape(8, 2, 128, 1024).transpose(0, 2, 1, 3).reshape(8, 128, 2048)),
        "w2d": c(d2.reshape(16, 128, 16).transpose(1, 0, 2).reshape(128, 256)),
        "wo2": c(g["w_out_2"][0].reshape(16, 128, 2048)),
        "wq": c(fm(g["peer_query_2"][0])),
        "sk": c(g["peer_sub_keys_2"][0].reshape(16, 128, 128).transpose(2, 0, 1).reshape(128, 2048)),
        "dn": c(g["peer_down_2"][0].reshape(128, 128, 16, 128).transpose(0, 3, 2, 1).reshape(128, 128, 2048)),
        "up": c(g["peer_up_2"][0].reshape(128, 128, 2048)),
    }


def kernel(**inputs):
    import concourse.bacc as bacc
    from concourse.bass_utils import run_bass_kernel_spmd

    arrays = lay_out(inputs)
    nc = bacc.Bacc("TRN2", target_bir_lowering=False, num_devices=1)
    args = [nc.dram_tensor(f"in_{k}", a.shape, mybir.dt.from_np(a.dtype), kind="ExternalInput").ap()
            for k, a in arrays.items()]
    o = nc.dram_tensor("out_0", (256, 2048), F32, kind="ExternalOutput").ap()
    build(nc, *args, o)
    r = run_bass_kernel_spmd(nc, [{f"in_{k}": a for k, a in arrays.items()}], core_ids=[0])
    return r.results[0]["out_0"].reshape(1, 256, 2048)
```

```python
import numpy as np
import concourse.bass as bass
from concourse import mybir
from contextlib import ExitStack

F32 = mybir.dt.float32
FR = mybir.dt.float32r
U32 = mybir.dt.uint32
I32 = mybir.dt.int32
ALU = mybir.AluOpType
ACT = mybir.ActivationFunctionType
AX = mybir.AxisListType

EPS = 1e-6
SCALE = 128.0 ** -0.5
NEG = -1e30
YFIRST = list(range(8, 16)) + list(range(8))
TOPK_PACE = 2
G_PACE = (3, 1)
SLOPES = [float(np.float32(2.0) ** np.float32(-8.0 * (i + 1) / 6.0)) for i in range(6)]

COLS = [("attn_norm", 16), ("ffn_norm", 16), ("ple_norm", 16), ("attn_norm_2", 16), ("ffn_norm_2", 16),
        ("lb", 4), ("hgrn", 1), ("foxq", 1), ("foxk", 1), ("mobq", 1), ("mobk", 1),
        ("cw0", 44), ("cw1", 44), ("cw2", 44), ("cb", 44), ("sbq", 1), ("sbk", 1),
        ("c20", 12), ("c21", 12), ("c22", 12), ("c23", 12), ("cb2", 12),
        ("sbo", 8), ("sso", 8), ("dsk", 8), ("bf", 1), ("dtb", 1), ("alog", 1)]
COFF = {}
_n = 0
for _k, _w in COLS:
    COFF[_k] = _n
    _n += _w
NCOL = _n


class Eng:

    def __init__(self, sem, chain):
        self.sem, self.n, self.q, self.chain = sem, 0, [], chain

    def op(self, fn, *after, inc=True, chain=None):
        waits = []
        stack = list(after)
        while stack:
            a = stack.pop(0)
            if isinstance(a, list):
                stack = a + stack
            elif a is not None:
                waits.append(a)
        if (self.chain if chain is None else chain) and self.n:
            waits.append((self.sem, self.n))
        if inc:
            self.n += 1
        self.q.append((waits, fn, (self.sem, 1) if inc else None))
        return (self.sem, self.n)

    def dma(self, out, in_, sem, count, *after):
        waits = []
        for a in after:
            waits += a if isinstance(a, list) else [a] if a is not None else []
        self.q.append((waits, lambda e: e.dma_start(out, in_), (sem, 16)))
        return (sem, 16 * count)

    def emit(self, eng):
        seen = {}
        for waits, fn, inc in self.q:
            for sem, v in waits:
                if seen.get(sem.name, 0) < v:
                    eng.wait_ge(sem, v)
                    seen[sem.name] = v
            ins = fn(eng)
            if inc is not None:
                ins.then_inc(*inc)


class Slot:
    def __init__(self, ap, sem=None):
        self.ap, self.sem, self.free, self.n = ap, sem, None, 0


def build(nc, x, pT, colsd, w1fm, w1v, wo1, wgu, wdn, plg, plp, w2fm, w2v, wo2, wq, sk, dn, up, out):
    ctx = ExitStack()
    with ctx:
        names = [0]

        def sb(name, n, dt=F32, at=None):
            return (at or ctx).enter_context(nc.sbuf_tensor(name, [128, n], dt))

        def sem(name):
            return ctx.enter_context(nc.semaphore(name))

        V = Eng(sem("s_v"), True)
        A = Eng(sem("s_a"), True)
        P = Eng(sem("s_p"), True)
        T = Eng(sem("s_t"), False)
        S = Eng(sem("s_s"), False)

        def vn():
            return (V.sem, V.n)

        def an():
            return (A.sem, A.n)

        def tn():
            return (T.sem, T.n)

        hsb = sb("hsb", 4096)
        h = hsb[:, :].rearrange("p (t d) -> p t d", t=2)
        AHt, ALt = sb("ah", 4096, FR), sb("al", 4096, FR)
        AH = AHt[:, :].rearrange("p (k t) -> p k t", k=16)
        AL = ALt[:, :].rearrange("p (k t) -> p k t", k=16)
        cols = sb("cols", NCOL)
        ident = sb("ident", 128)
        ones = sb("ones", 256)
        tri = sb("tri", 128)
        small = sb("small", 256)
        iot = sb("iot", 128)
        NRAW, NS, LA = 3, 4, 3
        rawt = sb("raw", NRAW * 1024)
        hit, lot = sb("whi", NS * 1024, FR), sb("wlo", NS * 1024, FR)
        raw = [Slot(rawt[:, i * 1024:(i + 1) * 1024], sem(f"s_w{i}")) for i in range(NRAW)]
        spl = [Slot((hit[:, i * 1024:(i + 1) * 1024], lot[:, i * 1024:(i + 1) * 1024])) for i in range(NS)]
        free_banks = [Slot(ctx.enter_context(nc.psum_tensor(f"b{i}", [128, 512], F32))[:, :]) for i in range(8)]

        def bank():
            return free_banks.pop(0)

        def give(b, *tok):
            b.free = list(tok)
            free_banks.append(b)

        def col(name, i=0, p=128):
            return cols[0:p, COFF[name] + i:COFF[name] + i + 1]

        phase = [None, None, 0]

        def arena(name, n):
            if phase[0] is not None:
                phase[0].close()
            phase[0] = ExitStack()
            phase[1] = sb(name, n, at=phase[0])
            phase[2] = 0
            return phase[1]

        def carve(n, where=None):
            if where is not None:
                phase[2] = where
            a = phase[1][:, phase[2]:phase[2] + n]
            phase[2] += n
            return a

        def mm(o, l, r, start, stop, *after, inc=False):
            return T.op(lambda e: e.matmul(o, l, r, start=start, stop=stop), *after, inc=inc)

        def mm3(o, l, r, start, stop, *after, inc=False):
            mm(o, l[0], r[0], start, False, *after)
            mm(o, l[0], r[1], False, False)
            return mm(o, l[1], r[0], False, stop, inc=inc)

        def tr(o, i, *after, inc=False, n=128):
            return T.op(lambda e: e.transpose(o, i, ident[0:n, 0:n]), *after, inc=inc)

        def act_(o, i, f, *after, bias=0.0, scale=1.0, acc=None):
            if acc is None:
                return A.op(lambda e: e.activation(o, i, f, bias=bias, scale=scale), *after)
            return A.op(lambda e: e.activation(o, i, f, bias=bias, scale=scale, accum_out=acc), *after)

        def cp(o, i, *after):
            return A.op(lambda e: e.activation(o, i, ACT.Copy), *after)

        def tt(o, a, b, op, *after, E=None):
            return (E or V).op(lambda e: e.tensor_tensor(o, a, b, op), *after)

        def ts(o, a, s1, s2, op0, op1, *after, E=None):
            if op1 is None:
                return (E or V).op(lambda e: e.tensor_scalar(o, a, s1, None, op0), *after)
            return (E or V).op(lambda e: e.tensor_scalar(o, a, s1, s2, op0, op1), *after)

        def stt(o, a, s, b, op0, op1, *after):
            return V.op(lambda e: e.scalar_tensor_tensor(out=o, in0=a, scalar=s, in1=b, op0=op0, op1=op1), *after)

        def recip(o, i, *after):
            return V.op(lambda e: e.reciprocal(o, i), *after)

        def memset(E, o, v, *after):
            return E.op(lambda e: e.memset(o, v), *after)

        def asel(o, i, pattern, op, fill, base, cm, *after):
            return P.op(lambda e: e.affine_select(out=o, in_=i, pattern=pattern, compare_op=op, fill=fill,
                                                  base=base, channel_multiplier=cm), *after)

        def bc(ap, n):
            return ap.unsqueeze(2).to_broadcast([ap.shape[0], ap.shape[1], n])

        def bm(ap, n):
            return ap.unsqueeze(1).to_broadcast([ap.shape[0], n, ap.shape[1]])

        def split(hi, lo, src, *after):
            ta = cp(hi, src, *after)
            return [ta, tt(lo, src, hi.bitcast(F32), ALU.subtract, ta)]

        def halves(src, n0, n1):
            return [src[i, :, j * 1024:(j + 1) * 1024] for i in range(n0, n1) for j in range(2)]

        def colhalves(src, n):
            return [src[k, :, c * 1024:(c + 1) * 1024] for c in range(2) for k in range(n)]

        seq = (colhalves(w1v, 16) + halves(w1fm, 0, 37) + colhalves(wo1, 16) + halves(wgu, 0, 88)
               + colhalves(wdn, 44) + colhalves(plg, 16) + colhalves(plp, 2)
               + [w2v[k, :, :] for k in range(16)] + halves(w2fm, 0, 37)
               + [wo2[k, :, c * 1024:(c + 1) * 1024] for c in range(2) for k in YFIRST] + halves(wq, 0, 16)
               + halves(dn, 0, 64) + [up[k, :, c * 1024:(c + 1) * 1024] for c in range(2) for k in range(64)]
               + halves(dn, 64, 128) + [up[k, :, c * 1024:(c + 1) * 1024] for c in range(2) for k in range(64, 128)])
        pumped, used = [0], [0]

        def pump(upto):
            while pumped[0] < min(upto + 1, len(seq)):
                n = pumped[0]
                pumped[0] += 1
                r, s = raw[n % NRAW], spl[n % NS]
                r.n += 1
                tl = S.dma(r.ap, seq[n], r.sem, r.n, r.free)
                s.tok = split(s.ap[0], s.ap[1], r.ap, tl, s.free)
                r.free = s.tok

        def unit():
            n = used[0]
            used[0] += 1
            pump(n + LA)
            return spl[n % NS]

        live = []

        def tick(n=1):
            for _ in range(n):
                for g in list(live):
                    try:
                        next(g)
                    except StopIteration:
                        live.remove(g)

        def drain():
            while live:
                tick()

        s_c = sem("s_c")
        t_cols = A.dma(cols[:, :], colsd, s_c, 1)
        s_x = sem("s_x")
        t_x = A.dma(h[:, :, :], x.rearrange("(t p) d -> p t d", p=128), s_x, 1)
        memset(P, ident[:, :], 0.0)
        t_id = asel(ident[:, :], ident[:, :], [[-1, 128]], ALU.not_equal, 1.0, 0, 1)
        memset(P, ones[:, :], 1.0)
        memset(P, tri[:, :], 1.0)
        asel(tri[:, :], tri[:, :], [[-1, 128]], ALU.is_ge, 0.0, 0, 1)
        t_const = P.op(lambda e: e.iota(iot[:, :], pattern=[[1, 128]], base=0, channel_multiplier=0,
                                        allow_small_or_imprecise_dtypes=True))

        def rsqrt(v, r, w, *after):
            ta = act_(r, v, ACT.Ln, *after)
            ta = act_(r, r, ACT.Exp, scale=-0.5)
            tt(w, r, r, ALU.mult, ta)
            tt(w, w, v, ALU.mult)
            ts(w, w, -0.5, 1.5, ALU.mult, ALU.add)
            return tt(r, r, w, ALU.mult)

        def squares(t, c, junk, *after):
            return act_(junk, h[:, t, c * 512:(c + 1) * 512], ACT.Square, *after, acc=small[:, t * 4 + c:t * 4 + c + 1])

        def norm_T(gain, xnt, t_sq):
            xn = xnt.rearrange("p (t d) -> p t d", t=2)
            V.op(lambda e: e.tensor_reduce(small[:, 8:10], small[:, 0:8].rearrange("p (t c) -> p t c", t=2),
                                           AX.X, ALU.add), t_sq)
            tv = ts(small[:, 10:12], small[:, 8:10], 1.0 / 2048, EPS, ALU.mult, ALU.add)
            tv = rsqrt(small[:, 10:12], small[:, 12:14], small[:, 14:16], tv)
            tx = {}
            for c in range(4):
                r = slice(c * 512, c * 512 + 512)
                tx[c, 0] = ts(xn[:, 0, r], h[:, 0, r], small[:, 12:13], None, ALU.mult, None)
                tx[c, 1] = act_(xn[:, 1, r], h[:, 1, r], ACT.Copy, tv, scale=small[:, 13:14])
            toks = []
            for g in range(8):
                b = bank()
                for k in (2 * g, 2 * g + 1):
                    for t in range(2):
                        o = (k % 2) * 256 + t * 128
                        tp = tr(b.ap[:, o:o + 128], xn[:, t, k * 128:(k + 1) * 128], tx[k // 4, 0], tx[k // 4, 1],
                                b.free, t_id, inc=(k % 2 == 1 and t == 1))
                for k in (2 * g, 2 * g + 1):
                    ta = act_(AH[:, k, :], b.ap[:, (k % 2) * 256:(k % 2) * 256 + 256], ACT.Copy, tp, t_cols,
                              scale=col(gain, k))
                for k in (2 * g, 2 * g + 1):
                    tv = stt(AL[:, k, :], b.ap[:, (k % 2) * 256:(k % 2) * 256 + 256], col(gain, k),
                             AH[:, k, :].bitcast(F32), ALU.mult, ALU.subtract, ta)
                    toks.append([ta, tv])
                give(b, tv, ta)
            return toks

        def fm_tiles(n, t_act, sink, every=1):
            for i in range(0, n, 2):
                b = bank()
                m = min(2, n - i)
                for j in range(m):
                    for kh in range(2):
                        s = unit()
                        for kk in range(8):
                            k = kh * 8 + kk
                            tp = mm3(b.ap[:, j * 256:j * 256 + 256],
                                     [a[:, kk * 128:(kk + 1) * 128] for a in s.ap], (AH[:, k, :], AL[:, k, :]),
                                     k == 0, k == 15, t_act[k], s.tok, b.free if k == 0 else None, inc=(kk == 7))
                        s.free = tp
                    if j < m - 1:
                        tick(every)
                give(b, *sink(i, m, b, tp))
                tick(every)

        def rows(ks, lhs, need, ev, halves=2, after=None):
            for ch in range(halves):
                bs = {(t, c): bank() for t in range(2) for c in range(2)}
                for n, k in enumerate(ks):
                    w = need(k)
                    s = unit()
                    for t in range(2):
                        for c in range(2):
                            b = bs[t, c]
                            last = n == len(ks) - 1
                            tp = mm3(b.ap, lhs(k, t), [a[:, c * 512:(c + 1) * 512] for a in s.ap], n == 0, last,
                                     s.tok, w, b.free if n == 0 else None, inc=last or (t == 1 and c == 1))
                    s.free = tp
                    if after is not None:
                        after(tp)
                    if n % 2 == 1:
                        tick()
                for t in range(2):
                    for c in range(2):
                        give(bs[t, c], *ev(t, 2 * ch + c, bs[t, c], tp))

        def add_h(t_sq):
            def ev(t, c, b, tp):
                r = slice(c * 512, c * 512 + 512)
                tv = tt(h[:, t, r], h[:, t, r], b.ap, ALU.add, tp)
                t_sq.append(squares(t, c, b.ap, tv))
                return [t_sq[-1]]
            return ev

        def act_lhs(k, t):
            return AH[:, k, t * 128:(t + 1) * 128], AL[:, k, t * 128:(t + 1) * 128]

        def rs_bcast(o, src_aps, n, sq, *after):
            w = o.shape[1]
            m = w // 128
            for i, a in enumerate(src_aps):
                ta = act_(sq[i], a, ACT.Square, *after)
            yield
            b = bank()
            c = small[:, 64 + 16 * rsn[0]:64 + 16 * rsn[0] + 16]
            rsn[0] = (rsn[0] + 1) % 12
            for j in range(m):
                for i in range(len(src_aps)):
                    tq = mm(b.ap[:, j:j + 1], sq[i][:, j * 128:(j + 1) * 128], ones[:, 0:1], i == 0,
                            i == len(src_aps) - 1, ta, b.free, t_const, inc=(j == m - 1 and i == len(src_aps) - 1))
            tv = ts(c[:, 0:m], b.ap[:, 0:m], 1.0 / n, EPS, ALU.mult, ALU.add, tq)
            give(b, tv)
            tv = rsqrt(c[:, 0:m], c[:, 4:4 + m], c[:, 8:8 + m], tv)
            yield
            b = bank()
            for j in range(m):
                tq = mm(b.ap[:, j * 128:(j + 1) * 128], c[:, 4 + j:5 + j].to_broadcast([128, 128]), ident[:, :],
                        True, True, tv, b.free, t_id, inc=(j == m - 1))
            o.tok, o.bank = tq, b

        rsn = [0]

        class Rs:
            def __init__(self, w):
                self.shape = (128, w)

        def av_T(o, v0, v1, w, *after):
            mm(o[:, 0:256], v0, w[:, 0:256], True, False, *after)
            return mm(o[:, 128:256], v1, w[:, 256:384], False, True, inc=True)

        arena("ar1", 28160)
        V1 = carve(4096, 0).rearrange("p (t c) -> p t c", t=2)
        Qa, Ka, Ga, Gs = carve(1024), carve(1024), carve(1024), carve(1024)
        xn = phase[1][:, phase[2]:phase[2] + 4096]
        QKf = carve(6144)
        X = [carve(1024), carve(1024)]
        EX = carve(1024)
        AT = carve(1536)
        DL = carve(512)
        M = carve(128 * 8)
        DIST = carve(384)
        CM = carve(384)
        FB = carve(768)
        FMK = carve(1536)
        SEL = carve(768)
        NB = 3
        SQb = [carve(512) for _ in range(NB)]
        LGb = [carve(384) for _ in range(NB)]
        WTb = [carve(384) for _ in range(NB)]
        HO = [X[0][:, 0:512], X[0][:, 512:1024]]

        t_sq = [squares(t, c, QKf[:, 4096:4608], t_x) for t in range(2) for c in range(4)]
        tA = norm_T("attn_norm", xn, t_sq[-1])
        tv0 = []

        def ev_v1(t, c, b, tp):
            tv0.append(cp(V1[:, t, c * 512:(c + 1) * 512], b.ap, tp))
            return [tv0[-1]]

        rows(range(16), act_lhs, lambda k: tA[k], ev_v1)
        t_v1 = tv0[-1]

        memset(P, M, 0.0)
        for li in range(7):
            L = 1 << li
            m = M[:, li * 128:(li + 1) * 128].rearrange("p (b u l) -> p b u l", u=2, l=L)[:, :, 1, :]
            n = 64 // L
            memset(P, m, 1.0)
            asel(m, m, [[-2 * L, n], [0, L]], ALU.is_ge, 0.0, 0, 1)
            asel(m, m, [[2 * L, n], [0, L]], ALU.is_ge, 0.0, L - 1, -1)
        P.op(lambda e: e.tensor_copy(M[:, 896:1024], ident[:, :]))
        memset(P, CM, 0.0)
        for o in (0, 256):
            asel(CM[:, o:o + 128], CM[:, o:o + 128], [[-1, 128]], ALU.is_ge, NEG, 0, 1)
        for o, base in ((0, 0), (128, -128), (256, 0)):
            P.op(lambda e, o=o, base=base: e.iota(DIST[:, o:o + 128], pattern=[[1, 128]], base=base,
                                                  channel_multiplier=-1, allow_small_or_imprecise_dtypes=True))
        for o in (0, 256):
            t_masks = asel(DIST[:, o:o + 128], DIST[:, o:o + 128], [[-1, 128]], ALU.is_ge, -1e33, 0, 1)

        lbv, lb1 = small[:, 16:20], small[:, 20:24]
        tv = tt(lbv, cols[:, COFF["lb"]:COFF["lb"] + 4], cols[:, COFF["lb"]:COFF["lb"] + 4], ALU.subtract, t_cols)
        ta = act_(lbv, lbv, ACT.Exp, tv)
        recip(lb1, lbv, ta)
        tt(lb1, lbv, lb1, ALU.mult)
        tt(lbv, lb1, lb1, ALU.subtract)
        ts(lb1, lbv, -1.0, 1.0, ALU.mult, ALU.add)

        for i, (n, s) in enumerate((("foxq", SCALE), ("foxk", 1.0), ("mobq", SCALE), ("mobk", 1.0), ("sbq", SCALE),
                                    ("sbk", 1.0))):
            t_gain = ts(small[:, 24 + i:25 + i], col(n), s, None, ALU.mult, None, t_cols)

        def sink_hg(i, m, b, tp):
            if i < 4:
                return [act_(Qa[:, i * 256:i * 256 + 512], b.ap, ACT.Silu, tp)]
            if i < 8:
                j = (i - 4) * 256
                return [act_(Gs[:, j:j + 512], b.ap, ACT.Silu, tp)]
            j = (i - 8) * 256
            act_(Ga[:, j:j + 512], b.ap, ACT.Sigmoid, tp)
            return [act_(Ka[:, j:j + 512], b.ap, ACT.Sigmoid, tp, scale=-1.0)]

        fm_tiles(12, tA, sink_hg)

        at4 = AT.rearrange("p (h w) -> p h w", h=4)
        OUT, MX = {}, {}

        def hgrn_mm(lhs, rhs, li, tv):
            for t in range(2):
                b = bank()
                for hh in range(4):
                    o = hh * 256 + t * 128
                    tp = mm(b.ap[:, hh * 128:(hh + 1) * 128], lhs[:, o:o + 128], rhs[:, o:o + 128], True, True, tv,
                            b.free, inc=(hh == 3))
                mk = M[:, li * 128:(li + 1) * 128].bitcast(I32)
                give(b, V.op(lambda e, t=t, b=b, mk=mk: e.copy_predicated(
                    at4[:, :, t * 256:t * 256 + 128], bm(mk, 4), b.ap.rearrange("p (h w) -> p h w", h=4)), tp, t_masks))
            return tp

        def hgrn(t_hg):
            for i in range(4):
                r = slice(i * 256, i * 256 + 256)
                ts(Ga[:, r], Ga[:, r], lb1[:, i:i + 1], lbv[:, i:i + 1], ALU.mult, ALU.add, t_hg)
                ts(Ka[:, r], Ka[:, r], lb1[:, i:i + 1], None, ALU.mult, None)
            yield
            ts(EX, Ga, 1e-30, 1e18, ALU.max, ALU.mult)
            ts(EX, EX, 1.0, None, ALU.min, None)
            tv = ts(Ga, Ga, 1e-18, None, ALU.max, None)
            act_(EX, EX, ACT.Ln, tv)
            ta = act_(Ga, Ga, ACT.Ln)
            yield
            memset(V, AT, 0.0)
            t_g = tt(Ga, Ga, EX, ALU.add, ta)
            yield
            hgrn_mm(Ka, Qa, 7, t_g)
            xfree = [None, None]
            for li in range(8):
                L = 1 << li
                x_ = X[li % 2]
                pv = Ga.rearrange("p (b u l) -> p b u l", u=2, l=L)
                ev = EX.rearrange("p (b u l) -> p b u l", u=2, l=L)
                xv = x_.rearrange("p (b u l) -> p b u l", u=2, l=L)
                qv = Qa.rearrange("p (b u l) -> p b u l", u=2, l=L)
                kv = Ka.rearrange("p (b u l) -> p b u l", u=2, l=L)
                tot = pv[:, :, 0, L - 1:L].to_broadcast([128, 512 // L, L])
                tv = tt(DL.rearrange("p (b l) -> p b l", l=L), tot, pv[:, :, 0, :], ALU.subtract)
                act_(ev[:, :, 1, :], pv[:, :, 1, :], ACT.Exp, tv)
                ta = act_(ev[:, :, 0, :], DL.rearrange("p (b l) -> p b l", l=L), ACT.Exp)
                yield
                tt(xv[:, :, 1, :], qv[:, :, 1, :], ev[:, :, 1, :], ALU.mult, ta, xfree[li % 2])
                tv = tt(xv[:, :, 0, :], kv[:, :, 0, :], ev[:, :, 0, :], ALU.mult)
                if L < 128:
                    tt(pv[:, :, 1, :], pv[:, :, 1, :], tot, ALU.add)
                    yield
                    xfree[li % 2] = hgrn_mm(x_, x_, li, tv)
            yield
            b = bank()
            for hh in range(4):
                tp = mm(b.ap[:, hh * 128:(hh + 1) * 128], x_[:, hh * 256:hh * 256 + 128],
                        x_[:, hh * 256 + 128:hh * 256 + 256], True, True, tv, b.free, inc=(hh == 3))
            t_at = cp(at4[:, :, 128:256], b.ap.rearrange("p (h w) -> p h w", h=4), tp, vn())
            give(b, t_at)
            yield
            for hp in range(2):
                b = bank()
                for j in range(2):
                    hh = 2 * hp + j
                    tp = av_T(b.ap[:, j * 256:j * 256 + 256], V1[:, 0, hh * 128:(hh + 1) * 128],
                              V1[:, 1, hh * 128:(hh + 1) * 128], at4[:, hh, :], t_at, t_v1, b.free)
                ta = cp(HO[hp], b.ap, tp)
                give(b, ta)
            for hp in range(2):
                rs = Rs(512)
                yield from rs_bcast(rs, [HO[hp]], 128, [EX[:, hp * 512:hp * 512 + 512]], ta, vn())
                tv = stt(HO[hp], HO[hp], col("hgrn"), rs.bank.ap, ALU.mult, ALU.mult, rs.tok)
                give(rs.bank, tv)
                tv = tt(HO[hp], HO[hp], Gs[:, hp * 512:hp * 512 + 512], ALU.mult)
                for j in range(2):
                    OUT[2 * hp + j] = HO[hp][:, j * 256:(j + 1) * 256], tv

        live.append(hgrn(an()))

        FX, FL, FN = [FB[0:6, i * 256:(i + 1) * 256] for i in range(3)]
        fmk = FMK[0:6, :].rearrange("p (h t) -> p h t", h=6)
        sel = SEL[0:6, :].rearrange("p (h t) -> p h t", h=6)
        tf = {}

        def fgate(tv):
            act_(FL, FX, ACT.Abs, tv)
            act_(FL, FL, ACT.Exp, scale=-1.0)
            ta = act_(FL, FL, ACT.Ln, bias=1.0)
            yield
            stt(FX, FX, 0.0, FL, ALU.min, ALU.subtract, ta)
            V.op(lambda e: e.tensor_tensor_scan(FL, ones[0:6, 0:256], FX, 0.0, ALU.mult, ALU.add), t_const)
            ts(FN, FL, -1.0, None, ALU.mult, None)
            tt(fmk, bm(FL, 6), bc(ident[0:6, 0:6], 256), ALU.mult, t_id)
            tf[0] = V.op(lambda e: e.tensor_copy(sel, bc(ident[0:6, 0:6], 128)))

        def sink_f(i, m, b, tp):
            tv = ts(FX, b.ap[0:6, 0:256], col("bf", 0, 6), None, ALU.add, None, tp)
            live.append(fgate(tv))
            return [tv]

        fm_tiles(1, tA, sink_f)

        buf_free = [None] * NB

        def head(hd, tin):
            fox = hd < 6
            n = hd % NB
            qk, sq, lg, wt = QKf[:, hd * 512:hd * 512 + 512], SQb[n], LGb[n], WTb[n]
            rs = Rs(512)
            yield from rs_bcast(rs, [qk], 128, [sq], tin, buf_free[n])
            for j in range(2):
                g = 24 + j + (0 if fox else 2)
                r = slice(j * 256, j * 256 + 256)
                tv = stt(qk[:, r], qk[:, r], small[:, g:g + 1], rs.bank.ap[:, r], ALU.mult, ALU.mult, rs.tok, t_gain)
            give(rs.bank, tv)
            yield
            b = bank()
            for qt, o, kl in ((0, 0, 128), (1, 128, 256)):
                tp = mm(b.ap[:, o:o + kl], qk[:, qt * 128:(qt + 1) * 128], qk[:, 256:256 + kl], True, not fox, tv,
                        b.free, inc=not fox)
                if fox:
                    mm(b.ap[:, o:o + kl], fmk[:, hd, qt * 128:(qt + 1) * 128], ones[0:6, 0:kl], False, False, tf[0])
                    tp = mm(b.ap[:, o:o + kl], sel[:, hd, :], FN[:, 0:kl], False, True, inc=True)
            if fox:
                tv = tt(lg, b.ap[:, 0:384], CM, ALU.add, tp, t_masks)
            else:
                tv = stt(lg, DIST, SLOPES[hd - 6], b.ap[:, 0:384], ALU.mult, ALU.add, tp, t_masks)
            give(b, tv)
            c = small[:, 40 + 8 * n:48 + 8 * n]
            V.op(lambda e: e.tensor_reduce(c[:, 0:1], lg[:, 0:128], AX.X, ALU.max, negate=True))
            tv = V.op(lambda e: e.tensor_reduce(c[:, 1:2], lg[:, 128:384], AX.X, ALU.max, negate=True))
            act_(lg[:, 0:128], lg[:, 0:128], ACT.Exp, tv, bias=c[:, 0:1], acc=c[:, 2:3])
            ta = act_(lg[:, 128:384], lg[:, 128:384], ACT.Exp, bias=c[:, 1:2], acc=c[:, 3:4])
            yield
            recip(c[:, 4:6], c[:, 2:4], ta)
            ts(lg[:, 0:128], lg[:, 0:128], c[:, 4:5], None, ALU.mult, None)
            tv = ts(lg[:, 128:384], lg[:, 128:384], c[:, 5:6], None, ALU.mult, None)
            yield
            b = bank()
            for i in range(3):
                tp = tr(b.ap[:, i * 128:(i + 1) * 128], lg[:, i * 128:(i + 1) * 128], tv, b.free, inc=(i == 2))
            ta = cp(wt, b.ap[:, 0:384], tp)
            give(b, ta)
            yield
            vo = 512 + hd * 128
            b = bank()
            tp = av_T(b.ap, V1[:, 0, vo:vo + 128], V1[:, 1, vo:vo + 128], wt, ta, t_v1, b.free)
            ta = cp(qk[:, 0:256], b.ap[:, 0:256], tp)
            give(b, ta)
            OUT[4 + hd] = qk[:, 0:256], ta
            buf_free[n] = tp

        qk_toks = []

        def sink_heads(i, m, b, tp):
            ta = cp(QKf[:, i * 256:i * 256 + 512], b.ap, tp)
            qk_toks.append(ta)
            return [ta]

        def run_heads():
            hd = 0
            mine = []
            while hd < 12 or mine:
                for g in list(mine):
                    try:
                        next(g)
                    except StopIteration:
                        mine.remove(g)
                if hd < 12 and len(mine) < NB and hd < len(qk_toks) and buf_ok(hd):
                    mine.append(head(hd, qk_toks[hd]))
                    hd += 1
                yield

        def buf_ok(hd):
            return hd < NB or (4 + hd - NB) in OUT

        live.append(run_heads())
        fm_tiles(24, tA, sink_heads)
        t_proj = tn()

        def mixed(srcs, ks, ahead=2):
            order = list(ks)

            def need(k):
                while k not in srcs:
                    tick()
                n = order.index(k)
                for q in order[n:n + 1 + ahead]:
                    if q in srcs and q not in MX:
                        a, tok = srcs[q]
                        MX[q] = split(AH[:, q, :], AL[:, q, :], a, tok, t_proj)
                return MX[k]
            return need

        t_sq = []
        rows(range(16), act_lhs, mixed(OUT, range(16)), add_h(t_sq))
        drain()

        arena("ar2", 4096)
        hth, htl = sb("hth", 11264, FR, phase[0]), sb("htl", 11264, FR, phase[0])
        HH = hth[:, :].rearrange("p (k t) -> p k t", t=256)
        HL = htl[:, :].rearrange("p (k t) -> p k t", t=256)
        xn = carve(4096)
        PADS = carve(4 * 514, 0)
        CVS = carve(4 * 256)
        tA = norm_T("ffn_norm", xn, t_sq[-1])
        memset(V, PADS, 0.0, tA[15])
        ht = {}
        pfree = [vn()] * 4

        def ffn_tile(i, pd, cv, ta):
            ts(cv, pd[:, 0:256], col("cw0", i), col("cb", i), ALU.mult, ALU.add, ta)
            stt(cv, pd[:, 1:257], col("cw1", i), cv, ALU.mult, ALU.add)
            tv = stt(cv, pd[:, 2:258], col("cw2", i), cv, ALU.mult, ALU.add)
            yield
            ta = act_(cv, cv, ACT.Gelu_apprx_tanh, tv)
            yield
            pfree[i % 4] = tv = tt(cv, cv, pd[:, 258:514], ALU.mult, ta)
            ta = cp(HH[:, i, :], cv, tv)
            yield
            ht[i] = [ta, tt(HL[:, i, :], cv, HH[:, i, :].bitcast(F32), ALU.subtract, ta)]

        def sink_ffn(i2, m, b, tp):
            i = i2 // 2
            pd, cv = PADS[:, (i % 4) * 514:(i % 4) * 514 + 514], CVS[:, (i % 4) * 256:(i % 4) * 256 + 256]
            ta = cp(pd[:, 2:514], b.ap, tp, pfree[i % 4])
            live.append(ffn_tile(i, pd, cv, ta))
            return [ta]

        fm_tiles(88, tA, sink_ffn)

        def need_ht(k):
            while k not in ht:
                tick()
            return ht[k]

        t_sq = []
        rows(range(44), lambda k, t: (HH[:, k, t * 128:(t + 1) * 128], HL[:, k, t * 128:(t + 1) * 128]), need_ht,
             add_h(t_sq))

        arena("ar3", 4096 + 4096 + 512)
        pth, ptl = sb("pth", 512, FR, phase[0]), sb("ptl", 512, FR, phase[0])
        xn = carve(4096)
        SG = carve(4096).rearrange("p (t d) -> p t d", t=2)
        PT = carve(512)
        tA = norm_T("ple_norm", xn, t_sq[-1])
        s_pt = sem("s_pt")
        t_pt = A.dma(PT, pT, s_pt, 1, t_sq[-1])
        t_pt = split(pth[:, :], ptl[:, :], PT, t_pt)

        def ev_sg(t, c, b, tp):
            return [act_(SG[:, t, c * 512:(c + 1) * 512], b.ap, ACT.Sigmoid, tp)]

        rows(range(16), act_lhs, lambda k: tA[k], ev_sg)
        t_sq = []

        def ev_ple(t, c, b, tp):
            r = slice(c * 512, c * 512 + 512)
            tt(SG[:, t, r], SG[:, t, r], b.ap, ALU.mult, tp, t_sg)
            tv = tt(h[:, t, r], h[:, t, r], SG[:, t, r], ALU.add)
            t_sq.append(squares(t, c, b.ap, tv))
            return [t_sq[-1]]

        t_sg = an()
        rows(range(2), lambda k, t: (pth[:, k * 256 + t * 128:k * 256 + t * 128 + 128],
                                     ptl[:, k * 256 + t * 128:k * 256 + t * 128 + 128]), lambda k: t_pt, ev_ple)

        arena("ar4", 27474)
        V2 = carve(2048).rearrange("p (t c) -> p t c", t=2)
        xn = phase[1][:, phase[2]:phase[2] + 4096]
        QKf = carve(4096)
        Z = carve(2048)
        XB = carve(3072).rearrange("p (i t) -> p i t", t=256)
        Y = carve(2048).rearrange("p (i t) -> p i t", t=256)
        XF = carve(2048).rearrange("p (t c) -> p t c", t=2)
        PADS = carve(3 * 518)
        SM, NM, SI = carve(384), carve(384), carve(384)
        SEL = carve(2048)
        CB = carve(768).rearrange("p (g w) -> p g w", g=2)
        SC = [carve(384) for _ in range(4)]
        SQb = [carve(512) for _ in range(NB)]
        SPb = [carve(384) for _ in range(NB)]
        LMb = [carve(384) for _ in range(NB)]
        DT, DA, CS = [carve(256)[0:16, :] for _ in range(3)]
        R = carve(384)[0:16, :]
        TK = carve(64)
        tA = norm_T("attn_norm_2", xn, t_sq[-1])

        memset(P, SM, 1.0, t_sq[-1])
        memset(P, SI, 1.0)
        memset(P, NM, 0.0)
        for o in (0, 256):
            asel(SM[:, o:o + 128], SM[:, o:o + 128], [[1, 128]], ALU.is_gt, 0.0, 0, -1)
            asel(SI[:, o:o + 128], SI[:, o:o + 128], [[1, 128]], ALU.is_ge, 0.0, 0, -1)
            t_masks2 = asel(NM[:, o:o + 128], NM[:, o:o + 128], [[1, 128]], ALU.is_gt, NEG, 0, -1)
        memset(V, PADS, 0.0)
        selh = SEL[0:16, :].rearrange("p (h t) -> p h t", h=16)
        t_sel = V.op(lambda e: e.tensor_copy(selh, bc(ident[0:16, 0:16], 128)), t_id)
        tv2 = []

        def ev_v2(t, c, b, tp):
            tv2.append(cp(V2[:, t, c * 512:(c + 1) * 512], b.ap, tp))
            return [tv2[-1]]

        rows(range(16), act_lhs, lambda k: tA[k], ev_v2, halves=1)
        t_v2 = tv2[-1]

        pfree = [t_sel] * 3
        xb_done = {}

        def conv4(i, pd, ta):
            for j in range(2):
                c, p, xo = i + j, pd[:, j * 259:(j + 1) * 259], XB[:, i + j, :]
                ts(xo, p[:, 0:256], col("c20", c), col("cb2", c), ALU.mult, ALU.add, ta)
                stt(xo, p[:, 1:257], col("c21", c), xo, ALU.mult, ALU.add)
                stt(xo, p[:, 2:258], col("c22", c), xo, ALU.mult, ALU.add)
                tv = stt(xo, p[:, 3:259], col("c23", c), xo, ALU.mult, ALU.add)
                if j == 1:
                    pfree[i // 2 % 3] = tv
                yield
                xb_done[c] = act_(xo, xo, ACT.Silu, tv)

        def sink_xbc(i, m, b, tp):
            n = i // 2 % 3
            pd = PADS[:, n * 518:(n + 1) * 518]
            ta = cp(pd.rearrange("p (a w) -> p a w", a=2)[:, :, 3:259], b.ap.rearrange("p (a w) -> p a w", a=2), tp,
                    pfree[n])
            live.append(conv4(i, pd, ta))
            return [ta]

        fm_tiles(12, tA, sink_xbc)
        fm_tiles(8, tA, lambda i, m, b, tp: [act_(Z[:, i * 256:i * 256 + 512], b.ap, ACT.Silu, tp)])
        t_z = an()

        ssd_ready = {}

        def ssd_prep(tv):
            while len(xb_done) < 12:
                yield
            t_xb = [xb_done[i] for i in range(12)]
            act_(DA, DT, ACT.Abs, tv)
            act_(DA, DA, ACT.Exp, scale=-1.0)
            act_(DA, DA, ACT.Ln, bias=1.0)
            AC = small[0:16, 60:61]
            ta = act_(AC, col("alog", 0, 16), ACT.Exp, vn())
            yield
            stt(DT, DT, 0.0, DA, ALU.max, ALU.add, ta)
            ts(AC, AC, -1.0, None, ALU.mult, None)
            ts(DA, DT, AC, None, ALU.mult, None)
            for t in range(2):
                r = slice(t * 128, t * 128 + 128)
                V.op(lambda e, r=r: e.tensor_tensor_scan(CS[:, r], ones[0:16, 0:128], DA[:, r], 0.0, ALU.mult,
                                                         ALU.add), t_const)
            V.op(lambda e: e.tensor_copy(R[:, 0:128], CS[:, 0:128]))
            V.op(lambda e: e.tensor_copy(R[:, 256:384], CS[:, 128:256]))
            t_R = ts(R[:, 128:256], CS[:, 128:256], CS[:, 127:128], None, ALU.add, None)
            yield
            b = bank()
            for a, src in enumerate((DT, CS)):
                for t in range(2):
                    tp = tr(b.ap[:, a * 32 + t * 16:a * 32 + t * 16 + 16], src[:, t * 128:(t + 1) * 128], t_R, b.free,
                            inc=(a == 1 and t == 1), n=16)
            t_tk = V.op(lambda e, b=b: e.tensor_copy(TK, b.ap[:, 0:64]), tp)
            give(b, t_tk)
            for g in range(2):
                b = bank()
                bmT, cmT = XB[:, 8 + g, :], XB[:, 10 + g, :]
                mm(b.ap[:, 0:256], bmT[:, 0:128], cmT[:, 0:256], True, True, t_xb, b.free)
                tp = mm(b.ap[:, 256:384], bmT[:, 128:256], cmT[:, 128:256], True, True, inc=True)
                give(b, tt(CB[:, g, :], b.ap[:, 0:384], SI, ALU.mult, tp, t_masks2))
            yield
            for t in range(2):
                for c2 in range(2):
                    b = bank()
                    for i in range(4):
                        tp = tr(b.ap[:, i * 128:(i + 1) * 128], XB[:, c2 * 4 + i, t * 128:(t + 1) * 128], t_xb, b.free,
                                inc=(i == 3))
                    t_xf = tt(XF[:, t, c2 * 512:(c2 + 1) * 512].rearrange("p (h c) -> p h c", c=64),
                              b.ap.rearrange("p (h c) -> p h c", c=64),
                              bc(TK[:, t * 16 + c2 * 8:t * 16 + c2 * 8 + 8], 64), ALU.mult, tp)
                    give(b, t_xf)
                    yield
            mine, pr = [], 0
            while pr < 8 or mine:
                for g in list(mine):
                    try:
                        next(g)
                    except StopIteration:
                        mine.remove(g)
                if pr < 8 and len(mine) < 2:
                    mine.append(ssd_pair(pr, t_R, t_xf))
                    pr += 1
                yield
            for g in range(2):
                yield from gnorm(g)

        sc_free = [None] * 4
        t_y = {}

        def ssd_pair(pr, t_R, t_xf):
            js = (2 * (pr % 2), 2 * (pr % 2) + 1)
            for j in range(2):
                hd, sc = 2 * pr + j, SC[js[j]]
                b = bank()
                tp = mm(b.ap[:, 0:384], selh[:, hd, :], R, True, True, t_sel, t_R, b.free, inc=True)
                ts(sc[:, 0:256], b.ap[:, 0:256], TK[:, 32 + hd:33 + hd], 0.0, ALU.subtract, ALU.min, tp,
                   sc_free[js[j]])
                tv = ts(sc[:, 256:384], b.ap[:, 256:384], TK[:, 48 + hd:49 + hd], 0.0, ALU.subtract, ALU.min)
                give(b, tv)
                ta = act_(sc, sc, ACT.Exp, tv)
            yield
            for j in range(2):
                tv = tt(SC[js[j]], SC[js[j]], CB[:, (2 * pr + j) // 8, :], ALU.mult, ta)
            yield
            b = bank()
            for j in range(2):
                hd, sc = 2 * pr + j, SC[js[j]]
                yo = b.ap[j * 64:j * 64 + 64, :]
                mm(yo[:, 0:256], XF[:, 0, hd * 64:hd * 64 + 64], sc[:, 0:256], True, False, tv, t_xf, b.free)
                tp = mm(yo[:, 128:256], XF[:, 1, hd * 64:hd * 64 + 64], sc[:, 256:384], False, True, inc=True)
                sc_free[js[j]] = tp
            tv = stt(Y[:, pr, :], XB[:, pr, :], col("dsk", pr), b.ap[:, 0:256], ALU.mult, ALU.add, tp)
            give(b, tv)
            t_y[pr] = tt(Y[:, pr, :], Y[:, pr, :], Z[:, pr * 256:pr * 256 + 256], ALU.mult, t_z)

        def gnorm(g):
            ys = [Y[:, g * 4 + i, :] for i in range(4)]
            rs = Rs(256)
            yield from rs_bcast(rs, ys, 512, [XB[:, 4 * g + i, :] for i in range(4)],
                                t_y[7], tn())
            for i in range(4):
                tv = stt(ys[i], ys[i], col("sso", g * 4 + i), rs.bank.ap[:, 0:256], ALU.mult, ALU.mult, rs.tok)
            give(rs.bank, tv)
            for i in range(4):
                OUT2[8 + 4 * g + i] = ys[i], tv

        OUT2 = {}

        def sink_dt(i, m, b, tp):
            tv = ts(DT, b.ap[0:16, 0:256], col("dtb", 0, 16), None, ALU.add, None, tp)
            live.append(ssd_prep(tv))
            return [tv]

        fm_tiles(1, tA, sink_dt)

        sb_free = [None] * NB
        sb_out = {}

        def sb_head(hd, tin):
            n = hd % NB
            qk, sq, sp, lm = QKf[:, hd * 512:hd * 512 + 512], SQb[n], SPb[n], LMb[n]
            lt = sq[:, 0:384]
            rs = Rs(512)
            yield from rs_bcast(rs, [qk], 128, [sq], tin, sb_free[n])
            for j in range(2):
                r = slice(j * 256, j * 256 + 256)
                tv = stt(qk[:, r], qk[:, r], small[:, 28 + j:29 + j], rs.bank.ap[:, r], ALU.mult, ALU.mult, rs.tok,
                         t_gain)
            give(rs.bank, tv)
            yield
            q, k = qk[:, 0:256], qk[:, 256:512]
            b = bank()
            mm(b.ap[:, 0:256], k[:, 0:128], q[:, 0:256], True, True, tv, b.free)
            tp = mm(b.ap[:, 256:384], k[:, 128:256], q[:, 128:256], True, True, inc=True)
            l = b.ap[:, 0:384]
            tv = tt(lm, l, NM, ALU.add, tp, t_masks2)
            act_(lt, l, ACT.Abs, tp, tv)
            act_(lt, lt, ACT.Exp, scale=-1.0)
            ta = act_(lt, lt, ACT.Ln, bias=1.0)
            yield
            tv = stt(sp, l, 0.0, lt, ALU.max, ALU.add, ta)
            give(b, tv)
            tv = tt(sp, sp, SM, ALU.mult)
            yield
            b = bank()
            mm(b.ap[:, 0:256], tri[:, :], sp[:, 0:256], True, False, tv, b.free)
            mm(b.ap[:, 128:256], ones[:, 0:128], sp[:, 256:384], False, True)
            tp = mm(b.ap[:, 256:384], tri[:, :], sp[:, 256:384], True, True, inc=True)
            tv = tt(lm, lm, b.ap[:, 0:384], ALU.subtract, tp)
            give(b, tv)
            ta = act_(lm, lm, ACT.Exp, tv)
            yield
            b = bank()
            tp = av_T(b.ap, V2[:, 0, hd * 128:(hd + 1) * 128], V2[:, 1, hd * 128:(hd + 1) * 128], lm, ta, t_v2, b.free)
            ta = cp(q, b.ap[:, 0:256], tp)
            give(b, ta)
            sb_free[n] = [tp, ta]
            sb_out[hd] = ta

        qk_toks = []

        def sink_sb(i, m, b, tp):
            ta = cp(QKf[:, i * 256:i * 256 + 512], b.ap, tp)
            qk_toks.append(ta)
            return [ta]

        def run_sb():
            hd, mine = 0, []
            while hd < 8 or mine:
                for g in list(mine):
                    try:
                        next(g)
                    except StopIteration:
                        mine.remove(g)
                if hd < 8 and len(mine) < NB and hd < len(qk_toks) and (hd < NB or hd - NB in sb_out):
                    mine.append(sb_head(hd, qk_toks[hd]))
                    hd += 1
                yield
            os = [QKf[:, i * 512:i * 512 + 256] for i in range(8)]
            while 15 not in OUT2:
                yield
            rs = Rs(256)
            yield from rs_bcast(rs, os, 1024, [XB[:, i, :] for i in range(8)], sb_out[7], vn(), tn())
            for i in range(8):
                tv = stt(os[i], os[i], col("sbo", i), rs.bank.ap[:, 0:256], ALU.mult, ALU.mult, rs.tok)
                OUT2[i] = os[i], tv
            give(rs.bank, tv)

        live.append(run_sb())
        fm_tiles(16, tA, sink_sb)
        t_proj = tn()
        MX.clear()
        t_sq = []
        rows(YFIRST, act_lhs, mixed(OUT2, YFIRST), add_h(t_sq))
        drain()

        arena("ar5", 26240)
        ash, asl = sb("ash", 1024, FR, phase[0]), sb("asl", 1024, FR, phase[0])
        NI = 64
        AGf = carve(NI * 256)
        AG = AGf.rearrange("p (i t) -> p i t", t=256)
        xn = AGf[:, 0:4096]
        QT = AGf[:, 12288:16384].rearrange("p (i t) -> p i t", t=256)
        SK = AGf[:, 10240:12288]
        SCS = [carve(2048), carve(2048)]
        CA = carve(2048)
        WK = carve(256)
        TS_, TI = carve(256), carve(256)
        TIU = carve(256).bitcast(U32)
        BS = carve(128)
        BP = carve(128).bitcast(U32)
        BA, BB = carve(128), carve(128)
        PK = carve(384)
        picks = carve(768)
        OH = CA
        GE = [carve(512), carve(512)]
        pk3 = picks.rearrange("p (c t) -> p c t", c=3)
        tA = norm_T("ffn_norm_2", xn, t_sq[-1])
        s_sk = sem("s_sk")
        t_sk = A.dma(SK, sk, s_sk, 1, t_sq[-1])
        fm_tiles(16, tA, lambda i, m, b, tp: [cp(QT[:, i:i + 2, :], b.ap.rearrange("p (a t) -> p a t", a=2), tp)])
        t_q = an()
        t_sc = []
        for t in range(2):
            for c in range(4):
                b = bank()
                for i4 in range(4):
                    i = c * 4 + i4
                    tp = mm(b.ap[:, i4 * 128:i4 * 128 + 128], QT[:, i, t * 128:(t + 1) * 128],
                            SK[:, i * 128:(i + 1) * 128], True, True, t_q, t_sk, b.free, inc=(i4 == 3))
                t_sc.append(cp(SCS[t][:, c * 512:(c + 1) * 512], b.ap, tp))
                give(b, t_sc[-1])
        t_qt = tn()

        def top16(vals, best, pos, *after):
            w = WK[:, 0:vals.shape[1]]
            V.op(lambda e: e.max(best[:, 0:8], vals), *after)
            V.op(lambda e: e.max_index(pos[:, 0:8], best[:, 0:8], vals))
            V.op(lambda e: e.match_replace(w, best[:, 0:8], vals, -3.0e38))
            V.op(lambda e: e.max(best[:, 8:16], w))
            V.op(lambda e: e.max_index(pos[:, 8:16], best[:, 8:16], w))

        def topk(pace):
            ts3 = TS_.rearrange("p (i k) -> p i k", k=16)
            tu3 = TIU.rearrange("p (i k) -> p i k", k=16)
            ti3 = TI.rearrange("p (h c k) -> p h c k", c=2, k=16)
            bs3 = BS.rearrange("p (h k) -> p h k", k=16)
            gg = PK[:, 256:384]
            g3 = gg.rearrange("p (h k) -> p h k", k=16)
            pkd = None
            for t in range(2):
                sc3 = SCS[t].rearrange("p (i k) -> p i k", k=128)
                for i in range(16):
                    top16(sc3[:, i, :], ts3[:, i, :], tu3[:, i, :], t_sc[-1])
                    if i % pace == pace - 1:
                        yield
                V.op(lambda e: e.tensor_copy(TI, TIU))
                for hd in range(8):
                    ca = CA[:, hd * 256:(hd + 1) * 256].rearrange("p (a b) -> p a b", b=16)
                    tt(ca, bc(ts3[:, 2 * hd, :], 16), bm(ts3[:, 2 * hd + 1, :], 16), ALU.add)
                    if hd % 4 == 3:
                        yield
                for hd in range(8):
                    k = slice(hd * 16, hd * 16 + 16)
                    top16(CA[:, hd * 256:(hd + 1) * 256], BS[:, k], BP[:, k])
                    if hd % 2 == 1:
                        yield
                tv = tt(g3, bs3, bs3[:, :, 0:1].to_broadcast([128, 8, 16]), ALU.subtract, pkd)
                ta = act_(gg, gg, ACT.Exp, tv)
                bau, bbu = BA.bitcast(U32), BB.bitcast(U32)
                V.op(lambda e: e.tensor_scalar(bau, BP, 4, None, ALU.logical_shift_right))
                V.op(lambda e: e.tensor_scalar(bbu, BP, 15, None, ALU.bitwise_and))
                V.op(lambda e: e.tensor_copy(BA, bau))
                V.op(lambda e: e.tensor_copy(BB, bbu))
                yield
                V.op(lambda e: e.tensor_reduce(small[:, 32:40], g3, AX.X, ALU.add), ta)
                recip(small[:, 48:56], small[:, 32:40])
                tt(g3, g3, bc(small[:, 48:56], 16), ALU.mult)
                TMP = SCS[t]
                for c, pos in ((0, BA), (1, BB)):
                    o3 = TMP.rearrange("p (n a) -> p n a", a=16)
                    tt(o3, bc(pos, 16), bm(iot[:, 0:16], 128), ALU.is_equal)
                    yield
                    for hd in range(8):
                        o = TMP[:, hd * 256:(hd + 1) * 256].rearrange("p (k a) -> p k a", a=16)
                        tt(o, o, bm(ti3[:, hd, c, :], 16), ALU.mult)
                    yield
                    tv = V.op(lambda e, c=c, o3=o3: e.tensor_reduce(PK[:, c * 128:(c + 1) * 128], o3, AX.X, ALU.add))
                    yield
                b = bank()
                for c in range(3):
                    tp = tr(b.ap[:, c * 128:(c + 1) * 128], PK[:, c * 128:(c + 1) * 128], tv, b.free, inc=(c == 2))
                pkd = tp
                tpk[t] = V.op(lambda e, b=b, t=t: e.tensor_copy(
                    pk3[:, :, t * 128:(t + 1) * 128], b.ap[:, 0:384].rearrange("p (c t) -> p c t", c=3)), tp)
                give(b, tpk[t])

        tpk = {}
        oh_free = [None, None]
        tcur, ndone = [0], [0]
        t_ag = []

        def gates(half, pace):
            def onehots(q):
                o = OH[:, (q % 2) * 768:(q % 2) * 768 + 768]
                oj = o[:, 0:512].rearrange("p (t j) -> p t j", t=4)
                t = 4 * q
                for j in range(4):
                    tg = ts(oj[:, j, :], iot[:, :], picks[:, 256 + t + j:257 + t + j], None, ALU.is_equal, None,
                            tpk[t // 128], tpk[1], oh_free[q % 2], E=P)
                    tv = ts(o[:, 512 + j * 64:576 + j * 64], iot[:, half * 64:half * 64 + 64],
                            picks[:, t + j:t + j + 1], picks[:, 512 + t + j:513 + t + j], ALU.is_equal, ALU.mult,
                            tpk[t // 128], oh_free[q % 2])
                return o, [tg, tv]

            nxt = onehots(0)
            for q in range(64):
                o, tok = nxt
                if q < 63:
                    nxt = onehots(q + 1)
                b = bank()
                for j in range(4):
                    tp = mm(b.ap[:, j * 64:(j + 1) * 64], o[:, j * 128:(j + 1) * 128], o[:, 512 + j * 64:576 + j * 64],
                            True, True, tok, b.free, inc=(j == 3))
                oh_free[q % 2] = tp
                pv = b.ap[:, 0:256].rearrange("p (t i) -> p i t", t=4)
                r, nd = slice(4 * q, 4 * q + 4), ndone[0]
                toks = []
                if nd:
                    toks.append(tt(AG[:, 0:nd, r], AG[:, 0:nd, r], pv[:, 0:nd, :], ALU.mult, tp, an()))
                if nd < NI:
                    toks.append(cp(AG[:, nd:NI, r], pv[:, nd:NI, :], tp, ag_free[0], vn()))
                give(b, *toks)
                t_ag[:] = toks
                tcur[0] = 4 * q + 4
                if q % pace == pace - 1:
                    yield

        ag_free = [None]

        def sink_dn(i, m, b, tp):
            tc = tcur[0]
            bv = b.ap.rearrange("p (a t) -> p a t", a=2)
            toks = []
            if tc:
                ge = GE[i // 2 % 2].rearrange("p (a t) -> p a t", a=2)
                ta = act_(ge[:, :, 0:tc], bv[:, :, 0:tc], ACT.Gelu, tp, vn())
                toks += [ta, tt(AG[:, i:i + 2, 0:tc], AG[:, i:i + 2, 0:tc], ge[:, :, 0:tc], ALU.mult, ta, an())]
            if tc < 256:
                toks.append(act_(AG[:, i:i + 2, tc:256], bv[:, :, tc:256], ACT.Gelu, tp, ag_free[0], vn()))
            ndone[0] = i + 2
            return toks

        asp = [Slot((ash[:, i * 256:(i + 1) * 256], asl[:, i * 256:(i + 1) * 256])) for i in range(4)]
        s_out = sem("s_out")
        nout = [0]
        outs = out.rearrange("(t p) d -> p t d", p=128)

        def ev_mid(t, c, b, tp):
            r = slice(c * 512, c * 512 + 512)
            return [tt(h[:, t, r], h[:, t, r], b.ap, ALU.add, tp)]

        def ev_last(t, c, b, tp):
            tv = ev_mid(t, c, b, tp)
            nout[0] += 1
            r = slice(c * 512, c * 512 + 512)
            S.dma(outs[:, t, r], h[:, t, r], s_out, nout[0], tv[0])
            return tv

        ag_free[0] = t_qt
        for half in range(2):
            tcur[0] = ndone[0] = 0

            def job(half=half):
                if half == 0:
                    yield from topk(TOPK_PACE)
                yield from gates(half, G_PACE[half])

            live.append(job())
            fm_tiles(64, tA, sink_dn)
            drain()
            t_agd = [an(), vn()]
            made, cnt = [0], [0]

            def asplit(upto):
                while made[0] < min(upto, 2 * NI):
                    n = made[0]
                    made[0] += 1
                    s = asp[n % 4]
                    s.tok = split(s.ap[0], s.ap[1], AG[:, n % NI, :], t_agd, s.free)

            def need_a(k):
                asplit(cnt[0] + 3)
                return asp[cnt[0] % 4].tok

            def used_a(tp):
                asp[cnt[0] % 4].free = tp
                cnt[0] += 1

            def lhs_a(k, t):
                s = asp[cnt[0] % 4]
                return s.ap[0][:, t * 128:(t + 1) * 128], s.ap[1][:, t * 128:(t + 1) * 128]

            rows(range(NI), lhs_a, need_a, ev_mid if half == 0 else ev_last, after=used_a)
            ag_free[0] = [an(), vn()]
        assert used[0] == len(seq)

        block = ctx.enter_context(nc.Block())

        @block.sync
        def _(e):
            S.emit(e)
            e.wait_ge(s_out, 16 * nout[0])

        @block.gpsimd
        def _(e):
            P.emit(e)

        @block.scalar
        def _(e):
            A.emit(e)

        @block.vector
        def _(e):
            V.emit(e)

        @block.tensor
        def _(e):
            T.emit(e)
        phase[0].close()


def lay_out(d):
    g = {k: np.asarray(v) for k, v in d.items()}

    def c(a):
        return np.ascontiguousarray(a)

    def colz(v):
        v = v.reshape(-1)
        if v.size < 128:
            v = np.concatenate([v, np.zeros(128 - v.size, v.dtype)])
        return v.reshape(-1, 128).T

    def fm(w):
        k, n = w.shape
        return w.reshape(k // 128, 128, n // 128, 128).transpose(2, 1, 0, 3).reshape(n // 128, 128, k)

    def pairs(q, k):
        n = q.shape[1] // 128
        return np.stack([q.reshape(-1, n, 128), k.reshape(-1, n, 128)], 2).reshape(-1, 2 * n * 128)

    wi = g["w_in"][0]
    s = [0, 512, 1024, 1536, 2048, 2816, 3584, 4352, 4358, 5126, 5894, 6662]
    aq, af, ai, ag, bq, bk, bv, bf, cq, ck, cv = [wi[:, s[i]:s[i + 1]] for i in range(11)]
    w2 = g["w_in_2"][0]
    q2, k2, v2, z2, x2, d2 = [w2[:, a:b] for a, b in ((0, 1024), (1024, 2048), (2048, 3072), (3072, 4096),
                                                      (4096, 5632), (5632, 5648))]
    par = {"attn_norm": g["attn_norm"], "ffn_norm": g["ffn_norm"], "ple_norm": g["ple_norm"],
           "attn_norm_2": g["attn_norm_2"], "ffn_norm_2": g["ffn_norm_2"], "lb": g["lb_logits"],
           "hgrn": g["hgrn_onorm"], "foxq": g["fox_qnorm"], "foxk": g["fox_knorm"], "mobq": g["moba_qnorm"],
           "mobk": g["moba_knorm"], "cw0": g["conv_w"][0, 0], "cw1": g["conv_w"][0, 1], "cw2": g["conv_w"][0, 2],
           "cb": g["conv_b"], "sbq": g["sb_q_norm_2"], "sbk": g["sb_k_norm_2"],
           "c20": g["conv_w_2"][0, 0], "c21": g["conv_w_2"][0, 1], "c22": g["conv_w_2"][0, 2],
           "c23": g["conv_w_2"][0, 3], "cb2": g["conv_b_2"], "sbo": g["sb_out_norm_2"], "sso": g["ssd_out_norm_2"],
           "dsk": np.repeat(g["d_skip_2"].reshape(-1), 64), "bf": g["fox_bf"], "dtb": g["dt_bias_2"],
           "alog": g["a_log_2"]}
    gu = np.stack([fm(g["w_gate"][0]), fm(g["w_up"][0])], 1).reshape(88, 128, 2048)
    return {
        "x": c(g["x"][0]),
        "pT": c(g["p"][0, 0].reshape(256, 2, 128).transpose(2, 1, 0).reshape(128, 512)),
        "cols": c(np.concatenate([colz(par[k]) for k, _ in COLS], 1)),
        "w1fm": c(fm(np.concatenate([aq, ag, af, bf, np.zeros((2048, 122), bf.dtype), pairs(bq, bk), pairs(cq, ck)], 1))),
        "w1v": c(np.concatenate([ai, bv, cv], 1).reshape(16, 128, 2048)),
        "wo1": c(g["w_out"][0].reshape(16, 128, 2048)),
        "wgu": c(gu),
        "wdn": c(g["w_down"][0].reshape(44, 128, 2048)),
        "plg": c(g["w_ple_gate"][0].reshape(16, 128, 2048)),
        "plp": c(g["w_ple_proj"][0].reshape(2, 128, 2048)),
        "w2fm": c(fm(np.concatenate([x2, z2, d2, np.zeros((2048, 112), d2.dtype), pairs(q2, k2)], 1))),
        "w2v": c(v2.reshape(16, 128, 1024)),
        "wo2": c(g["w_out_2"][0].reshape(16, 128, 2048)),
        "wq": c(fm(g["peer_query_2"][0])),
        "sk": c(g["peer_sub_keys_2"][0].reshape(16, 128, 128).transpose(2, 0, 1).reshape(128, 2048)),
        "dn": c(g["peer_down_2"][0].reshape(128, 128, 16, 128).transpose(0, 3, 2, 1).reshape(128, 128, 2048)),
        "up": c(g["peer_up_2"][0].reshape(128, 128, 2048)),
    }


def kernel(**inputs):
    import concourse.bacc as bacc
    from concourse.bass_utils import run_bass_kernel_spmd

    arrays = lay_out(inputs)
    nc = bacc.Bacc("TRN2", target_bir_lowering=False, num_devices=1)
    args = [nc.dram_tensor(f"in_{k}", a.shape, mybir.dt.from_np(a.dtype), kind="ExternalInput").ap()
            for k, a in arrays.items()]
    o = nc.dram_tensor("out_0", (256, 2048), F32, kind="ExternalOutput").ap()
    build(nc, *args, o)
    r = run_bass_kernel_spmd(nc, [{f"in_{k}": a for k, a in arrays.items()}], core_ids=[0])
    return r.results[0]["out_0"].reshape(1, 256, 2048)
```

```python
import numpy as np
import concourse.bass as bass
from concourse import mybir
from contextlib import ExitStack

F32 = mybir.dt.float32
FR = mybir.dt.float32r
U32 = mybir.dt.uint32
I32 = mybir.dt.int32
ALU = mybir.AluOpType
ACT = mybir.ActivationFunctionType
AX = mybir.AxisListType

EPS = 1e-6
SCALE = 128.0 ** -0.5
NEG = -1e30
G_STEP = (1, 2)
SLOPES = [float(np.float32(2.0) ** np.float32(-8.0 * (i + 1) / 6.0)) for i in range(6)]

COLS = [("attn_norm", 16), ("ffn_norm", 16), ("ple_norm", 16), ("attn_norm_2", 16), ("ffn_norm_2", 16),
        ("lb", 4), ("hgrn", 1), ("foxq", 1), ("foxk", 1), ("mobq", 1), ("mobk", 1),
        ("cw0", 44), ("cw1", 44), ("cw2", 44), ("cb", 44), ("sbq", 1), ("sbk", 1),
        ("c20", 12), ("c21", 12), ("c22", 12), ("c23", 12), ("cb2", 12),
        ("sbo", 8), ("sso", 8), ("dsk", 8), ("bf", 1), ("dtb", 1), ("alog", 1)]
COFF = {}
_n = 0
for _k, _w in COLS:
    COFF[_k] = _n
    _n += _w
NCOL = _n


class Eng:

    def __init__(self, sem, chain):
        self.sem, self.n, self.q, self.chain = sem, 0, [], chain

    def op(self, fn, *after, inc=True, chain=None):
        waits = []
        stack = list(after)
        while stack:
            a = stack.pop(0)
            if isinstance(a, list):
                stack = a + stack
            elif a is not None:
                waits.append(a)
        if (self.chain if chain is None else chain) and self.n:
            waits.append((self.sem, self.n))
        if inc:
            self.n += 1
        self.q.append((waits, fn, (self.sem, 1) if inc else None))
        return (self.sem, self.n)

    def dma(self, out, in_, sem, count, *after):
        waits = []
        for a in after:
            waits += a if isinstance(a, list) else [a] if a is not None else []
        self.q.append((waits, lambda e: e.dma_start(out, in_), (sem, 16)))
        return (sem, 16 * count)

    def emit(self, eng):
        seen = {}
        for waits, fn, inc in self.q:
            for sem, v in waits:
                if seen.get(sem.name, 0) < v:
                    eng.wait_ge(sem, v)
                    seen[sem.name] = v
            ins = fn(eng)
            if inc is not None:
                ins.then_inc(*inc)


class Slot:
    def __init__(self, ap, sem=None):
        self.ap, self.sem, self.free, self.n = ap, sem, None, 0


def build(nc, x, pT, colsd, w1fm, w1v, wo1, wgu, wdn, plg, plp, w2fm, w2v, wo2, wq, sk, dn, up, out):
    ctx = ExitStack()
    with ctx:
        names = [0]

        def sb(name, n, dt=F32, at=None):
            return (at or ctx).enter_context(nc.sbuf_tensor(name, [128, n], dt))

        def sem(name):
            return ctx.enter_context(nc.semaphore(name))

        V = Eng(sem("s_v"), True)
        A = Eng(sem("s_a"), True)
        P = Eng(sem("s_p"), True)
        T = Eng(sem("s_t"), False)
        S = Eng(sem("s_s"), False)

        def vn():
            return (V.sem, V.n)

        def an():
            return (A.sem, A.n)

        def tn():
            return (T.sem, T.n)

        hsb = sb("hsb", 4096)
        h = hsb[:, :].rearrange("p (t d) -> p t d", t=2)
        AHt, ALt = sb("ah", 4096, FR), sb("al", 4096, FR)
        AH = AHt[:, :].rearrange("p (k t) -> p k t", k=16)
        AL = ALt[:, :].rearrange("p (k t) -> p k t", k=16)
        cols = sb("cols", NCOL)
        ident = sb("ident", 128)
        ones = sb("ones", 256)
        tri = sb("tri", 128)
        small = sb("small", 256)
        iot = sb("iot", 128)
        NRAW, NS, LA = 3, 5, 3
        rawt = sb("raw", NRAW * 1024)
        hit, lot = sb("whi", NS * 1024, FR), sb("wlo", NS * 1024, FR)
        raw = [Slot(rawt[:, i * 1024:(i + 1) * 1024], sem(f"s_w{i}")) for i in range(NRAW)]
        spl = [Slot((hit[:, i * 1024:(i + 1) * 1024], lot[:, i * 1024:(i + 1) * 1024])) for i in range(NS)]
        free_banks = [Slot(ctx.enter_context(nc.psum_tensor(f"b{i}", [128, 512], F32))[:, :]) for i in range(8)]

        def bank():
            return free_banks.pop(0)

        def give(b, *tok):
            b.free = list(tok)
            free_banks.append(b)

        def col(name, i=0, p=128):
            return cols[0:p, COFF[name] + i:COFF[name] + i + 1]

        phase = [None, None, 0]

        def arena(name, n):
            if phase[0] is not None:
                phase[0].close()
            phase[0] = ExitStack()
            phase[1] = sb(name, n, at=phase[0])
            phase[2] = 0
            return phase[1]

        def carve(n, where=None):
            if where is not None:
                phase[2] = where
            a = phase[1][:, phase[2]:phase[2] + n]
            phase[2] += n
            return a

        def mm(o, l, r, start, stop, *after, inc=False):
            return T.op(lambda e: e.matmul(o, l, r, start=start, stop=stop), *after, inc=inc)

        def mm3(o, l, r, start, stop, *after, inc=False):
            mm(o, l[0], r[0], start, False, *after)
            mm(o, l[0], r[1], False, False)
            return mm(o, l[1], r[0], False, stop, inc=inc)

        def tr(o, i, *after, inc=False, n=128):
            return T.op(lambda e: e.transpose(o, i, ident[0:n, 0:n]), *after, inc=inc)

        def act_(o, i, f, *after, bias=0.0, scale=1.0, acc=None, chain=None):
            if acc is None:
                return A.op(lambda e: e.activation(o, i, f, bias=bias, scale=scale), *after, chain=chain)
            return A.op(lambda e: e.activation(o, i, f, bias=bias, scale=scale, accum_out=acc), *after, chain=chain)

        def cp(o, i, *after, chain=None):
            return A.op(lambda e: e.activation(o, i, ACT.Copy), *after, chain=chain)

        def tt(o, a, b, op, *after, chain=None):
            return V.op(lambda e: e.tensor_tensor(o, a, b, op), *after, chain=chain)

        def ts(o, a, s1, s2, op0, op1, *after, chain=None):
            if op1 is None:
                return V.op(lambda e: e.tensor_scalar(o, a, s1, None, op0), *after, chain=chain)
            return V.op(lambda e: e.tensor_scalar(o, a, s1, s2, op0, op1), *after, chain=chain)

        def stt(o, a, s, b, op0, op1, *after, chain=None):
            return V.op(lambda e: e.scalar_tensor_tensor(out=o, in0=a, scalar=s, in1=b, op0=op0, op1=op1), *after,
                        chain=chain)

        def recip(o, i, *after):
            return V.op(lambda e: e.reciprocal(o, i), *after)

        def memset(E, o, v, *after):
            return E.op(lambda e: e.memset(o, v), *after)

        def asel(o, i, pattern, op, fill, base, cm, *after):
            return P.op(lambda e: e.affine_select(out=o, in_=i, pattern=pattern, compare_op=op, fill=fill,
                                                  base=base, channel_multiplier=cm), *after)

        def bc(ap, n):
            return ap.unsqueeze(2).to_broadcast([ap.shape[0], ap.shape[1], n])

        def bm(ap, n):
            return ap.unsqueeze(1).to_broadcast([ap.shape[0], n, ap.shape[1]])

        def split(hi, lo, src, *after, by=V):
            ta = A.op(lambda e: e.activation(hi, src, ACT.Copy), *after, chain=False)
            return [ta, by.op(lambda e: e.tensor_tensor(lo, src, hi.bitcast(F32), ALU.subtract), *after, ta,
                              chain=False)]

        def halves(src, n0, n1):
            return [src[i, :, j * 1024:(j + 1) * 1024] for i in range(n0, n1) for j in range(2)]

        def colhalves(src, n):
            return [src[k, :, c * 1024:(c + 1) * 1024] for c in range(2) for k in range(n)]

        seq = (colhalves(w1v, 16) + halves(w1fm, 0, 37) + [wo1[k, :, c * 1024:(c + 1) * 1024] for n in (0, 8) for c in range(2) for k in range(n, n + 8)] + halves(wgu, 0, 88)
               + colhalves(wdn, 44) + colhalves(plp, 2) + colhalves(plg, 16)
               + [w2v[k, :, :] for k in range(16)] + halves(w2fm, 0, 25) + halves(w2fm, 29, 37) + halves(w2fm, 25, 29)
               + [wo2[k, :, c * 1024:(c + 1) * 1024] for n in (8, 0) for c in range(2) for k in range(n, n + 8)] + halves(wq, 0, 16)
               + halves(dn, 0, 64) + [up[k, :, c * 1024:(c + 1) * 1024] for c in range(2) for k in range(64)]
               + halves(dn, 64, 128) + [up[k, :, c * 1024:(c + 1) * 1024] for c in range(2) for k in range(64, 128)])
        pumped, used = [0], [0]
        helped = [False]

        def pump(upto):
            while pumped[0] < min(upto + 1, len(seq)):
                n = pumped[0]
                pumped[0] += 1
                r, s = raw[n % NRAW], spl[n % NS]
                r.n += 1
                tl = S.dma(r.ap, seq[n], r.sem, r.n, r.free)
                s.tok = split(s.ap[0], s.ap[1], r.ap, tl, s.free, by=P if helped[0] and n % 2 else V)
                r.free = s.tok

        def unit():
            n = used[0]
            used[0] += 1
            pump(n + LA)
            return spl[n % NS]

        live = []
        fine = [False]

        def tick(n=1):
            for _ in range(n):
                for g in list(live):
                    try:
                        next(g)
                    except StopIteration:
                        live.remove(g)

        def drain():
            while live:
                tick()

        s_x = [sem("s_x0"), sem("s_x1")]
        t_x = [S.dma(h[:, t, :], x[t * 128:(t + 1) * 128, :], s_x[t], 1) for t in range(2)]
        s_c = sem("s_c")
        t_cols = A.dma(cols[:, :], colsd, s_c, 1)
        memset(P, ident[:, :], 0.0)
        t_id = asel(ident[:, :], ident[:, :], [[-1, 128]], ALU.not_equal, 1.0, 0, 1)
        memset(P, ones[:, :], 1.0)
        memset(P, tri[:, :], 1.0)
        asel(tri[:, :], tri[:, :], [[-1, 128]], ALU.is_ge, 0.0, 0, 1)
        t_const = P.op(lambda e: e.iota(iot[:, :], pattern=[[1, 128]], base=0, channel_multiplier=0,
                                        allow_small_or_imprecise_dtypes=True))

        def expln():
            A.q.append(([], lambda e: e.preload_act_table_set("natural_log_exp_and_others"), None))

        def rsqrt(v, r, w, *after):
            act_(r, v, ACT.Ln, *after)
            return newton(v, r, w, act_(r, r, ACT.Exp, scale=-0.5))

        def newton(v, r, w, ta):
            tt(w, r, r, ALU.mult, ta)
            tt(w, w, v, ALU.mult)
            ts(w, w, -0.5, 1.5, ALU.mult, ALU.add)
            return tt(r, r, w, ALU.mult)

        def squares(t, c, junk, *after):
            return act_(junk, h[:, t, c * 512:(c + 1) * 512], ACT.Square, *after, acc=small[:, t * 4 + c:t * 4 + c + 1])

        def norm_T(gain, xnt, t_sq, table=False):
            xn = xnt.rearrange("p (c t d) -> p c t d", c=3, t=2)
            if not table:
                expln()
            V.op(lambda e: e.tensor_reduce(small[:, 8:10], small[:, 0:8].rearrange("p (t c) -> p t c", t=2),
                                           AX.X, ALU.add), t_sq)
            tv = ts(small[:, 10:12], small[:, 8:10], 1.0 / 2048, EPS, ALU.mult, ALU.add)
            ts_ = rsqrt(small[:, 10:12], small[:, 12:14], small[:, 14:16], tv)
            toks, tps = [], []

            def scaled(c):
                r = slice(c * 512, c * 512 + 512)
                x_, w = xn[:, c % 3], tps[2 * (c - 3) + 1] if c >= 3 else None
                return [ts(x_[:, 0, :], h[:, 0, r], small[:, 12:13], None, ALU.mult, None, ts_, w, chain=False),
                        act_(x_[:, 1, :], h[:, 1, r], ACT.Copy, ts_, w, scale=small[:, 13:14], chain=False)]

            txs = [scaled(0), scaled(1)]
            for c in range(4):
                x_, tx = xn[:, c % 3], txs[c]
                if c == 1:
                    txs += [scaled(2)]
                if c == 2:
                    txs += [scaled(3)]
                for g in (2 * c, 2 * c + 1):
                    b = bank()
                    for k in (2 * g, 2 * g + 1):
                        for t in range(2):
                            o = (k % 2) * 256 + t * 128
                            tp = tr(b.ap[:, o:o + 128], x_[:, t, (k % 4) * 128:(k % 4 + 1) * 128], tx,
                                    b.free, t_id, inc=(k % 2 == 1 and t == 1))
                    tps.append(tp)
                    for k in (2 * g, 2 * g + 1):
                        ta = act_(AH[:, k, :], b.ap[:, (k % 2) * 256:(k % 2) * 256 + 256], ACT.Copy, tp, t_cols,
                                  scale=col(gain, k), chain=False)
                    for k in (2 * g, 2 * g + 1):
                        tv = stt(AL[:, k, :], b.ap[:, (k % 2) * 256:(k % 2) * 256 + 256], col(gain, k),
                                 AH[:, k, :].bitcast(F32), ALU.mult, ALU.subtract, ta, chain=False)
                        toks.append([ta, tv])
                    give(b, tv, ta)
            return toks

        def fm_tiles(n, t_act, sink):
            for i in range(0, n, 2):
                b = bank()
                m = min(2, n - i)
                for j in range(m):
                    for kh in range(2):
                        s = unit()
                        for kk in range(8):
                            k = kh * 8 + kk
                            tp = mm3(b.ap[:, j * 256:j * 256 + 256],
                                     [a[:, kk * 128:(kk + 1) * 128] for a in s.ap], (AH[:, k, :], AL[:, k, :]),
                                     k == 0, k == 15, t_act[k], s.tok, b.free if k == 0 else None, inc=(kk == 7))
                            if fine[0] and kk == 3:
                                tick()
                        s.free = tp
                        if j < m - 1 or kh == 0:
                            tick()
                give(b, *sink(i, m, b, tp))
                tick()

        def rows(ks, lhs, need, ev, halves=2, after=None):
            for ch in range(halves):
                bs = {(t, c): bank() for t in range(2) for c in range(2)}
                tps = {}
                for n, k in enumerate(ks):
                    w = need(k)
                    s = unit()
                    for t in range(2):
                        for c in range(2):
                            b = bs[t, c]
                            last = n == len(ks) - 1
                            tp = mm3(b.ap, lhs(k, t), [a[:, c * 512:(c + 1) * 512] for a in s.ap], n == 0, last,
                                     s.tok, w, b.free if n == 0 else None, inc=last or (t == 1 and c == 1))
                            tps[t, c] = tp
                        if fine[0] and t == 0:
                            tick()
                    s.free = tp
                    if after is not None:
                        after(tp)
                    if True:
                        tick()
                for t in range(2):
                    for c in range(2):
                        give(bs[t, c], *ev(t, 2 * ch + c, bs[t, c], tps[t, c]))

        def add_h(t_sq):
            def ev(t, c, b, tp):
                r = slice(c * 512, c * 512 + 512)
                tv = tt(h[:, t, r], h[:, t, r], b.ap, ALU.add, tp, chain=False)
                if (t, c) == (0, 2):
                    expln()
                t_sq.append(squares(t, c, b.ap, tv))
                return [t_sq[-1]]
            return ev

        def act_lhs(k, t):
            return AH[:, k, t * 128:(t + 1) * 128], AL[:, k, t * 128:(t + 1) * 128]

        def rs_bcast(o, src_aps, n, sq, *after):
            w = o.shape[1]
            m = w // 128
            for i, a in enumerate(src_aps):
                ta = act_(sq[i], a, ACT.Square, *after, chain=False)
            yield
            b = bank()
            c = small[:, 64 + 16 * rsn[0]:64 + 16 * rsn[0] + 16]
            rsn[0] = (rsn[0] + 1) % 12
            for j in range(m):
                for i in range(len(src_aps)):
                    tq = mm(b.ap[:, j:j + 1], sq[i][:, j * 128:(j + 1) * 128], ones[:, 0:1], i == 0,
                            i == len(src_aps) - 1, ta, b.free, t_const, inc=(j == m - 1 and i == len(src_aps) - 1))
            yield
            tv = ts(c[:, 0:m], b.ap[:, 0:m], 1.0 / n, EPS, ALU.mult, ALU.add, tq)
            give(b, tv)
            yield
            act_(c[:, 4:4 + m], c[:, 0:m], ACT.Ln, tv)
            ta = act_(c[:, 4:4 + m], c[:, 4:4 + m], ACT.Exp, scale=-0.5)
            yield
            tv = newton(c[:, 0:m], c[:, 4:4 + m], c[:, 8:8 + m], ta)
            yield
            b = bank()
            for j in range(m):
                tq = mm(b.ap[:, j * 128:(j + 1) * 128], c[:, 4 + j:5 + j].to_broadcast([128, 128]), ident[:, :],
                        True, True, tv, b.free, t_id, inc=(j == m - 1))
            o.tok, o.bank = tq, b
            yield

        rsn = [0]

        class Rs:
            def __init__(self, w):
                self.shape = (128, w)

        def av_T(o, v0, v1, w, *after):
            mm(o[:, 0:256], v0, w[:, 0:256], True, False, *after)
            return mm(o[:, 128:256], v1, w[:, 256:384], False, True, inc=True)

        arena("ar1", 25856)
        V1 = carve(4096, 0).rearrange("p (t c) -> p t c", t=2)
        Qa, Ka, Ga, Gs = carve(1024), carve(1024), carve(1024), carve(1024)
        xn = phase[1][:, phase[2]:phase[2] + 3072]
        QKf = carve(6144)
        X = [carve(1024), carve(1024)]
        EX = carve(1024)
        AT = carve(1536)
        DL = carve(512)
        M = carve(128 * 8)
        DIST = carve(384)
        CM = carve(384)
        FB = carve(768)
        NB = 3
        SQb = [carve(512) for _ in range(NB)]
        LGb = [carve(384) for _ in range(NB)]
        WTb = [carve(384) for _ in range(NB)]
        HO = [X[0][:, 0:512], X[0][:, 512:1024]]

        t_sq = [squares(t, c, QKf[:, 4096:4608], t_x[t]) for t in range(2) for c in range(4)]
        tA = norm_T("attn_norm", xn, t_sq[-1])
        tv0 = []

        def ev_v1(t, c, b, tp):
            tv0.append(cp(V1[:, t, c * 512:(c + 1) * 512], b.ap, tp))
            return [tv0[-1]]

        rows(range(16), act_lhs, lambda k: tA[k], ev_v1)
        t_v1 = tv0[-1]

        memset(P, M, 0.0)
        for li in range(7):
            L = 1 << li
            m = M[:, li * 128:(li + 1) * 128].rearrange("p (b u l) -> p b u l", u=2, l=L)[:, :, 1, :]
            n = 64 // L
            memset(P, m, 1.0)
            asel(m, m, [[-2 * L, n], [0, L]], ALU.is_ge, 0.0, 0, 1)
            asel(m, m, [[2 * L, n], [0, L]], ALU.is_ge, 0.0, L - 1, -1)
        P.op(lambda e: e.tensor_copy(M[:, 896:1024], ident[:, :]))
        memset(P, CM, 0.0)
        for o in (0, 256):
            asel(CM[:, o:o + 128], CM[:, o:o + 128], [[-1, 128]], ALU.is_ge, NEG, 0, 1)
        for o, base in ((0, 0), (128, -128), (256, 0)):
            P.op(lambda e, o=o, base=base: e.iota(DIST[:, o:o + 128], pattern=[[1, 128]], base=base,
                                                  channel_multiplier=-1, allow_small_or_imprecise_dtypes=True))
        for o in (0, 256):
            t_masks = asel(DIST[:, o:o + 128], DIST[:, o:o + 128], [[-1, 128]], ALU.is_ge, -1e33, 0, 1)

        lbv, lb1 = small[:, 16:20], small[:, 20:24]
        tv = tt(lbv, cols[:, COFF["lb"]:COFF["lb"] + 4], cols[:, COFF["lb"]:COFF["lb"] + 4], ALU.subtract, t_cols)
        ta = act_(lbv, lbv, ACT.Exp, tv)
        recip(lb1, lbv, ta)
        tt(lb1, lbv, lb1, ALU.mult)
        tt(lbv, lb1, lb1, ALU.subtract)
        ts(lb1, lbv, -1.0, 1.0, ALU.mult, ALU.add)

        for i, (n, s) in enumerate((("foxq", SCALE), ("foxk", 1.0), ("mobq", SCALE), ("mobk", 1.0), ("sbq", SCALE),
                                    ("sbk", 1.0))):
            t_gain = ts(small[:, 24 + i:25 + i], col(n), s, None, ALU.mult, None, t_cols)

        def sink_hg(i, m, b, tp):
            if i < 4:
                return [act_(Qa[:, i * 256:i * 256 + 512], b.ap, ACT.Silu, tp)]
            if i < 8:
                j = (i - 4) * 256
                return [act_(Gs[:, j:j + 512], b.ap, ACT.Silu, tp)]
            j = (i - 8) * 256
            act_(Ga[:, j:j + 512], b.ap, ACT.Sigmoid, tp)
            return [act_(Ka[:, j:j + 512], b.ap, ACT.Sigmoid, tp, scale=-1.0)]

        fm_tiles(12, tA, sink_hg)

        at4 = AT.rearrange("p (h w) -> p h w", h=4)
        OUT, MX = {}, {}

        def hgrn_mm(lhs, rhs, li, tv):
            bs = []
            for t in range(2):
                b = bank()
                for hh in range(4):
                    o = hh * 256 + t * 128
                    tp = mm(b.ap[:, hh * 128:(hh + 1) * 128], lhs[:, o:o + 128], rhs[:, o:o + 128], True, True, tv,
                            b.free, inc=(hh == 3))
                bs.append((b, tp))
            yield
            for t in range(2):
                b, tp = bs[t]
                mk = M[:, li * 128:(li + 1) * 128].bitcast(I32)
                give(b, V.op(lambda e, t=t, b=b, mk=mk: e.copy_predicated(
                    at4[:, :, t * 256:t * 256 + 128], bm(mk, 4), b.ap.rearrange("p (h w) -> p h w", h=4)), tp, t_masks))
            return tp

        def hgrn(t_hg):
            for i in range(4):
                r = slice(i * 256, i * 256 + 256)
                ts(Ga[:, r], Ga[:, r], lb1[:, i:i + 1], lbv[:, i:i + 1], ALU.mult, ALU.add, t_hg, chain=(i == 0))
                ts(Ka[:, r], Ka[:, r], lb1[:, i:i + 1], None, ALU.mult, None, t_hg, chain=False)
            yield
            ts(EX, Ga, 1e-30, 1e18, ALU.max, ALU.mult)
            ts(EX, EX, 1.0, None, ALU.min, None)
            tv = ts(Ga, Ga, 1e-18, None, ALU.max, None)
            yield
            expln()
            act_(EX, EX, ACT.Ln, tv)
            ta = act_(Ga, Ga, ACT.Ln)
            yield
            memset(V, AT, 0.0)
            t_g = tt(Ga, Ga, EX, ALU.add, ta)
            yield
            yield
            yield from hgrn_mm(Ka, Qa, 7, t_g)
            xfree = [None, None]
            for li in range(8):
                L = 1 << li
                x_ = X[li % 2]
                pv = Ga.rearrange("p (b u l) -> p b u l", u=2, l=L)
                ev = EX.rearrange("p (b u l) -> p b u l", u=2, l=L)
                xv = x_.rearrange("p (b u l) -> p b u l", u=2, l=L)
                qv = Qa.rearrange("p (b u l) -> p b u l", u=2, l=L)
                kv = Ka.rearrange("p (b u l) -> p b u l", u=2, l=L)
                tot = pv[:, :, 0, L - 1:L].to_broadcast([128, 512 // L, L])
                tv = tt(DL.rearrange("p (b l) -> p b l", l=L), tot, pv[:, :, 0, :], ALU.subtract)
                yield
                act_(ev[:, :, 1, :], pv[:, :, 1, :], ACT.Exp, tv)
                ta = act_(ev[:, :, 0, :], DL.rearrange("p (b l) -> p b l", l=L), ACT.Exp)
                yield
                tt(xv[:, :, 1, :], qv[:, :, 1, :], ev[:, :, 1, :], ALU.mult, ta, xfree[li % 2])
                tv = tt(xv[:, :, 0, :], kv[:, :, 0, :], ev[:, :, 0, :], ALU.mult)
                if L < 128:
                    tt(pv[:, :, 1, :], pv[:, :, 1, :], tot, ALU.add)
                    yield
                    xfree[li % 2] = yield from hgrn_mm(x_, x_, li, tv)
            yield
            b = bank()
            for hh in range(4):
                tp = mm(b.ap[:, hh * 128:(hh + 1) * 128], x_[:, hh * 256:hh * 256 + 128],
                        x_[:, hh * 256 + 128:hh * 256 + 256], True, True, tv, b.free, inc=(hh == 3))
            yield
            t_at = cp(at4[:, :, 128:256], b.ap.rearrange("p (h w) -> p h w", h=4), tp, t_g)
            give(b, t_at)
            yield
            for hp in range(2):
                b = bank()
                for j in range(2):
                    hh = 2 * hp + j
                    tp = av_T(b.ap[:, j * 256:j * 256 + 256], V1[:, 0, hh * 128:(hh + 1) * 128],
                              V1[:, 1, hh * 128:(hh + 1) * 128], at4[:, hh, :], t_at, t_v1, b.free)
                yield
                ta = cp(HO[hp], b.ap, tp)
                give(b, ta)
            for hp in range(2):
                rs = Rs(512)
                yield from rs_bcast(rs, [HO[hp]], 128, [EX[:, hp * 512:hp * 512 + 512]], ta, tv)
                tv = stt(HO[hp], HO[hp], col("hgrn"), rs.bank.ap, ALU.mult, ALU.mult, rs.tok)
                give(rs.bank, tv)
                tv = tt(HO[hp], HO[hp], Gs[:, hp * 512:hp * 512 + 512], ALU.mult)
                for j in range(2):
                    OUT[2 * hp + j] = HO[hp][:, j * 256:(j + 1) * 256], tv

        fine[0] = False
        live.append(hgrn(an()))

        FX, FL, FN = [FB[0:6, i * 256:(i + 1) * 256] for i in range(3)]
        tf = {}

        def fgate(tv):
            yield
            act_(FL, FX, ACT.Abs, tv)
            act_(FL, FL, ACT.Exp, scale=-1.0)
            ta = act_(FL, FL, ACT.Ln, bias=1.0)
            yield
            stt(FX, FX, 0.0, FL, ALU.min, ALU.subtract, ta)
            V.op(lambda e: e.tensor_tensor_scan(FL, ones[0:6, 0:256], FX, 0.0, ALU.mult, ALU.add), t_const)
            tf[0] = ts(FN, FL, -1.0, None, ALU.mult, None)

        def sink_f(i, m, b, tp):
            tv = ts(FX, b.ap[0:6, 0:256], col("bf", 0, 6), None, ALU.add, None, tp)
            live.append(fgate(tv))
            return [tv]

        fm_tiles(1, tA, sink_f)

        buf_free = [None] * NB

        def head(hd, tin):
            fox = hd < 6
            n = hd % NB
            qk, sq, lg, wt = QKf[:, hd * 512:hd * 512 + 512], SQb[n], LGb[n], WTb[n]
            rs = Rs(512)
            yield from rs_bcast(rs, [qk], 128, [sq], tin, buf_free[n])
            for j in range(2):
                g = 24 + j + (0 if fox else 2)
                r = slice(j * 256, j * 256 + 256)
                tv = stt(qk[:, r], qk[:, r], small[:, g:g + 1], rs.bank.ap[:, r], ALU.mult, ALU.mult, rs.tok, t_gain,
                         chain=False)
            give(rs.bank, tv)
            yield
            b = bank()
            for qt, o, kl in ((0, 0, 128), (1, 128, 256)):
                tp = mm(b.ap[:, o:o + kl], qk[:, qt * 128:(qt + 1) * 128], qk[:, 256:256 + kl], True, not fox, tv,
                        b.free, inc=not fox)
                if fox:
                    one = ident[0:6, hd:hd + 1]
                    mm(b.ap[:, o:o + kl], FL[:, qt * 128:(qt + 1) * 128], one.to_broadcast([6, kl]), False, False, tf[0])
                    tp = mm(b.ap[:, o:o + kl], one.to_broadcast([6, 128]), FN[:, 0:kl], False, True, inc=True)
            yield
            if fox:
                tv = tt(lg, b.ap[:, 0:384], CM, ALU.add, tp, t_masks)
            else:
                tv = stt(lg, DIST, SLOPES[hd - 6], b.ap[:, 0:384], ALU.mult, ALU.add, tp, t_masks)
            give(b, tv)
            c = small[:, 40 + 8 * n:48 + 8 * n]
            V.op(lambda e: e.tensor_reduce(c[:, 0:1], lg[:, 0:128], AX.X, ALU.max, negate=True))
            tv = V.op(lambda e: e.tensor_reduce(c[:, 1:2], lg[:, 128:384], AX.X, ALU.max, negate=True))
            yield
            act_(lg[:, 0:128], lg[:, 0:128], ACT.Exp, tv, bias=c[:, 0:1], acc=c[:, 2:3])
            ta = act_(lg[:, 128:384], lg[:, 128:384], ACT.Exp, bias=c[:, 1:2], acc=c[:, 3:4])
            yield
            recip(c[:, 4:6], c[:, 2:4], ta)
            ts(lg[:, 0:128], lg[:, 0:128], c[:, 4:5], None, ALU.mult, None)
            tv = ts(lg[:, 128:384], lg[:, 128:384], c[:, 5:6], None, ALU.mult, None)
            yield
            b = bank()
            for i in range(3):
                tp = tr(b.ap[:, i * 128:(i + 1) * 128], lg[:, i * 128:(i + 1) * 128], tv, b.free, inc=(i == 2))
            yield
            ta = cp(wt, b.ap[:, 0:384], tp)
            give(b, ta)
            yield
            vo = 512 + hd * 128
            b = bank()
            tp = av_T(b.ap, V1[:, 0, vo:vo + 128], V1[:, 1, vo:vo + 128], wt, ta, t_v1, b.free)
            yield
            ta = cp(qk[:, 0:256], b.ap[:, 0:256], tp)
            give(b, ta)
            OUT[4 + hd] = qk[:, 0:256], ta
            buf_free[n] = tp

        qk_toks = []

        def sink_heads(i, m, b, tp):
            ta = cp(QKf[:, i * 256:i * 256 + 512], b.ap, tp)
            qk_toks.append(ta)
            return [ta]

        def run_heads():
            hd = 0
            mine = []
            while hd < 12 or mine:
                for g in list(mine):
                    try:
                        next(g)
                    except StopIteration:
                        mine.remove(g)
                if hd < 12 and len(mine) < NB and hd < len(qk_toks) and buf_ok(hd):
                    mine.append(head(hd, qk_toks[hd]))
                    hd += 1
                yield

        def buf_ok(hd):
            return hd < NB or (4 + hd - NB) in OUT

        live.append(run_heads())
        fm_tiles(24, tA, sink_heads)
        t_proj = tn()

        def mixed(srcs, ks, ahead=2):
            order = list(ks)

            def need(k):
                while k not in srcs:
                    tick()
                n = order.index(k)
                for q in order[n:n + 1 + ahead]:
                    if q in srcs and q not in MX:
                        a, tok = srcs[q]
                        MX[q] = split(AH[:, q, :], AL[:, q, :], a, tok, t_proj)
                return MX[k]
            return need

        def add_only(t, c, b, tp):
            r = slice(c * 512, c * 512 + 512)
            return [tt(h[:, t, r], h[:, t, r], b.ap, ALU.add, tp, chain=False)]

        t_sq = []
        rows(range(8), act_lhs, mixed(OUT, range(8)), add_only)
        rows(range(8, 16), act_lhs, mixed(OUT, range(8, 16)), add_h(t_sq))
        drain()

        fine[0] = False
        arena("ar2", 3080)
        hth, htl = sb("hth", 11264, FR, phase[0]), sb("htl", 11264, FR, phase[0])
        HH = hth[:, :].rearrange("p (k t) -> p k t", t=256)
        HL = htl[:, :].rearrange("p (k t) -> p k t", t=256)
        xn = carve(3072)
        PADS = carve(4 * 514, 0)
        CVS = carve(4 * 256)
        tA = norm_T("ffn_norm", xn, t_sq[-1], True)
        memset(V, PADS.rearrange("p (a w) -> p a w", w=514)[:, :, 0:2], 0.0, tA[15])
        ht = {}
        pfree = [vn()] * 4

        def ffn_tile(i, pd, cv, ta):
            ts(cv, pd[:, 0:256], col("cw0", i), col("cb", i), ALU.mult, ALU.add, ta)
            stt(cv, pd[:, 1:257], col("cw1", i), cv, ALU.mult, ALU.add)
            tv = stt(cv, pd[:, 2:258], col("cw2", i), cv, ALU.mult, ALU.add)
            yield
            ta = act_(cv, cv, ACT.Gelu_apprx_tanh, tv)
            yield
            pfree[i % 4] = tv = tt(cv, cv, pd[:, 258:514], ALU.mult, ta)
            ta = cp(HH[:, i, :], cv, tv)
            yield
            ht[i] = [ta, tt(HL[:, i, :], cv, HH[:, i, :].bitcast(F32), ALU.subtract, ta)]

        def sink_ffn(i2, m, b, tp):
            i = i2 // 2
            pd, cv = PADS[:, (i % 4) * 514:(i % 4) * 514 + 514], CVS[:, (i % 4) * 256:(i % 4) * 256 + 256]
            ta = cp(pd[:, 2:514], b.ap, tp, pfree[i % 4])
            live.append(ffn_tile(i, pd, cv, ta))
            return [ta]

        fm_tiles(88, tA, sink_ffn)

        def need_ht(k):
            while k not in ht:
                tick()
            return ht[k]

        t_sq = []
        rows(range(44), lambda k, t: (HH[:, k, t * 128:(t + 1) * 128], HL[:, k, t * 128:(t + 1) * 128]), need_ht,
             add_h(t_sq))

        arena("ar3", 3 * 4096 + 512)
        pth, ptl = sb("pth", 512, FR, phase[0]), sb("ptl", 512, FR, phase[0])
        xn = carve(3072)
        SG = carve(4096).rearrange("p (t d) -> p t d", t=2)
        PT = carve(512)
        PP = carve(4096).rearrange("p (t d) -> p t d", t=2)
        s_pt = sem("s_pt")
        t_pt = S.dma(PT, pT, s_pt, 1, tn())
        t_pt = split(pth[:, :], ptl[:, :], PT, t_pt)

        def ev_pp(t, c, b, tp):
            return [cp(PP[:, t, c * 512:(c + 1) * 512], b.ap, tp)]

        rows(range(2), lambda k, t: (pth[:, k * 256 + t * 128:k * 256 + t * 128 + 128],
                                     ptl[:, k * 256 + t * 128:k * 256 + t * 128 + 128]), lambda k: t_pt, ev_pp)
        t_pp = an()
        tA = norm_T("ple_norm", xn, t_sq[-1], True)

        t_sq, pend = [], []

        def ev_ple(t, c, b, tp):
            r = slice(c * 512, c * 512 + 512)
            ta = act_(SG[:, t, r], b.ap, ACT.Sigmoid, tp, t_pp, chain=False)
            tv = tt(SG[:, t, r], SG[:, t, r], PP[:, t, r], ALU.mult, ta, chain=False)
            if (t, c) == (1, 3):
                expln()
            pend.append((t, c, r, tt(h[:, t, r], h[:, t, r], SG[:, t, r], ALU.add, tv, chain=False)))
            if t == 1:
                for _ in range(2 if c % 2 == 0 else len(pend)):
                    t_, c_, r_, tv = pend.pop(0)
                    t_sq.append(squares(t_, c_, PP[:, t_, r_], tv))
            return [ta]

        rows(range(16), act_lhs, lambda k: tA[k], ev_ple)

        arena("ar4", 26194)
        V2 = carve(2048).rearrange("p (t c) -> p t c", t=2)
        xn = phase[1][:, phase[2]:phase[2] + 3072]
        QKf = carve(4096)
        Z = carve(2048)
        XB = carve(3072).rearrange("p (i t) -> p i t", t=256)
        Y = carve(2048).rearrange("p (i t) -> p i t", t=256)
        XF = carve(2048).rearrange("p (t c) -> p t c", t=2)
        PADS = carve(3 * 518)
        SM, NM, SI = carve(384), carve(384), carve(384)
        CB = carve(768).rearrange("p (g w) -> p g w", g=2)
        SC = [carve(384) for _ in range(6)]
        SQb = [carve(512) for _ in range(NB)]
        SPb = [carve(384) for _ in range(NB)]
        LMb = [carve(384) for _ in range(NB)]
        DT, DA, CS = [carve(256)[0:16, :] for _ in range(3)]
        R = carve(384)[0:16, :]
        TK = carve(64)
        tA = norm_T("attn_norm_2", xn, t_sq[-1], True)

        memset(P, SM, 1.0, t_sq[-1])
        memset(P, SI, 1.0)
        memset(P, NM, 0.0)
        for o in (0, 256):
            asel(SM[:, o:o + 128], SM[:, o:o + 128], [[1, 128]], ALU.is_gt, 0.0, 0, -1)
            asel(SI[:, o:o + 128], SI[:, o:o + 128], [[1, 128]], ALU.is_ge, 0.0, 0, -1)
            t_masks2 = asel(NM[:, o:o + 128], NM[:, o:o + 128], [[1, 128]], ALU.is_gt, NEG, 0, -1)
        memset(V, PADS.rearrange("p (a w) -> p a w", w=259)[:, :, 0:3], 0.0)
        t_pad = vn()
        tv2 = []

        def ev_v2(t, c, b, tp):
            tv2.append(cp(V2[:, t, c * 512:(c + 1) * 512], b.ap, tp))
            return [tv2[-1]]

        rows(range(16), act_lhs, lambda k: tA[k], ev_v2, halves=1)
        t_v2 = tv2[-1]

        pfree = [t_pad] * 3
        xb_done = {}

        def conv4(i, pd, ta):
            for j in range(2):
                c, p, xo = i + j, pd[:, j * 259:(j + 1) * 259], XB[:, i + j, :]
                ts(xo, p[:, 0:256], col("c20", c), col("cb2", c), ALU.mult, ALU.add, ta)
                stt(xo, p[:, 1:257], col("c21", c), xo, ALU.mult, ALU.add)
                stt(xo, p[:, 2:258], col("c22", c), xo, ALU.mult, ALU.add)
                tv = stt(xo, p[:, 3:259], col("c23", c), xo, ALU.mult, ALU.add)
                if j == 1:
                    pfree[i // 2 % 3] = tv
                yield
                xb_done[c] = act_(xo, xo, ACT.Silu, tv)

        def sink_xbc(i, m, b, tp):
            n = i // 2 % 3
            pd = PADS[:, n * 518:(n + 1) * 518]
            ta = cp(pd.rearrange("p (a w) -> p a w", a=2)[:, :, 3:259], b.ap.rearrange("p (a w) -> p a w", a=2), tp,
                    pfree[n])
            live.append(conv4(i, pd, ta))
            return [ta]

        fine[0] = False
        fm_tiles(12, tA, sink_xbc)
        t_z = {}

        def sink_z(i, m, b, tp):
            ta = cp(Z[:, i * 256:i * 256 + 512], b.ap, tp)
            if i == 6:
                t_z[0] = act_(Z, Z, ACT.Silu)
                expln()
            return [ta]

        ssd_ready = {}

        def ssd_prep(tv):
            while len(xb_done) < 12:
                yield
            t_xb = [xb_done[i] for i in range(12)]
            expln()
            act_(DA, DT, ACT.Abs, tv)
            act_(DA, DA, ACT.Exp, scale=-1.0)
            act_(DA, DA, ACT.Ln, bias=1.0)
            AC = small[0:16, 60:61]
            ta = act_(AC, col("alog", 0, 16), ACT.Exp, t_cols)
            yield
            stt(DT, DT, 0.0, DA, ALU.max, ALU.add, ta)
            ts(AC, AC, -1.0, None, ALU.mult, None)
            ts(DA, DT, AC, None, ALU.mult, None)
            for t in range(2):
                r = slice(t * 128, t * 128 + 128)
                V.op(lambda e, r=r: e.tensor_tensor_scan(CS[:, r], ones[0:16, 0:128], DA[:, r], 0.0, ALU.mult,
                                                         ALU.add), t_const)
            V.op(lambda e: e.tensor_copy(R[:, 0:128], CS[:, 0:128]))
            V.op(lambda e: e.tensor_copy(R[:, 256:384], CS[:, 128:256]))
            t_R = ts(R[:, 128:256], CS[:, 128:256], CS[:, 127:128], None, ALU.add, None)
            yield
            b = bank()
            for a, src in enumerate((DT, CS)):
                for t in range(2):
                    tp = tr(b.ap[:, a * 32 + t * 16:a * 32 + t * 16 + 16], src[:, t * 128:(t + 1) * 128], t_R, b.free,
                            inc=(a == 1 and t == 1), n=16)
            t_tk = V.op(lambda e, b=b: e.tensor_copy(TK, b.ap[:, 0:64]), tp)
            give(b, t_tk)
            for g in range(2):
                b = bank()
                bmT, cmT = XB[:, 8 + g, :], XB[:, 10 + g, :]
                mm(b.ap[:, 0:256], bmT[:, 0:128], cmT[:, 0:256], True, True, t_xb, b.free)
                tp = mm(b.ap[:, 256:384], bmT[:, 128:256], cmT[:, 128:256], True, True, inc=True)
                give(b, tt(CB[:, g, :], b.ap[:, 0:384], SI, ALU.mult, tp, t_masks2))
            yield
            for t in range(2):
                for c2 in range(2):
                    b = bank()
                    for i in range(4):
                        tp = tr(b.ap[:, i * 128:(i + 1) * 128], XB[:, c2 * 4 + i, t * 128:(t + 1) * 128], t_xb, b.free,
                                inc=(i == 3))
                    t_xf = tt(XF[:, t, c2 * 512:(c2 + 1) * 512].rearrange("p (h c) -> p h c", c=64),
                              b.ap.rearrange("p (h c) -> p h c", c=64),
                              bc(TK[:, t * 16 + c2 * 8:t * 16 + c2 * 8 + 8], 64), ALU.mult, tp)
                    give(b, t_xf)
                    yield
            mine, pr = [], 0
            while pr < 8 or mine:
                for g in list(mine):
                    try:
                        next(g)
                    except StopIteration:
                        mine.remove(g)
                if pr < 8 and len(mine) < 3:
                    mine.append(ssd_pair(pr, t_R, t_xf))
                    pr += 1
                yield
            while 0 not in t_z:
                yield
            yf = Y.rearrange("p i t -> p (i t)")
            for g in range(2):
                r = slice(g * 1024, g * 1024 + 1024)
                t_y[g] = tt(yf[:, r], yf[:, r], Z[:, r], ALU.mult, t_z[0])
                yield
            mine = [gnorm(0), gnorm(1)]
            while mine:
                for g in list(mine):
                    try:
                        next(g)
                    except StopIteration:
                        mine.remove(g)
                yield

        sc_free = [None] * 6
        t_y = {}

        def ssd_pair(pr, t_R, t_xf):
            js = (2 * (pr % 3), 2 * (pr % 3) + 1)
            bs = []
            for j in range(2):
                hd, b = 2 * pr + j, bank()
                tp = mm(b.ap[:, 0:384], ident[0:16, hd:hd + 1].to_broadcast([16, 128]), R, True, True, t_id, t_R, b.free,
                        inc=True)
                bs.append((b, tp))
            yield
            for j in range(2):
                hd, sc = 2 * pr + j, SC[js[j]]
                b, tp = bs[j]
                ts(sc[:, 0:256], b.ap[:, 0:256], TK[:, 32 + hd:33 + hd], 0.0, ALU.subtract, ALU.min, tp,
                   sc_free[js[j]])
                tv = ts(sc[:, 256:384], b.ap[:, 256:384], TK[:, 48 + hd:49 + hd], 0.0, ALU.subtract, ALU.min)
                give(b, tv)
                ta = act_(sc, sc, ACT.Exp, tv)
            yield
            for j in range(2):
                tv = tt(SC[js[j]], SC[js[j]], CB[:, (2 * pr + j) // 8, :], ALU.mult, ta)
            yield
            b = bank()
            for j in range(2):
                hd, sc = 2 * pr + j, SC[js[j]]
                yo = b.ap[j * 64:j * 64 + 64, :]
                mm(yo[:, 0:256], XF[:, 0, hd * 64:hd * 64 + 64], sc[:, 0:256], True, False, tv, t_xf, b.free)
                tp = mm(yo[:, 128:256], XF[:, 1, hd * 64:hd * 64 + 64], sc[:, 256:384], False, True, inc=True)
                sc_free[js[j]] = tp
            yield
            tv = stt(Y[:, pr, :], XB[:, pr, :], col("dsk", pr), b.ap[:, 0:256], ALU.mult, ALU.add, tp)
            give(b, tv)
            t_y[pr] = tv

        def gnorm(g):
            ys = [Y[:, g * 4 + i, :] for i in range(4)]
            rs = Rs(256)
            yield from rs_bcast(rs, ys, 512, [XB[:, 4 * g + i, :] for i in range(4)],
                                t_y[1])
            for i in range(4):
                tv = stt(ys[i], ys[i], col("sso", g * 4 + i), rs.bank.ap[:, 0:256], ALU.mult, ALU.mult, rs.tok,
                         chain=False)
            give(rs.bank, tv)
            for i in range(4):
                OUT2[8 + 4 * g + i] = ys[i], tv

        OUT2 = {}

        def sink_dt(i, m, b, tp):
            tv = ts(DT, b.ap[0:16, 0:256], col("dtb", 0, 16), None, ALU.add, None, tp)
            live.append(ssd_prep(tv))
            return [tv]

        fm_tiles(1, tA, sink_dt)

        sb_free = [None] * NB
        sb_out = {}

        def sb_head(hd, tin):
            n = hd % NB
            qk, sq, sp, lm = QKf[:, hd * 512:hd * 512 + 512], SQb[n], SPb[n], LMb[n]
            lt = sq[:, 0:384]
            rs = Rs(512)
            yield from rs_bcast(rs, [qk], 128, [sq], tin, sb_free[n])
            for j in range(2):
                r = slice(j * 256, j * 256 + 256)
                tv = stt(qk[:, r], qk[:, r], small[:, 28 + j:29 + j], rs.bank.ap[:, r], ALU.mult, ALU.mult, rs.tok,
                         t_gain, chain=False)
            give(rs.bank, tv)
            yield
            q, k = qk[:, 0:256], qk[:, 256:512]
            b = bank()
            mm(b.ap[:, 0:256], k[:, 0:128], q[:, 0:256], True, True, tv, b.free)
            tp = mm(b.ap[:, 256:384], k[:, 128:256], q[:, 128:256], True, True, inc=True)
            l = b.ap[:, 0:384]
            yield
            tv = tt(lm, l, NM, ALU.add, tp, t_masks2)
            act_(lt, l, ACT.Abs, tp, tv)
            act_(lt, lt, ACT.Exp, scale=-1.0)
            ta = act_(lt, lt, ACT.Ln, bias=1.0)
            yield
            tv = stt(sp, l, 0.0, lt, ALU.max, ALU.add, ta)
            give(b, tv)
            tv = tt(sp, sp, SM, ALU.mult)
            yield
            b = bank()
            mm(b.ap[:, 0:256], tri[:, :], sp[:, 0:256], True, False, tv, b.free)
            mm(b.ap[:, 128:256], ones[:, 0:128], sp[:, 256:384], False, True)
            tp = mm(b.ap[:, 256:384], tri[:, :], sp[:, 256:384], True, True, inc=True)
            yield
            tv = tt(lm, lm, b.ap[:, 0:384], ALU.subtract, tp)
            give(b, tv)
            yield
            ta = act_(lm, lm, ACT.Exp, tv)
            yield
            b = bank()
            tp = av_T(b.ap, V2[:, 0, hd * 128:(hd + 1) * 128], V2[:, 1, hd * 128:(hd + 1) * 128], lm, ta, t_v2, b.free)
            yield
            ta = cp(q, b.ap[:, 0:256], tp)
            give(b, ta)
            sb_free[n] = [tp, ta]
            sb_out[hd] = ta

        qk_toks = []

        def sink_sb(i, m, b, tp):
            ta = cp(QKf[:, i * 256:i * 256 + 512], b.ap, tp)
            qk_toks.append(ta)
            return [ta]

        def run_sb():
            hd, mine = 0, []
            while hd < 8 or mine:
                for g in list(mine):
                    try:
                        next(g)
                    except StopIteration:
                        mine.remove(g)
                if hd < 8 and len(mine) < NB and hd < len(qk_toks) and (hd < NB or hd - NB in sb_out):
                    mine.append(sb_head(hd, qk_toks[hd]))
                    hd += 1
                yield
            os = [QKf[:, i * 512:i * 512 + 256] for i in range(8)]
            while 15 not in OUT2:
                yield
            rs = Rs(256)
            yield from rs_bcast(rs, os, 1024, [XB[:, i, :] for i in range(8)], sb_out[7], OUT2[15][1])
            for i in range(8):
                tv = stt(os[i], os[i], col("sbo", i), rs.bank.ap[:, 0:256], ALU.mult, ALU.mult, rs.tok, chain=False)
                OUT2[i] = os[i], tv
            give(rs.bank, tv)

        live.append(run_sb())
        fm_tiles(12, tA, sink_sb)
        fm_tiles(8, tA, sink_z)
        fm_tiles(4, tA, lambda i, m, b, tp: sink_sb(i + 12, m, b, tp))
        t_proj = tn()
        MX.clear()
        t_sq = []
        rows(range(8, 16), act_lhs, mixed(OUT2, range(8, 16)), add_only)
        rows(range(8), act_lhs, mixed(OUT2, range(8)), add_h(t_sq))
        drain()

        fine[0] = False
        arena("ar5", 23936)
        ash, asl = sb("ash", 1024, FR, phase[0]), sb("asl", 1024, FR, phase[0])
        NI = 64
        AGf = carve(NI * 256)
        AG = AGf.rearrange("p (i t) -> p i t", t=256)
        xn = AGf[:, 0:3072]
        QT = AGf[:, 12288:16384].rearrange("p (i t) -> p i t", t=256)
        SK = AGf[:, 10240:12288]
        SCS = [carve(2048), AGf[:, 8192:10240]]
        CA = carve(2048)
        TS_, TI = carve(256), carve(256)
        TIU = carve(256).bitcast(U32)
        BS = carve(128)
        BP = carve(128).bitcast(U32)
        BA, BB = carve(128), carve(128)
        PK = carve(384)
        picks = carve(768)
        OH = CA
        GE = [carve(512), carve(512)]
        pk3 = picks.rearrange("p (c t) -> p c t", c=3)
        tA = norm_T("ffn_norm_2", xn, t_sq[-1], True)
        s_sk = sem("s_sk")
        t_sk = A.dma(SK, sk, s_sk, 1, t_sq[-1])
        fm_tiles(16, tA, lambda i, m, b, tp: [cp(QT[:, i:i + 2, :], b.ap.rearrange("p (a t) -> p a t", a=2), tp)])
        t_q = an()
        t_sc = []
        for t in range(2):
            for c in range(4):
                b = bank()
                for i4 in range(4):
                    i = c * 4 + i4
                    tp = mm(b.ap[:, i4 * 128:i4 * 128 + 128], QT[:, i, t * 128:(t + 1) * 128],
                            SK[:, i * 128:(i + 1) * 128], True, True, t_q, t_sk, b.free, inc=(i4 == 3))
                t_sc.append(cp(SCS[t][:, c * 512:(c + 1) * 512], b.ap, tp))
                give(b, t_sc[-1])
        t_qt = tn()

        def top16(items, *after):
            def each(fn, was):
                return [V.op(lambda e, it=it: fn(e, *it), w, chain=False) for it, w in zip(items, was)]

            t = each(lambda e, v, b, p: e.max(b[:, 0:8], v), [list(after)] * len(items))
            t = each(lambda e, v, b, p: e.max_index(p[:, 0:8], b[:, 0:8], v), t)
            t = each(lambda e, v, b, p: e.match_replace(v, b[:, 0:8], v, -3.0e38), t)
            t = each(lambda e, v, b, p: e.max(b[:, 8:16], v), t)
            return each(lambda e, v, b, p: e.max_index(p[:, 8:16], b[:, 8:16], v), t)

        def topk():
            ts3 = TS_.rearrange("p (i k) -> p i k", k=16)
            tu3 = TIU.rearrange("p (i k) -> p i k", k=16)
            ti3 = TI.rearrange("p (h c k) -> p h c k", c=2, k=16)
            bs3 = BS.rearrange("p (h k) -> p h k", k=16)
            gg = PK[:, 256:384]
            g3 = gg.rearrange("p (h k) -> p h k", k=16)
            pkd = None
            helped[0] = True
            for t in range(2):
                sc3 = SCS[t].rearrange("p (i k) -> p i k", k=128)
                for i in range(0, 16, 4):
                    top16([(sc3[:, j, :], ts3[:, j, :], tu3[:, j, :]) for j in range(i, i + 4)], t_sc[-1], vn())
                    yield
                    yield
                V.op(lambda e: e.tensor_copy(TI, TIU))
                for hd in range(8):
                    ca = CA[:, hd * 256:(hd + 1) * 256].rearrange("p (a b) -> p a b", b=16)
                    tv = tt(ca, bc(ts3[:, 2 * hd, :], 16), bm(ts3[:, 2 * hd + 1, :], 16), ALU.add, chain=(hd == 0))
                    if hd % 4 == 3:
                        yield
                for h4 in range(0, 8, 4):
                    top16([(CA[:, hd * 256:(hd + 1) * 256], BS[:, hd * 16:hd * 16 + 16], BP[:, hd * 16:hd * 16 + 16])
                           for hd in range(h4, h4 + 4)], tv)
                    yield
                    yield
                if t == 1:
                    t_sc1[0] = tv
                tv = tt(g3, bs3, bs3[:, :, 0:1].to_broadcast([128, 8, 16]), ALU.subtract, pkd)
                ta = act_(gg, gg, ACT.Exp, tv)
                bau, bbu = BA.bitcast(U32), BB.bitcast(U32)
                V.op(lambda e: e.tensor_scalar(bau, BP, 4, None, ALU.logical_shift_right))
                V.op(lambda e: e.tensor_scalar(bbu, BP, 15, None, ALU.bitwise_and))
                V.op(lambda e: e.tensor_copy(BA, bau))
                V.op(lambda e: e.tensor_copy(BB, bbu))
                yield
                V.op(lambda e: e.tensor_reduce(small[:, 32:40], g3, AX.X, ALU.add), ta)
                recip(small[:, 48:56], small[:, 32:40])
                tt(g3, g3, bc(small[:, 48:56], 16), ALU.mult)
                TMP = SCS[0]
                for c, pos in ((0, BA), (1, BB)):
                    o3 = TMP.rearrange("p (n a) -> p n a", a=16)
                    tt(o3, bc(pos, 16), bm(iot[:, 0:16], 128), ALU.is_equal)
                    yield
                    yield
                    for hd in range(8):
                        o = TMP[:, hd * 256:(hd + 1) * 256].rearrange("p (k a) -> p k a", a=16)
                        tt(o, o, bm(ti3[:, hd, c, :], 16), ALU.mult, chain=(hd == 0))
                    yield
                    yield
                    tv = V.op(lambda e, c=c, o3=o3: e.tensor_reduce(PK[:, c * 128:(c + 1) * 128], o3, AX.X, ALU.add))
                    yield
                    yield
                b = bank()
                for c in range(3):
                    tp = tr(b.ap[:, c * 128:(c + 1) * 128], PK[:, c * 128:(c + 1) * 128], tv, b.free, inc=(c == 2))
                pkd = tp
                tpk[t] = V.op(lambda e, b=b, t=t: e.tensor_copy(
                    pk3[:, :, t * 128:(t + 1) * 128], b.ap[:, 0:384].rearrange("p (c t) -> p c t", c=3)), tp)
                give(b, tpk[t])
            helped[0] = False

        tpk, t_sc1 = {}, [None]
        oh_free = [None, None]
        tcur, ndone = [0], [0]
        t_ag = []

        def gates(half):
            def onehots(q):
                o = OH[:, (q % 2) * 768:(q % 2) * 768 + 768]
                oj = o[:, 0:512].rearrange("p (t j) -> p t j", t=4)
                t = 4 * q
                tg = tt(oj, bm(iot[:, :], 4), bc(picks[:, 256 + t:260 + t], 128), ALU.is_equal, tpk[1],
                        t_const, oh_free[q % 2], chain=False)
                for j in range(4):
                    oi = o[:, 512 + j * 64:576 + j * 64]
                    tv = V.op(lambda e, oi=oi, t=t + j: e.tensor_scalar(
                        oi, iot[:, half * 64:half * 64 + 64], picks[:, t:t + 1], picks[:, 512 + t:513 + t],
                        ALU.is_equal, ALU.mult), tpk[1], oh_free[q % 2], chain=False)
                return o, [tg, tv]

            nxt = onehots(0)
            yield
            for q in range(64):
                o, tok = nxt
                if q < 63:
                    nxt = onehots(q + 1)
                b = bank()
                for j in range(4):
                    tp = mm(b.ap[:, j * 64:(j + 1) * 64], o[:, j * 128:(j + 1) * 128], o[:, 512 + j * 64:576 + j * 64],
                            True, True, tok, b.free, inc=(j == 3))
                oh_free[q % 2] = tp
                pv = b.ap[:, 0:256].rearrange("p (t i) -> p i t", t=4)
                r, nd = slice(4 * q, 4 * q + 4), ndone[0]
                toks = []
                if nd:
                    toks.append(tt(AG[:, 0:nd, r], AG[:, 0:nd, r], pv[:, 0:nd, :], ALU.mult, tp, lastA[0], ge_free, chain=False))
                    t_agv[0] = toks[0]
                if nd < NI:
                    lastC[0] = V.op(lambda e, nd=nd, r=r, pv=pv: e.tensor_copy(AG[:, nd:NI, r], pv[:, nd:NI, :]),
                                    tp, ag_free[0], chain=False)
                    toks = [lastC[0]]
                give(b, *toks)
                t_ag[:] = toks
                tcur[0] = 4 * q + 4
                for _ in range(G_STEP[half]):
                    yield

        t_agv = [None]
        ag_free, ge_free, lastA, lastC = [None], [None, None], [None], [None]

        def sink_dn(i, m, b, tp):
            tc = tcur[0]
            if i >= 32 and half == 0:
                while t_sc1[0] is None:
                    tick()
                tp = [tp, t_sc1[0]]
            bv = b.ap.rearrange("p (a t) -> p a t", a=2)
            toks = []
            if tc:
                n = i // 2 % 2
                ge = GE[n].rearrange("p (a t) -> p a t", a=2)
                ta = act_(ge[:, :, 0:tc], bv[:, :, 0:tc], ACT.Gelu, tp, ge_free[n])
                ge_free[n] = tt(AG[:, i:i + 2, 0:tc], AG[:, i:i + 2, 0:tc], ge[:, :, 0:tc], ALU.mult, ta, lastC[0], t_agv[0],
                               chain=False)
                toks = [ta]
            if tc < 256:
                lastA[0] = act_(AG[:, i:i + 2, tc:256], bv[:, :, tc:256], ACT.Gelu, tp, ag_free[0])
                toks = [lastA[0]]
            ndone[0] = i + 2
            return toks

        asp = [Slot((ash[:, i * 256:(i + 1) * 256], asl[:, i * 256:(i + 1) * 256])) for i in range(4)]
        s_out = sem("s_out")
        nout = [0]
        outs = out.rearrange("(t p) d -> p t d", p=128)

        def ev_mid(t, c, b, tp):
            r = slice(c * 512, c * 512 + 512)
            return [tt(h[:, t, r], h[:, t, r], b.ap, ALU.add, tp)]

        def ev_last(t, c, b, tp):
            tv = ev_mid(t, c, b, tp)
            nout[0] += 1
            r = slice(c * 512, c * 512 + 512)
            S.dma(outs[:, t, r], h[:, t, r], s_out, nout[0], tv[0])
            return tv

        ag_free[0] = t_qt
        for half in range(2):
            tcur[0] = ndone[0] = 0

            def job(half=half):
                if half == 0:
                    yield from topk()
                yield from gates(half)

            live.append(job())
            fm_tiles(64, tA, sink_dn)
            drain()
            t_agd = [an(), vn()]
            made, cnt = [0], [0]

            def asplit(upto):
                while made[0] < min(upto, 2 * NI):
                    n = made[0]
                    made[0] += 1
                    s = asp[n % 4]
                    s.tok = split(s.ap[0], s.ap[1], AG[:, n % NI, :], t_agd, s.free)

            def need_a(k):
                asplit(cnt[0] + 3)
                return asp[cnt[0] % 4].tok

            def used_a(tp):
                asp[cnt[0] % 4].free = tp
                cnt[0] += 1

            def lhs_a(k, t):
                s = asp[cnt[0] % 4]
                return s.ap[0][:, t * 128:(t + 1) * 128], s.ap[1][:, t * 128:(t + 1) * 128]

            rows(range(NI), lhs_a, need_a, ev_mid if half == 0 else ev_last, after=used_a)
            ag_free[0] = [an(), vn()]
        assert used[0] == len(seq)

        block = ctx.enter_context(nc.Block())

        @block.sync
        def _(e):
            S.emit(e)
            e.wait_ge(s_out, 16 * nout[0])

        @block.gpsimd
        def _(e):
            P.emit(e)

        @block.scalar
        def _(e):
            A.emit(e)

        @block.vector
        def _(e):
            V.emit(e)

        @block.tensor
        def _(e):
            T.emit(e)
        phase[0].close()


def lay_out(d):
    g = {k: np.asarray(v) for k, v in d.items()}

    def c(a):
        return np.ascontiguousarray(a)

    def colz(v):
        v = v.reshape(-1)
        if v.size < 128:
            v = np.concatenate([v, np.zeros(128 - v.size, v.dtype)])
        return v.reshape(-1, 128).T

    def fm(w):
        k, n = w.shape
        return w.reshape(k // 128, 128, n // 128, 128).transpose(2, 1, 0, 3).reshape(n // 128, 128, k)

    def pairs(q, k):
        n = q.shape[1] // 128
        return np.stack([q.reshape(-1, n, 128), k.reshape(-1, n, 128)], 2).reshape(-1, 2 * n * 128)

    wi = g["w_in"][0]
    s = [0, 512, 1024, 1536, 2048, 2816, 3584, 4352, 4358, 5126, 5894, 6662]
    aq, af, ai, ag, bq, bk, bv, bf, cq, ck, cv = [wi[:, s[i]:s[i + 1]] for i in range(11)]
    w2 = g["w_in_2"][0]
    q2, k2, v2, z2, x2, d2 = [w2[:, a:b] for a, b in ((0, 1024), (1024, 2048), (2048, 3072), (3072, 4096),
                                                      (4096, 5632), (5632, 5648))]
    par = {"attn_norm": g["attn_norm"], "ffn_norm": g["ffn_norm"], "ple_norm": g["ple_norm"],
           "attn_norm_2": g["attn_norm_2"], "ffn_norm_2": g["ffn_norm_2"], "lb": g["lb_logits"],
           "hgrn": g["hgrn_onorm"], "foxq": g["fox_qnorm"], "foxk": g["fox_knorm"], "mobq": g["moba_qnorm"],
           "mobk": g["moba_knorm"], "cw0": g["conv_w"][0, 0], "cw1": g["conv_w"][0, 1], "cw2": g["conv_w"][0, 2],
           "cb": g["conv_b"], "sbq": g["sb_q_norm_2"], "sbk": g["sb_k_norm_2"],
           "c20": g["conv_w_2"][0, 0], "c21": g["conv_w_2"][0, 1], "c22": g["conv_w_2"][0, 2],
           "c23": g["conv_w_2"][0, 3], "cb2": g["conv_b_2"], "sbo": g["sb_out_norm_2"], "sso": g["ssd_out_norm_2"],
           "dsk": np.repeat(g["d_skip_2"].reshape(-1), 64), "bf": g["fox_bf"], "dtb": g["dt_bias_2"],
           "alog": g["a_log_2"]}
    gu = np.stack([fm(g["w_gate"][0]), fm(g["w_up"][0])], 1).reshape(88, 128, 2048)
    return {
        "x": c(g["x"][0]),
        "pT": c(g["p"][0, 0].reshape(256, 2, 128).transpose(2, 1, 0).reshape(128, 512)),
        "cols": c(np.concatenate([colz(par[k]) for k, _ in COLS], 1)),
        "w1fm": c(fm(np.concatenate([aq, ag, af, bf, np.zeros((2048, 122), bf.dtype), pairs(bq, bk), pairs(cq, ck)], 1))),
        "w1v": c(np.concatenate([ai, bv, cv], 1).reshape(16, 128, 2048)),
        "wo1": c(g["w_out"][0].reshape(16, 128, 2048)),
        "wgu": c(gu),
        "wdn": c(g["w_down"][0].reshape(44, 128, 2048)),
        "plg": c(g["w_ple_gate"][0].reshape(16, 128, 2048)),
        "plp": c(g["w_ple_proj"][0].reshape(2, 128, 2048)),
        "w2fm": c(fm(np.concatenate([x2, d2, np.zeros((2048, 112), d2.dtype), pairs(q2, k2), z2], 1))),
        "w2v": c(v2.reshape(16, 128, 1024)),
        "wo2": c(g["w_out_2"][0].reshape(16, 128, 2048)),
        "wq": c(fm(g["peer_query_2"][0])),
        "sk": c(g["peer_sub_keys_2"][0].reshape(16, 128, 128).transpose(2, 0, 1).reshape(128, 2048)),
        "dn": c(g["peer_down_2"][0].reshape(128, 128, 16, 128).transpose(0, 3, 2, 1).reshape(128, 128, 2048)),
        "up": c(g["peer_up_2"][0].reshape(128, 128, 2048)),
    }


def kernel(**inputs):
    import concourse.bacc as bacc
    from concourse.bass_utils import run_bass_kernel_spmd

    arrays = lay_out(inputs)
    nc = bacc.Bacc("TRN2", target_bir_lowering=False, num_devices=1)
    args = [nc.dram_tensor(f"in_{k}", a.shape, mybir.dt.from_np(a.dtype), kind="ExternalInput").ap()
            for k, a in arrays.items()]
    o = nc.dram_tensor("out_0", (256, 2048), F32, kind="ExternalOutput").ap()
    build(nc, *args, o)
    r = run_bass_kernel_spmd(nc, [{f"in_{k}": a for k, a in arrays.items()}], core_ids=[0])
    return r.results[0]["out_0"].reshape(1, 256, 2048)
```
